# Optimizing a Trainium2 kernel written in Bass

```python
import math
import jax, jax.numpy as jnp
from jax import lax
import numpy as np

D_MODEL = 1024
BATCH = 1
SEQ = 512
DEPTH = 2

HEAD_DIM = 64
N_GROUP_HEADS = 4
GROUP_WIDTH = N_GROUP_HEADS * HEAD_DIM
N_MIXERS = 4
MIX_WIDTH = N_MIXERS * GROUP_WIDTH
ROPE_THETA = 500000.0
ROPE_FRACTION = 4
RMS_EPS = 1e-6

MOBA_BLOCK = 256
MOBA_TOPK = 3
MOBA_Q_CHUNK = 16
RWKV_DECAY_LORA = 64
RWKV_A_LORA = 64
RWKV_GATE_LORA = 128
RWKV_LN_EPS = 64e-5
RWKV_SPLITS = [GROUP_WIDTH, RWKV_DECAY_LORA, GROUP_WIDTH, GROUP_WIDTH, RWKV_A_LORA, RWKV_GATE_LORA]
RWKV_WIDTH = sum(RWKV_SPLITS)
SGU_CHUNK = 128
DIFF_QK_DIM = HEAD_DIM // 2
DIFF_Q_BLOCK = 128
DIFF_SUBLN_EPS = 1e-5

A_COLS = 3 * GROUP_WIDTH
B_COLS = RWKV_WIDTH
C_COLS = 2 * GROUP_WIDTH
D_COLS = 3 * GROUP_WIDTH
IN_WIDTH = A_COLS + B_COLS + C_COLS + D_COLS

N_EXPERT_GROUPS = 4
EXPERTS_PER_GROUP = 8
N_EXPERTS = N_EXPERT_GROUPS * EXPERTS_PER_GROUP
EXPERT_TOPK = 2
EXPERT_FF = D_MODEL // 2
MOE_ROW_BLOCK = 128

kernel_name = 'hybrid_moba_rwkv7_sgu_diffattn_hmoe'

def rmsnorm(x, g, eps=RMS_EPS):
    xf = x.astype(jnp.float32)
    y = xf * lax.rsqrt(jnp.mean(xf * xf, axis=-1, keepdims=True) + eps)
    return (y * g).astype(x.dtype)

def layernorm(x, g, b, eps=1e-5):
    xf = x.astype(jnp.float32)
    mu = jnp.mean(xf, axis=-1, keepdims=True)
    var = jnp.mean(jnp.square(xf - mu), axis=-1, keepdims=True)
    return ((xf - mu) * lax.rsqrt(var + eps) * g + b).astype(x.dtype)

def rope_tables(seq, rot_dim):
    inv = ROPE_THETA ** (-jnp.arange(0, rot_dim, 2, dtype=jnp.float32) / rot_dim)
    ang = jnp.arange(seq, dtype=jnp.float32)[:, None] * inv[None, :]
    return jnp.cos(ang), jnp.sin(ang)

def apply_partial_rope(t, cos, sin):
    half = cos.shape[-1]
    c = cos.astype(t.dtype)
    s = sin.astype(t.dtype)
    t1 = t[..., :half]
    t2 = t[..., half:2 * half]
    return jnp.concatenate([t1 * c - t2 * s, t2 * c + t1 * s, t[..., 2 * half:]], axis=-1)

def split_heads(t, n):
    b, s, _ = t.shape
    return t.reshape(b, s, n, -1).transpose(0, 2, 1, 3)

def merge_heads(t):
    b, h, s, d = t.shape
    return t.transpose(0, 2, 1, 3).reshape(b, s, h * d)

def moba_attention(q, k, v, cos, sin):
    B, H, S, Dh = q.shape
    q = apply_partial_rope(q, cos, sin)
    k = apply_partial_rope(k, cos, sin)
    nb = -(-S // MOBA_BLOCK)
    sp = nb * MOBA_BLOCK
    pad = ((0, 0), (0, 0), (0, sp - S), (0, 0))
    q, k, v = jnp.pad(q, pad), jnp.pad(k, pad), jnp.pad(v, pad)
    kb = k.reshape(B, H, nb, MOBA_BLOCK, Dh)
    vb = v.reshape(B, H, nb, MOBA_BLOCK, Dh)
    kmean = jnp.mean(kb.astype(jnp.float32), axis=3)
    gate = jnp.einsum('bhsd,bhnd->bhsn', q.astype(jnp.float32), kmean)
    qpos = jnp.arange(sp)
    qblk = qpos // MOBA_BLOCK
    past = jnp.arange(nb)[None, :] < qblk[:, None]
    gate = jnp.where(past, gate, -jnp.inf)
    n_sel = min(MOBA_TOPK, max(nb - 1, 1))
    _, top_idx = lax.top_k(gate, n_sel)
    top_valid = top_idx < qblk[:, None]
    own = jnp.broadcast_to(qblk[:, None], (B, H, sp, 1)).astype(top_idx.dtype)
    blk_idx = jnp.concatenate([top_idx, own], axis=-1)
    blk_valid = jnp.concatenate([top_valid, jnp.ones((B, H, sp, 1), bool)], axis=-1)

    nc = sp // MOBA_Q_CHUNK

    def to_chunks(t):
        t = t.reshape((B, H, nc, MOBA_Q_CHUNK) + t.shape[3:])
        return jnp.moveaxis(t, 2, 0)

    bi = jnp.arange(B)[:, None, None, None]
    hi = jnp.arange(H)[None, :, None, None]
    scale = Dh ** -0.5

    def attend(args):
        qc, ic, mc, pc = args
        kg = kb[bi, hi, ic]
        vg = vb[bi, hi, ic]
        s = jnp.einsum('bhcd,bhcnkd->bhcnk', qc, kg).astype(jnp.float32) * scale
        kpos = ic[..., None] * MOBA_BLOCK + jnp.arange(MOBA_BLOCK)
        mask = mc[..., None] & (kpos <= pc[None, None, :, None, None])
        s = jnp.where(mask, s, -jnp.inf)
        p = jax.nn.softmax(s.reshape(B, H, MOBA_Q_CHUNK, -1), axis=-1).reshape(s.shape)
        return jnp.einsum('bhcnk,bhcnkd->bhcd', p.astype(vg.dtype), vg)

    out = lax.map(attend, (to_chunks(q), to_chunks(blk_idx), to_chunks(blk_valid),
                           qpos.reshape(nc, MOBA_Q_CHUNK)))
    out = jnp.moveaxis(out, 0, 2).reshape(B, H, sp, Dh)[:, :, :S]
    return merge_heads(out)

def rwkv7_time_mix(proj, mu, w0, w2, a0, a2, g2, k_k, k_a, r_k, ln_g, ln_b):
    dt = proj.dtype
    B, S, _ = proj.shape
    H, N = N_GROUP_HEADS, HEAD_DIM
    prev = jnp.pad(proj, ((0, 0), (1, 0), (0, 0)))[:, :-1]
    xs = proj + (prev - proj) * mu
    r, wd, k, v, ad, gd = jnp.split(xs, list(np.cumsum(RWKV_SPLITS)[:-1]), axis=-1)
    w_log = -jax.nn.softplus(-(w0 + jnp.tanh(wd) @ w2).astype(jnp.float32)) - 0.5
    decay = jnp.exp(-jnp.exp(w_log))
    a = jax.nn.sigmoid(a0 + ad @ a2)
    g = jax.nn.sigmoid(gd) @ g2
    kk = (k * k_k).reshape(B, S, H, N).astype(jnp.float32)
    kk = kk / jnp.maximum(jnp.linalg.norm(kk, axis=-1, keepdims=True), 1e-12)
    k = k * (1.0 + (a - 1.0) * k_a)

    f32 = lambda t: t.reshape(B, S, H, N).astype(jnp.float32)
    r_h, k_h, v_h, a_h = f32(r), f32(k), f32(v), f32(a)
    w_h = decay.reshape(B, S, H, N)
    seq_first = lambda t: jnp.moveaxis(t, 1, 0)

    def step(state, inp):
        r_t, w_t, k_t, v_t, a_t, b_t = inp
        sa = jnp.einsum('bhvk,bhk->bhv', state, a_t)
        state = (state * w_t[:, :, None, :] + sa[..., None] * b_t[:, :, None, :]
                 + v_t[..., None] * k_t[:, :, None, :])
        return state, jnp.einsum('bhvk,bhk->bhv', state, r_t)

    state0 = jnp.zeros((B, H, N, N), jnp.float32)
    _, y = lax.scan(step, state0, (seq_first(r_h), seq_first(w_h), seq_first(k_h),
                                   seq_first(v_h), seq_first(-kk), seq_first(kk * a_h)))
    y = jnp.moveaxis(y, 0, 1)
    mean = jnp.mean(y, axis=-1, keepdims=True)
    var = jnp.mean(jnp.square(y - mean), axis=-1, keepdims=True)
    y = ((y - mean) * lax.rsqrt(var + RWKV_LN_EPS)).reshape(B, S, GROUP_WIDTH) * ln_g + ln_b
    bonus = jnp.sum(r_h * k_h * r_k.astype(jnp.float32), axis=-1, keepdims=True) * v_h
    return ((y + bonus.reshape(B, S, GROUP_WIDTH)) * g).astype(dt)

def sgu_mix(u, v, ln_g, ln_b, w_s, b_s):
    u = jax.nn.gelu(u, approximate=False)
    v = layernorm(jax.nn.gelu(v, approximate=False), ln_g, ln_b)
    B, S, _ = v.shape
    nc = S // SGU_CHUNK
    vh = v.reshape(B, nc, SGU_CHUNK, N_GROUP_HEADS, HEAD_DIM)
    causal = jnp.tril(jnp.ones((SGU_CHUNK, SGU_CHUNK), bool))
    w = jnp.where(causal[None], w_s, 0.0).astype(v.dtype)
    mixed = jnp.einsum('hts,bcshd->bcthd', w, vh) + b_s.T[None, None, :, :, None]
    return u * mixed.reshape(B, S, GROUP_WIDTH)

def diff_attention(q, k, v, lq1, lk1, lq2, lk2, subln_g, lambda_init, cos, sin):
    B, S, _ = q.shape
    H = N_GROUP_HEADS
    q = q.reshape(B, S, H, 2, DIFF_QK_DIM).transpose(0, 2, 3, 1, 4)
    k = k.reshape(B, S, H, 2, DIFF_QK_DIM).transpose(0, 2, 3, 1, 4)
    q = apply_partial_rope(q, cos, sin)
    k = apply_partial_rope(k, cos, sin)
    vh = split_heads(v, H)
    f = lambda t: t.astype(jnp.float32)
    lam = jnp.exp(jnp.sum(f(lq1) * f(lk1))) - jnp.exp(jnp.sum(f(lq2) * f(lk2))) + lambda_init
    scale = DIFF_QK_DIM ** -0.5
    outs = []
    for i in range(S // DIFF_Q_BLOCK):
        q0 = i * DIFF_Q_BLOCK
        end = q0 + DIFF_Q_BLOCK
        s = jnp.einsum('bhiqd,bhikd->bhiqk', q[:, :, :, q0:end], k[:, :, :, :end]).astype(jnp.float32) * scale
        mask = jnp.arange(end)[None, :] <= (q0 + jnp.arange(DIFF_Q_BLOCK))[:, None]
        p = jax.nn.softmax(jnp.where(mask, s, -jnp.inf), axis=-1)
        attn = p[:, :, 0] - lam * p[:, :, 1]
        outs.append(jnp.einsum('bhqk,bhkd->bhqd', attn.astype(vh.dtype), vh[:, :, :end]))
    o = jnp.concatenate(outs, axis=2)
    o = rmsnorm(o, subln_g, DIFF_SUBLN_EPS) * (1.0 - lambda_init)
    return merge_heads(o)

def hier_moe(x, wg, bg, we, be, w_gate, w_up, w_down):
    B, S, D = x.shape
    T = B * S
    xt = x.reshape(T, D)
    gprob = jax.nn.softmax((xt @ wg + bg).astype(jnp.float32), axis=-1)
    gp, gidx = lax.top_k(gprob, 1)
    elog = (xt @ we + be).astype(jnp.float32).reshape(T, N_EXPERT_GROUPS, EXPERTS_PER_GROUP)
    elog = jnp.take_along_axis(elog, gidx[:, :, None], axis=1)[:, 0]
    ep, eidx = lax.top_k(jax.nn.softmax(elog, axis=-1), EXPERT_TOPK)
    weight = gp * (ep / jnp.sum(ep, axis=-1, keepdims=True))
    expert = gidx * EXPERTS_PER_GROUP + eidx

    M = T * EXPERT_TOPK
    e_flat = expert.reshape(M)
    w_flat = weight.reshape(M)
    tok = jnp.repeat(jnp.arange(T), EXPERT_TOPK)
    order = jnp.argsort(e_flat)
    e_s, tok_s, w_s = e_flat[order], tok[order], w_flat[order]
    counts = jax.ops.segment_sum(jnp.ones((M,), jnp.int32), e_flat, num_segments=N_EXPERTS)
    starts = jnp.cumsum(counts) - counts
    pcounts = (counts + MOE_ROW_BLOCK - 1) // MOE_ROW_BLOCK * MOE_ROW_BLOCK
    pends = jnp.cumsum(pcounts)
    pstarts = pends - pcounts
    dest = pstarts[e_s] + (jnp.arange(M) - starts[e_s])
    P = M + N_EXPERTS * MOE_ROW_BLOCK
    nblk = P // MOE_ROW_BLOCK
    row_tok = jnp.full((P,), T, jnp.int32).at[dest].set(tok_s)
    row_w = jnp.zeros((P,), x.dtype).at[dest].set(w_s.astype(x.dtype))
    blk_expert = jnp.minimum(jnp.searchsorted(pends, jnp.arange(nblk) * MOE_ROW_BLOCK, side='right'),
                             N_EXPERTS - 1)
    xpad = jnp.concatenate([xt, jnp.zeros((1, D), xt.dtype)], axis=0)
    rows = xpad[row_tok].reshape(nblk, MOE_ROW_BLOCK, D)

    def expert_block(args):
        xb, e = args
        hdn = jax.nn.silu(xb @ w_gate[e]) * (xb @ w_up[e])
        return hdn @ w_down[e]

    y = lax.map(expert_block, (rows, blk_expert)).reshape(P, D)
    out = jnp.zeros((T + 1, D), x.dtype).at[row_tok].add(y * row_w[:, None])[:T]
    return out.reshape(B, S, D)

def setup_inputs(seed: int = 0) -> dict:
    key = jax.random.key(seed)
    ks = iter(jax.random.split(key, 40))

    def nrm(shape, scale):
        return jax.random.normal(next(ks), shape, jnp.float32) * scale

    L, D, GW, H, N = DEPTH, D_MODEL, GROUP_WIDTH, N_GROUP_HEADS, HEAD_DIM
    E, F = N_EXPERTS, EXPERT_FF
    return {
        'x': nrm((BATCH, SEQ, D), 1.0),
        'norm1_g': 1.0 + nrm((L, D), 0.02),
        'w_in': nrm((L, D, IN_WIDTH), D ** -0.5),
        'rwkv_mu': jax.random.uniform(next(ks), (L, RWKV_WIDTH), jnp.float32),
        'rwkv_w0': jax.random.uniform(next(ks), (L, GW), jnp.float32, minval=-6.0, maxval=1.0),
        'rwkv_w2': nrm((L, RWKV_DECAY_LORA, GW), 0.5 * RWKV_DECAY_LORA ** -0.5),
        'rwkv_a0': nrm((L, GW), 0.1),
        'rwkv_a2': nrm((L, RWKV_A_LORA, GW), RWKV_A_LORA ** -0.5),
        'rwkv_g2': nrm((L, RWKV_GATE_LORA, GW), RWKV_GATE_LORA ** -0.5),
        'rwkv_kk': 0.85 + nrm((L, GW), 0.02),
        'rwkv_ka': 1.0 + nrm((L, GW), 0.02),
        'rwkv_rk': nrm((L, H, N), 0.1),
        'rwkv_ln_g': 1.0 + nrm((L, GW), 0.02),
        'rwkv_ln_b': nrm((L, GW), 0.02),
        'sgu_ln_g': 1.0 + nrm((L, GW), 0.02),
        'sgu_ln_b': nrm((L, GW), 0.02),
        'sgu_w': nrm((L, H, SGU_CHUNK, SGU_CHUNK), SGU_CHUNK ** -0.5),
        'sgu_b': 1.0 + nrm((L, H, SGU_CHUNK), 0.02),
        'diff_lq1': nrm((L, DIFF_QK_DIM), 0.1),
        'diff_lk1': nrm((L, DIFF_QK_DIM), 0.1),
        'diff_lq2': nrm((L, DIFF_QK_DIM), 0.1),
        'diff_lk2': nrm((L, DIFF_QK_DIM), 0.1),
        'diff_subln_g': 1.0 + nrm((L, N), 0.02),
        'w_out': nrm((L, MIX_WIDTH, D), MIX_WIDTH ** -0.5),
        'norm2_g': 1.0 + nrm((L, D), 0.02),
        'router_group_w': nrm((L, D, N_EXPERT_GROUPS), D ** -0.5),
        'router_group_b': nrm((L, N_EXPERT_GROUPS), 0.01),
        'router_expert_w': nrm((L, D, E), D ** -0.5),
        'router_expert_b': nrm((L, E), 0.01),
        'moe_w_gate': nrm((L, E, D, F), D ** -0.5),
        'moe_w_up': nrm((L, E, D, F), D ** -0.5),
        'moe_w_down': nrm((L, E, F, D), F ** -0.5),
        'final_g': 1.0 + nrm((D,), 0.02),
    }

def reference(x, norm1_g, w_in, rwkv_mu, rwkv_w0, rwkv_w2, rwkv_a0, rwkv_a2, rwkv_g2,
              rwkv_kk, rwkv_ka, rwkv_rk, rwkv_ln_g, rwkv_ln_b, sgu_ln_g, sgu_ln_b, sgu_w, sgu_b,
              diff_lq1, diff_lk1, diff_lq2, diff_lk2, diff_subln_g, w_out, norm2_g,
              router_group_w, router_group_b, router_expert_w, router_expert_b,
              moe_w_gate, moe_w_up, moe_w_down, final_g):
    S = x.shape[1]
    cos_a, sin_a = rope_tables(S, HEAD_DIM // ROPE_FRACTION)
    cos_d, sin_d = rope_tables(S, DIFF_QK_DIM // ROPE_FRACTION)
    cut = [A_COLS, A_COLS + B_COLS, A_COLS + B_COLS + C_COLS]
    for l in range(DEPTH):
        proj = rmsnorm(x, norm1_g[l]) @ w_in[l]
        pa, pb, pc, pd = jnp.split(proj, cut, axis=-1)
        qa, ka, va = jnp.split(pa, 3, axis=-1)
        out_a = moba_attention(split_heads(qa, N_GROUP_HEADS), split_heads(ka, N_GROUP_HEADS),
                               split_heads(va, N_GROUP_HEADS), cos_a, sin_a)
        out_b = rwkv7_time_mix(pb, rwkv_mu[l], rwkv_w0[l], rwkv_w2[l], rwkv_a0[l], rwkv_a2[l],
                               rwkv_g2[l], rwkv_kk[l], rwkv_ka[l], rwkv_rk[l], rwkv_ln_g[l], rwkv_ln_b[l])
        uc, vc = jnp.split(pc, 2, axis=-1)
        out_c = sgu_mix(uc, vc, sgu_ln_g[l], sgu_ln_b[l], sgu_w[l], sgu_b[l])
        qd, kd, vd = jnp.split(pd, 3, axis=-1)
        lambda_init = 0.8 - 0.6 * math.exp(-0.3 * l)
        out_d = diff_attention(qd, kd, vd, diff_lq1[l], diff_lk1[l], diff_lq2[l], diff_lk2[l],
                               diff_subln_g[l], lambda_init, cos_d, sin_d)
        mixed = jnp.concatenate([out_a, out_b, out_c, out_d], axis=-1)
        x = x + mixed @ w_out[l]
        x = x + hier_moe(rmsnorm(x, norm2_g[l]), router_group_w[l], router_group_b[l],
                         router_expert_w[l], router_expert_b[l],
                         moe_w_gate[l], moe_w_up[l], moe_w_down[l])
    return rmsnorm(x, final_g)


_drawn_inputs = setup_inputs


def setup_inputs(seed=0):
    import zlib

    import numpy as np

    out = dict(_drawn_inputs(seed))
    spreads = {}
    factors = {'rwkv_ln_b': 16.044,
     'sgu_ln_g': 33.185,
     'sgu_ln_b': 31.598,
     'sgu_b': 17.539,
     'router_group_b': 16.336,
     'final_g': 20.589,
     'rwkv_w2': 3.959,
     'rwkv_a0': 2.98,
     'rwkv_kk': 20.488,
     'rwkv_ka': 4.805,
     'rwkv_ln_g': 22.014,
     'diff_lk2': 3.89,
     'diff_subln_g': 16.269,
     'router_expert_b': 19.994,
     'norm2_g': 4.569}
    for name, (base, spread) in spreads.items():
        noise = np.random.default_rng([zlib.crc32(name.encode()), seed]).standard_normal(out[name].shape)
        drawn = base * np.exp(spread * noise) if base else spread * noise
        out[name] = __import__('jax').numpy.asarray(drawn.astype(out[name].dtype))
    for name, factor in factors.items():
        out[name] = (out[name] * factor).astype(out[name].dtype)
    return out
```

```python
import math
from contextlib import ExitStack

import concourse.bass as bass
from concourse import mybir
import numpy as np

F32 = mybir.dt.float32
I32 = mybir.dt.int32
U8 = mybir.dt.uint8
ALU = mybir.AluOpType
ACT = mybir.ActivationFunctionType
AX = mybir.AxisListType

P = 128
SEQ, D, DEPTH = 512, 1024, 2
NT = SEQ // P
KD = D // P
HEADS, HD, GW = 4, 64, 256
NE, GROUPS, EPG, FF = 32, 4, 8, 512
KF = FF // P
CAP = 80
NOV = (2 * SEQ - NE) // CAP
ROWS = (NE + NOV) * CAP
NR = GROUPS + NE
BN = 512
NEG = -1.0e30
RMS_EPS, SUBLN_EPS, LN_EPS, RWKV_LN_EPS = 1e-6, 1e-5, 1e-5, 64e-5
LOG_DECAY = -math.exp(-0.5)
LEVELS = [1, 2, 4, 8, 16, 32, 64]


def layout(fields):
    at, out = 0, {}
    for name, n in fields:
        out[name] = (at, n)
        at += n
    return out, at


CF, NCF = layout([("ident", P), ("causal", P), ("unit", 4 * P), ("head", P), ("ones", P),
                  ("cosA", NT * 8), ("sinA", NT * 8), ("cosD", NT * 4), ("sinD", NT * 4),
                  ("down4", GROUPS), ("down8", EPG), ("slot0", NE), ("hop", NE), ("blocks", NOV)])
PC, NPC = layout([("g1", KD), ("mu", 8), ("w0", 2), ("a0", 2), ("kk", 2), ("ka", 2), ("rk", 2),
                  ("lng", 2), ("lnb", 2), ("sgub", HEADS)])
PR, NPR = layout([("sgug", GW), ("sgub", GW), ("subln", HD), ("lq1", 32), ("lk1", 32), ("lq2", 32),
                  ("lk2", 32), ("lam", 1), ("oml", 1), ("rb", NR)])


def build(nc, x, w_in, w_out, pcol, prow, w2a2, g2, sguT, router, norm2_g, w_gate, w_up, w_down,
          final_g, cf, cm, out):
    ctx, of_layer = ExitStack(), ExitStack()
    with ctx:
        def sb(name, n, dt=F32):
            return ctx.enter_context(nc.sbuf_tensor(name, [P, n], dt))

        def view(t, lo, n, pat=None, **kw):
            v = t[:, lo:lo + n]
            return v.rearrange(pat, **kw) if pat else v

        sems = []

        def sem(name):
            sems.append(of_layer.enter_context(nc.semaphore(name)))
            return sems[-1]

        X = sb("X", NT * D)
        XNTb = sb("XNT", KD * SEQ)
        RING = sb("RING", 6 * 4096)
        TOK = sb("TOK", 4 * 2048)
        XSb = sb("XS", 8 * SEQ)
        SC = sb("SCAN", 4096)
        CFs = sb("CF", NCF)
        CMs = sb("CM", 14 * P, U8)
        PCs = sb("PCOL", NPC)
        PRs = sb("PROW", NPR)
        OMU = sb("OMU", 8)
        OKA = sb("OKA", 2)
        RT = sb("ROUTER", KD * NR)
        SM = sb("SMALL", 300)
        IDX = sb("IDX", 8, I32)
        WT = sb("WT", 8)
        OVI = sb("OVI", NOV + 1, I32)
        PSALL = ctx.enter_context(nc.psum_tensor("banks", [P, 8 * BN], F32))
        PS = [PSALL[:, i * BN:(i + 1) * BN] for i in range(8)]

        def cst(name):
            lo, n = CF[name]
            return CFs[:, lo:lo + n]

        def pc(name, i):
            return PCs[:, PC[name][0] + i:PC[name][0] + i + 1]

        def pr(name):
            lo, n = PR[name]
            return PRs[:, lo:lo + n]

        X3 = X[:, :].rearrange("p (i d) -> p i d", i=NT)
        XNT = XNTb[:, :].rearrange("p (k t) -> p k t", k=KD)
        QKT = view(XNTb, 0, 2048, "p (j t) -> p j t", j=4)
        PB = view(XNTb, 2048, 2048, "p (b m t) -> p b m t", b=2, m=2)
        MT = view(XNTb, 0, 3072, "p (j t) -> p j t", j=6)
        SLOT = [RING[:, s * 4096:(s + 1) * 4096] for s in range(6)]
        SC0 = 3 * 4096
        XN = view(RING, SC0, 4096, "p (i d) -> p i d", i=NT)
        WORK = [view(RING, SC0 + 516 * i, 516) for i in range(7)]
        UB = view(RING, SC0, 4096, "p (u n) -> p u n", u=8)
        DB = view(RING, SC0 + 4096, 1024, "p (u n) -> p u n", u=8)
        EB = view(RING, SC0 + 5120, 1024, "p (u n) -> p u n", u=8)
        MB = view(RING, SC0 + 6144, 1024, "p (u n) -> p u n", u=8)
        TT = view(RING, SC0 + 7168, 1536, "p (w m n) -> p w m n", w=3, m=4)
        ZB = view(RING, SC0 + 8704, 128)
        SA = view(RING, SC0 + 8832, 128)
        ST = view(RING, SC0 + 8960, 128)
        PT = view(RING, SC0 + 9088, 1024, "p (b t) -> p b t", b=2)
        Y = view(RING, SC0 + 10112, 1024, "p (c t) -> p c t", c=2)
        W2A2 = view(RING, SC0 + 11136, 256)
        G2 = view(RING, SC0 + 11392, 256)
        SGT = view(RING, SC0 + 11648, 512, "p (h t) -> p h t", h=HEADS)
        TK = [view(TOK, b * 2048, 2048, "p (i n) -> p i n", i=NT) for b in range(4)]
        QKV = {"A": TK[0], "D": TK[2]}
        VAD, UV = TK[1], TK[3]
        XS = XSb[:, :].rearrange("p (g t) -> p g t", g=8)
        AR = view(SC, 0, 2048, "p (c m w t) -> p c m w t", c=2, m=4, w=2)
        BT = view(SC, 2048, 1024, "p (c t) -> p c t", c=2)
        KT = view(SC, 3072, 1024, "p (c t) -> p c t", c=2)
        G2ROW = view(SC, 0, D)
        XN2 = view(TOK, 0, 4096, "p (i d) -> p i d", i=NT)
        XR = [view(TOK, 4096 + b * 1024, 1024) for b in range(2)]
        XT = [view(TOK, 6144 + b * KD * CAP, KD * CAP, "p (k s) -> p k s", k=KD) for b in range(2)]
        HS = [view(XSb, b * 320, KF * CAP, "p (k s) -> p k s", k=KF) for b in range(2)]
        HT = [view(XSb, 640 + b * 320, KF * CAP, "p (k s) -> p k s", k=KF) for b in range(2)]
        YS = [view(XSb, 1280 + b * 1024, 1024) for b in range(2)]
        YG = [view(TOK, n * 1024, 1024) for n in range(8)]
        RW = view(XSb, 3328, 768)
        small_at = [0]

        def small(n):
            lo = small_at[0]
            small_at[0] += n
            assert small_at[0] <= 300
            return SM[:, lo:lo + n]

        ss1, rs1, ss2, rs2 = small(4), small(4), small(4), small(4)
        epend, enbeg, carry = small(8), small(8), small(8)
        nmx, sums, rsum = small(48), small(48), small(48)
        lamt, lamv = small(4), small(1)
        bnv, bns, srs = small(8), small(24), small(4)
        dss = small(16)
        xslots = nc.dram_tensor("x_slots", (ROWS, D), F32).ap()
        yslots = nc.dram_tensor("y_slots", (ROWS, D), F32).ap()
        xs_e = xslots.rearrange("(e s) d -> e s d", s=CAP)
        ys_e = yslots.rearrange("(e s) d -> e s d", s=CAP)
        wg_v = w_gate.rearrange("l e (p k) f -> (l e) p (k f)", p=P)
        wu_v = w_up.rearrange("l e (p k) f -> (l e) p (k f)", p=P)
        wd_v = w_down.rearrange("l e (k p) d -> (l e) p k d", p=P)

        const_in = ctx.enter_context(nc.semaphore("const_in"))
        slots_zeroed = ctx.enter_context(nc.semaphore("slots_zeroed"))
        zero_tile = ctx.enter_context(nc.semaphore("zero_tile"))
        masks_made = ctx.enter_context(nc.semaphore("masks_made"))

        scattered = ctx.enter_context(nc.semaphore("scattered"))
        gathered = [ctx.enter_context(nc.semaphore(f"gathered{n}")) for n in range(8)]

        with nc.Block() as block:
            @block.sync
            def _(sp):
                sp.dma_start(X3, x.rearrange("b (i p) d -> p (b i) d", p=P)).then_inc(const_in, 16)
                sp.dma_start(CFs[:, :], cf).then_inc(const_in, 16)
                sp.dma_start(RING[:, 0:14 * P], cm).then_inc(const_in, 16)
                sp.wait_ge(const_in, 48)

            @block.vector
            def _(dve):
                dve.wait_ge(const_in, 48)
                nc.vector.tensor_copy(CMs[:, :], RING[:, 0:14 * P]).then_inc(masks_made, 1)

            @block.gpsimd
            def _(pool):
                nc.gpsimd.memset(XR[0], 0.0).then_inc(zero_tile, 1)
                pool.wait_ge(zero_tile, 1)
                for e in range(0, NE + NOV, 4):
                    pool.dma_start(xs_e[e:e + 4, :, :].rearrange("e s d -> s e d"),
                                   XR[0][0:CAP, None, :].to_broadcast([CAP, 4, D])).then_inc(slots_zeroed, 16)
                for e in range(NE, NE + NOV, 4):
                    pool.dma_start(ys_e[e:e + 4, :, :].rearrange("e s d -> s e d"),
                                   XR[0][0:CAP, None, :].to_broadcast([CAP, 4, D])).then_inc(slots_zeroed, 16)
                pool.wait_ge(slots_zeroed, 16 * ((NE + 2 * NOV) // 4))

        params_in = sem("params_in")
        g2row_in = sem("g2row_in")
        slot_full = [sem(f"slot_full{s}") for s in range(6)]
        prep_done = sem("prep_done")
        n1_squares, n1_scaled = sem("n1_squares"), sem("n1_scaled")
        n1_turned = sem("n1_turned")
        n1_copied_a, n1_copied_v = sem("n1_copied_a"), sem("n1_copied_v")
        proj_ps, xs_scaled, xs_mixed, proj_copied = sem("proj_ps"), sem("xs_scaled"), sem("xs_mixed"), sem("proj_copied")
        lora_in = sem("lora_in")
        vec, gp, root_in, root_out = sem("vec"), sem("gp"), sem("root_in"), sem("root_out")
        cs_ready, exps_ready, scan_in, kk_sq = sem("cs_ready"), sem("exps_ready"), sem("scan_in"), sem("kk_sq")
        gelu_done, sgu_v, sgu_ps, sgu_w = sem("gelu_done"), sem("sgu_v"), sem("sgu_ps"), sem("sgu_w")
        roped = {m: sem(f"roped{m}") for m in "AD"}
        mix = {}
        for m in "AD":
            mix[m] = {n: sem(f"{n}{m}") for n in (
                "qk_ps", "qk_copied", "scores", "maxed", "exped", "probs", "pt_ps", "pt_copied", "o_ps", "o_done",
                "eye", "prod_ps", "prod_masked", "turn_ps", "turned", "m1_ps", "m1_copied",
                "de_ps", "de_merged", "z_ps", "z_copied", "sa_ps", "sa_copied", "y_ps", "y_copied", "s_ps", "s_done",
                "fin_in", "fin_ps", "fin_sq", "y_done")}
        mixed_done, mt_ps, mt_a, mt_v = sem("mixed_done"), sem("mt_ps"), sem("mt_a"), sem("mt_v")
        res_ps, res_added = sem("res_ps"), sem("res_added")
        n2_squares, n2_scaled, n2_turned, n2_copied_a, n2_copied_v = (
            sem("n2_squares"), sem("n2_scaled"), sem("n2_turned"), sem("n2_copied_a"), sem("n2_copied_v"))
        logits, exp_in, exp_done, chosen, ranks, routed = sem("logits"), sem("exp_in"), sem("exp_done"), sem("chosen"), sem("ranks"), sem("routed")
        route_in = sem("route_in")
        xt_ps, xt_copied = sem("xt_ps"), sem("xt_copied")
        gate_ps, up_ps, gated, hidden = sem("gate_ps"), sem("up_ps"), sem("gated"), sem("hidden")
        y2_ps, y2_copied, y2_stored = sem("y2_ps"), sem("y2_copied"), [sem("y2_stored0"), sem("y2_stored1")]
        ov_go, ov_in, ov_turn, ov_turned, ov_gu, ov_silu, ov_hid, ov_y, ov_out, ov_st, ov_end = (
            sem(f"ov_{n}") for n in ("go", "in", "turn", "turned", "gu", "silu", "hid", "y", "out", "st", "end"))
        combined = sem("combined")
        rows_full, rows_sent = [sem("rows_full0"), sem("rows_full1")], sem("rows_sent")
        lam_in, sgu_done = sem("lam_in"), sem("sgu_done")

        RSTEPS = ["P", "T"] + [("L", n) for n in range(1, 7)] + [("C", m) for m in range(4)] + ["F"]
        USTEPS = 18

        def half_steps():
            r, u = 0, 0
            while r < len(RSTEPS) or u < USTEPS:
                if r < len(RSTEPS):
                    yield "rwkv", RSTEPS[r]
                    r += 1
                for _ in range(2 if r % 2 else 1):
                    if u < USTEPS:
                        yield "attn", u
                        u += 1

        HALVES = [(0, "A"), (1, "D")]
        PROJ = ([("b", g) for g in range(8)] + [("t", (0, i)) for i in range(NT)] + [("l", n) for n in range(6)]
                + [("t", (1, i)) for i in range(NT)] + [("n", c) for c in range(2)]
                + [("t", (b, i)) for b in range(2, 4) for i in range(NT)])

        def copied(*group):
            return PROJ.index(group) - 7

        BLOCK_USED = [4, 8] + [PROJ.index(("t", (b, NT - 1))) + 1 for b in range(4)]
        MT_OF = {0: 0, 1: 1, 4: 2, 5: 3, 6: 4, 7: 5}
        unit_of = [(i, h) for i in range(NT) for h in range(HEADS)]

        with nc.Fori(0, DEPTH) as layer:
            with nc.Block() as block:

                @block.sync
                def _(sp):
                    one = bass.ds(layer, 1)
                    for dst, src in ((PCs[:, :], pcol[one].rearrange("a p n -> p (a n)")),
                                     (PRs[:, :], prow[one, :].to_broadcast([P, NPR])),
                                     (W2A2, w2a2[one].rearrange("a p n -> p (a n)")),
                                     (G2, g2[one].rearrange("a p n -> p (a n)")),
                                     (SGT, sguT[one].rearrange("a p h t -> p (a h) t")),
                                     (RT[:, :], router[one].rearrange("a p n -> p (a n)"))):
                        sp.dma_start(dst, src).then_inc(params_in, 16)
                    for n in range(6):
                        if n >= 3:
                            sp.wait_ge(proj_ps, BLOCK_USED[n - 3])
                        sp.dma_start(SLOT[n % 3], w_in[one, n].rearrange("a p n -> p (a n)")).then_inc(slot_full[n % 3], 16)
                    for n in range(2):
                        sp.wait_ge(proj_ps, BLOCK_USED[n + 3])
                        sp.dma_start(SLOT[n], w_out[one, n].rearrange("a p n -> p (a n)")).then_inc(slot_full[n], 16)

                    def load(e, h, waits):
                        for m, v in enumerate((wg_v, wu_v, wd_v)):
                            s = (2 + 3 * h + m) % 6
                            sp.wait_ge(*waits[m])
                            src = v[bass.ds(layer * NE + e, 1)]
                            if m < 2:
                                sp.dma_start(SLOT[s], src.rearrange("a p n -> p (a n)")).then_inc(slot_full[s], 16)
                            else:
                                sp.dma_start(SLOT[s].rearrange("p (k d) -> p k d", k=KF),
                                             src.rearrange("a p k d -> p (a k) d")).then_inc(slot_full[s], 16)

                    load(0, 0, [(proj_ps, BLOCK_USED[5]), (mixed_done, 1), (mixed_done, 1)])
                    sp.dma_start(G2ROW, norm2_g[one, :].to_broadcast([P, D])).then_inc(g2row_in, 16)
                    load(1, 1, [(res_ps, 8), (res_ps, 8), (res_ps, 8)])
                    def load_rows(e, h):
                        sp.dma_start(XR[h][0:CAP, :], xs_e[bass.ds(e, 1)].rearrange("a s d -> s (a d)")).then_inc(rows_full[h], 16)

                    sp.wait_ge(rows_sent, 1)
                    load_rows(0, 0)
                    load_rows(1, 1)
                    with sp.Fori(1, NE // 2) as i:
                        for h in range(2):
                            e = 2 * i + h
                            sp.wait_ge(xt_ps, e - 1)
                            load_rows(e, h)
                            load(e, h, [(gate_ps, e - 1), (up_ps, e - 1), (y2_ps, e - 1)])
                    sp.wait_ge(xt_ps, NE - 1)
                    load_rows(NE, 0)
                    sp.wait_ge(routed, 1)
                    nov = sp.value_load(OVI[0:1, NOV:NOV + 1], min_val=0, max_val=NOV)
                    with sp.If(nov > 0):
                        with sp.Fori(0, nov) as j:
                            sp.wait_ge(ov_go, j + 1)
                            e = sp.value_load(OVI[0:1, bass.ds(j, 1)], min_val=0, max_val=NE - 1)
                            w = layer * NE + e
                            sp.dma_start(SLOT[0], wg_v[bass.ds(w, 1)].rearrange("a p n -> p (a n)")).then_inc(ov_in, 16)
                            sp.dma_start(SLOT[1], wu_v[bass.ds(w, 1)].rearrange("a p n -> p (a n)")).then_inc(ov_in, 16)
                            sp.dma_start(SLOT[2].rearrange("p (k d) -> p k d", k=KF),
                                         wd_v[bass.ds(w, 1)].rearrange("a p k d -> p (a k) d")).then_inc(ov_in, 16)
                            sp.dma_start(XR[1][0:CAP, :], xs_e[bass.ds(j + NE, 1)].rearrange("a s d -> s (a d)")).then_inc(ov_in, 16)
                            sp.wait_ge(ov_out, j + 1)
                            sp.dma_start(ys_e[bass.ds(j + NE, 1)].rearrange("a s d -> s (a d)"), YS[0][0:CAP, :]).then_inc(ov_st, 16)
                            sp.wait_ge(ov_st, 16 * (j + 1))
                            sp.sem_inc(ov_go, 1)
                    sp.sem_inc(ov_end, 1)

                @block.tensor
                def _(pe):
                    mm, tr = nc.tensor.matmul, nc.tensor.transpose
                    ident = cst("ident")

                    for k in range(KD):
                        for i in range(NT):
                            if k == 0:
                                pe.wait_ge(n1_scaled, i + 1)
                            last = tr(PS[k][:, i * P:(i + 1) * P], XN[:, i, k * P:(k + 1) * P], ident)
                        last.then_inc(n1_turned, 1)

                    pe.wait_ge(n1_copied_a, 4)
                    pe.wait_ge(n1_copied_v, 4)
                    for g, (kind, a) in enumerate(PROJ):
                        bank = PS[g % 8]
                        if g >= 8:
                            if g < 16:
                                pe.wait_ge(xs_mixed, g - 7)
                            else:
                                pe.wait_ge(proj_copied, g - 15)
                        if kind == "b":
                            n, j = g // 4, g % 4
                            if j == 0:
                                pe.wait_ge(slot_full[n], 16)
                            w = SLOT[n].rearrange("p (k n) -> p k n", k=KD)
                            for k in range(KD):
                                last = mm(bank[:, :], w[:, k, j * P:(j + 1) * P], XNT[:, k, :], start=(k == 0), stop=(k == KD - 1))
                            last.then_inc(proj_ps, 1)
                        elif kind == "t":
                            b, i = a
                            n = b + 2
                            if i == 0:
                                pe.wait_ge(slot_full[n % 3], 16 * (n // 3 + 1))
                            w = SLOT[n % 3].rearrange("p (k n) -> p k n", k=KD)
                            for k in range(KD):
                                last = mm(bank[:, :], XNT[:, k, i * P:(i + 1) * P], w[:, k, :], start=(k == 0), stop=(k == KD - 1))
                            last.then_inc(proj_ps, 1)
                        elif kind == "n":
                            pe.wait_ge(kk_sq, a + 1)
                            mm(bank[:, :], cst("head"), WORK[5 + a][:, 0:SEQ], start=True, stop=True).then_inc(proj_ps, 1)
                        else:
                            w, c = divmod(a, 2)
                            cols = slice(c * P, (c + 1) * P)
                            if a == 0:
                                pe.wait_ge(params_in, 96)
                                pe.wait_ge(lora_in, 1)
                                pe.wait_ge(xs_mixed, 8)
                            if w == 0:
                                last = mm(bank[:, :], W2A2[0:64, cols], XS[0:64, 0, :], start=True, stop=True)
                            elif w == 1:
                                last = mm(bank[:, :], W2A2[64:128, cols], XS[64:128, 0, :], start=True, stop=True)
                            else:
                                pe.wait_ge(lora_in, 2)
                                last = mm(bank[:, :], G2[:, cols], XS[:, 5, :], start=True, stop=True)
                            last.then_inc(proj_ps, 1)

                    pe.wait_ge(proj_copied, len(PROJ) - 8)
                    pe.wait_ge(sgu_v, 1)
                    pe.wait_ge(sgu_w, 1)
                    for i in range(NT):
                        for h in range(HEADS):
                            last = mm(PS[6 + i // 2][:, (i % 2) * GW + h * HD:(i % 2) * GW + (h + 1) * HD],
                                      SGT[:, h, :], UV[:, i, GW + h * HD:GW + (h + 1) * HD], start=True, stop=True)
                    last.then_inc(sgu_ps, 1)

                    def rwkv(c, m, step):
                        s = mix[m]
                        head = lambda t, j: t[j * HD:(j + 1) * HD]
                        if step == "P":
                            pe.wait_ge(scan_in, c + 1)
                            if c:
                                pe.wait_ge(mix["A"]["y_done"], 1)
                            for u in range(8):
                                ch, j = divmod(u, 2)
                                if u >= 2:
                                    pe.wait_ge(s["prod_masked"], u - 1)
                                bank, t = PS[1 + u % 2], slice(ch * P, (ch + 1) * P)
                                ar = head(AR[:, c, ch, :, :], j).rearrange("p w t -> p (w t)")
                                mm(bank[:, 0:256], head(BT[:, c, t], j), ar, start=True, stop=True)
                                mm(bank[:, 256:512], head(KT[:, c, t], j), ar, start=True, stop=True).then_inc(s["prod_ps"], 1)
                            for j in range(2):
                                for ch in range(4):
                                    last = mm(PS[3 + j][:, ch * P:(ch + 1) * P], head(AR[:, c, ch, 0, :], j),
                                              head(BT[:, c, ch * P:(ch + 1) * P], j), start=True, stop=True)
                                last.then_inc(s["prod_ps"], 1)
                        elif step == "T":
                            pe.wait_ge(s["prod_masked"], 10)
                            for w, src in enumerate((BT[:, c, :], KT[:, c, :], XS[:, 3 + c, :])):
                                for ch in range(4):
                                    last = tr(PS[1 + w][:, ch * P:(ch + 1) * P], src[:, ch * P:(ch + 1) * P], ident)
                                last.then_inc(s["turn_ps"], 1)
                        elif step[0] == "L":
                            n = step[1]
                            for q in range(2):
                                if n == 1:
                                    pe.wait_ge(s["turned"], 3)
                                    pe.wait_ge(s["eye"], 6)
                                else:
                                    pe.wait_ge(s["de_merged"], 4 * (n - 2) + 2 * q + 2)
                                for w in range(4):
                                    u = 4 * q + w
                                    last = mm(PS[1 + q][:, w * P:(w + 1) * P], UB[:, u, 0:P], DB[:, u, :], start=True, stop=True)
                                last.then_inc(s["m1_ps"], 1)
                            for q in range(2):
                                pe.wait_ge(s["m1_copied"], 2 * (n - 1) + q + 1)
                                for side in range(2):
                                    if n == 6 and side == 0:
                                        continue
                                    if n == 6:
                                        pe.wait_ge(s["de_merged"], 20 + q)
                                    elif n > 1 or q > 0:
                                        pe.wait_ge(s["de_merged"], 4 * (n - 1) + 2 * q + side - 1)
                                    for w in range(4):
                                        u = 4 * q + w
                                        if side == 0:
                                            last = mm(PS[3][:, w * P:(w + 1) * P], EB[:, u, :], MB[:, u, :], start=True, stop=True)
                                        else:
                                            last = mm(PS[4][:, w * P:(w + 1) * P], MB[:, u, :], EB[:, u, :], start=True, stop=True)
                                    last.then_inc(s["de_ps"], 1)
                        elif step[0] == "C":
                            ch = step[1]
                            if ch == 0:
                                pe.wait_ge(s["de_merged"], 22)
                            else:
                                pe.wait_ge(s["s_done"], ch)
                            v = lambda j: TT[:, 2, ch, j * HD:(j + 1) * HD]
                            hc = lambda j: slice(j * HD, (j + 1) * HD)
                            for j in range(2):
                                last = mm(PS[1][:, hc(j)], UB[:, 2 * ch + j, 256:384], v(j), start=(j == 0), stop=(ch == 0 and j == 1))
                            if ch:
                                last = mm(PS[1][:, 0:P], AR[:, c, ch, 0, :], ST, start=False, stop=True)
                            last.then_inc(s["z_ps"], 1)
                            pe.wait_ge(s["z_copied"], ch + 1)
                            for j in range(2):
                                last = mm(PS[2][:, hc(j)], EB[:, 2 * ch + j, :], ZB[:, hc(j)], start=True, stop=True)
                            last.then_inc(s["sa_ps"], 1)
                            pe.wait_ge(s["sa_copied"], ch + 1)
                            if ch < 3:
                                mm(PS[4][:, 0:P], TT[:, 0, ch, :], SA, start=True, stop=False)
                                last = mm(PS[4][:, 0:P], TT[:, 1, ch, :], TT[:, 2, ch, :], start=False, stop=True)
                                last.then_inc(s["s_ps"], 1)
                            if ch:
                                pe.wait_ge(s["y_copied"], ch)
                            for j in range(2):
                                u, o = 2 * ch + j, PS[3][j * HD:(j + 1) * HD, 0:P]
                                mm(o, SA[:, hc(j)], UB[:, u, 128:256], start=True, stop=False)
                                last = mm(o, v(j), UB[:, u, 384:512], start=False, stop=(ch == 0))
                            if ch:
                                last = mm(PS[3][:, 0:P], ST, AR[:, c, ch, 1, :], start=False, stop=True)
                            last.then_inc(s["y_ps"], 1)
                        else:
                            pe.wait_ge(s["y_copied"], 4)
                            mm(PS[1][:, :], cst("head"), Y[:, c, :], start=True, stop=True).then_inc(s["fin_ps"], 1)
                            pe.wait_ge(s["fin_in"], 1)
                            mm(PS[2][:, :], cst("head"), UB[:, 1, :], start=True, stop=True).then_inc(s["fin_ps"], 1)
                            pe.wait_ge(s["fin_sq"], 1)
                            mm(PS[3][:, :], cst("head"), UB[:, 2, :], start=True, stop=True).then_inc(s["fin_ps"], 1)

                    def attn(m, u):
                        s, nm = mix[m], 2 if m == "D" else 1
                        if u == 0:
                            pe.wait_ge(roped[m], 2)
                            pe.wait_ge(sgu_done, 1)
                            for j in range(4):
                                if j >= 2:
                                    pe.wait_ge(s["qk_copied"], j - 1)
                                for i in range(NT):
                                    last = tr(PS[5 + j % 2][:, i * P:(i + 1) * P], QKV[m][:, i, j * P:(j + 1) * P], ident)
                                last.then_inc(s["qk_ps"], 1)
                            pe.wait_ge(s["qk_copied"], 4)
                        if u < 16:
                            i, h = unit_of[u]
                            w = (i + 1) * P
                            for a in range(nm):
                                n = u if m == "A" else 2 * u + a
                                if n >= 2:
                                    pe.wait_ge(s["exped"], n - 1)
                                if m == "A":
                                    rows = slice((h % 2) * 64, (h % 2) * 64 + 64)
                                else:
                                    rows = slice((h % 2) * 64 + a * 32, (h % 2) * 64 + a * 32 + 32)
                                bank = PS[5 + n % 2]
                                mm(bank[:, 0:w], QKT[rows, h // 2, i * P:w], QKT[rows, 2 + h // 2, 0:w], start=True, stop=False)
                                mm(bank[:, i * P:w], ident, cst("causal"), start=False, stop=True).then_inc(s["scores"], 1)
                        if 1 <= u <= 16:
                            i, h = unit_of[u - 1]
                            pe.wait_ge(s["exped"] if m == "A" else s["probs"], u)
                            if u >= 2:
                                pe.wait_ge(s["pt_copied"], u - 1)
                            for b in range(i + 1):
                                last = tr(PS[7][:, b * P:(b + 1) * P], PB[:, (u - 1) % 2, nm - 1, b * P:(b + 1) * P], ident)
                            last.then_inc(s["pt_ps"], 1)
                        if u >= 2:
                            n = u - 2
                            i, h = unit_of[n]
                            pe.wait_ge(s["pt_copied"], n + 1)
                            if n >= 1:
                                pe.wait_ge(s["o_done"], n)
                            elif m == "D":
                                pe.wait_ge(mix["A"]["o_done"], 16)
                            v0 = (0 if m == "A" else GW) + h * HD
                            for b in range(i + 1):
                                last = mm(PS[0][:, 0:HD], PT[:, n % 2, b * P:(b + 1) * P], VAD[:, b, v0:v0 + HD],
                                          start=(b == 0), stop=(b == i))
                            last.then_inc(s["o_ps"], 1)

                    for c, m in HALVES:
                        for kind, step in half_steps():
                            rwkv(c, m, step) if kind == "rwkv" else attn(m, step)

                    pe.wait_ge(mixed_done, 1)
                    srcs = [(QKV["A"], 0), (QKV["A"], 1), (UV, 0), (UV, 1), (QKV["D"], 0), (QKV["D"], 1)]
                    for j, (src, t) in enumerate(srcs):
                        for i in range(NT):
                            last = tr(PS[j][:, i * P:(i + 1) * P], src[:, i, t * P:(t + 1) * P], ident)
                        last.then_inc(mt_ps, 1)
                    pe.wait_ge(mt_a, 3)
                    pe.wait_ge(mt_v, 3)
                    for n in range(2):
                        pe.wait_ge(slot_full[n], 48)
                        w = SLOT[n].rearrange("p (k n) -> p k n", k=KD)
                        for i in range(NT):
                            for k in range(KD):
                                src = Y[:, k - 2, :] if k in (2, 3) else MT[:, MT_OF[k], :]
                                last = mm(PS[4 * n + i][:, :], src[:, i * P:(i + 1) * P], w[:, k, :], start=(k == 0), stop=(k == KD - 1))
                            last.then_inc(res_ps, 1)

                    pe.wait_ge(res_added, 8)
                    for k in range(KD):
                        for i in range(NT):
                            if k == 0:
                                pe.wait_ge(n2_scaled, i + 1)
                            last = tr(PS[k][:, i * P:(i + 1) * P], XN2[:, i, k * P:(k + 1) * P], ident)
                        last.then_inc(n2_turned, 1)
                    pe.wait_ge(n2_copied_a, 4)
                    pe.wait_ge(n2_copied_v, 4)
                    rw = RT[:, :].rearrange("p (k n) -> p k n", k=KD)
                    for i in range(NT):
                        for k in range(KD):
                            last = mm(PS[0][:, i * NR:(i + 1) * NR], XNT[:, k, i * P:(i + 1) * P], rw[:, k, :], start=(k == 0), stop=(k == KD - 1))
                    last.then_inc(logits, 1)
                    pe.wait_ge(chosen, 1)
                    M = RW[:, 0:NT * NE].rearrange("p (i e) -> p i e", i=NT)
                    before_me = CFs[:, CF["unit"][0]:CF["unit"][0] + P]
                    for i in range(NT):
                        o = PS[1][:, i * NE:(i + 1) * NE]
                        mm(o, before_me, M[:, i, :], start=True, stop=(i == 0))
                        for b in range(i):
                            mm(o, cst("ones"), M[:, b, :], start=False, stop=(b == i - 1))
                    for i in range(NT):
                        last = mm(PS[1][:, NT * NE:(NT + 1) * NE], cst("ones"), M[:, i, :], start=(i == 0), stop=(i == NT - 1))
                    last.then_inc(ranks, 1)

                    def turn_rows(src, done):
                        rows = src[0:CAP, :].rearrange("s (p k) -> s p k", k=KD)
                        for k in range(KD):
                            last = tr(PS[k // 4][:, (k % 4) * CAP:(k % 4 + 1) * CAP], rows[:, :, k], ident[0:CAP, 0:CAP])
                        last.then_inc(done, 1)

                    def gate_or_up(w, bank, xt):
                        w = w.rearrange("p (k n) -> p k n", k=KD)
                        for f in range(KF):
                            for k in range(KD):
                                last = mm(bank[:, f * CAP:(f + 1) * CAP], w[:, k, f * P:(f + 1) * P], xt[:, k, :], start=(k == 0), stop=(k == KD - 1))
                        return last

                    def down(w, ht):
                        w = w.rearrange("p (k d) -> p k d", k=KF)
                        for n in range(2):
                            for k in range(KF):
                                last = mm(PS[6 + n][0:CAP, :], ht[:, k, :], w[:, k, n * BN:(n + 1) * BN], start=(k == 0), stop=(k == KF - 1))
                        return last

                    pe.wait_ge(route_in, 1)
                    pe.wait_ge(rows_full[0], 16)
                    turn_rows(XR[0], xt_ps)
                    full0 = (3, 3, 2, 0, 0, 0)
                    with pe.Fori(0, NE // 2) as i:
                        for h in range(2):
                            e = 2 * i + h
                            sg, su, sd = [(2 + 3 * h + m) % 6 for m in range(3)]
                            pe.wait_ge(xt_copied, e + 1)
                            pe.wait_ge(slot_full[sg], 16 * (i + full0[sg] + 1))
                            pe.wait_ge(hidden, e + 1)
                            gate_or_up(SLOT[sg], PS[2 + h], XT[h]).then_inc(gate_ps, 1)
                            pe.wait_ge(slot_full[su], 16 * (i + full0[su] + 1))
                            gate_or_up(SLOT[su], PS[4 + h], XT[h]).then_inc(up_ps, 1)
                            if h == 0:
                                pe.wait_ge(rows_full[1], 16 * (i + 1))
                            else:
                                pe.wait_ge(rows_full[0], 16 * (i + 2))
                            turn_rows(XR[1 - h], xt_ps)
                            pe.wait_ge(hidden, e + 3)
                            pe.wait_ge(slot_full[sd], 16 * (i + full0[sd] + 1))
                            pe.wait_ge(y2_copied, e + 1)
                            down(SLOT[sd], HT[h]).then_inc(y2_ps, 1)
                    pe.wait_ge(xt_copied, NE + 1)
                    pe.wait_ge(y2_ps, NE)
                    pe.sem_inc(ov_go, 1)
                    nov = pe.value_load(OVI[0:1, NOV:NOV + 1], min_val=0, max_val=NOV)
                    with pe.If(nov > 0):
                        pe.wait_ge(y2_copied, NE + 1)
                        with pe.Fori(0, nov) as j:
                            pe.wait_ge(ov_in, 64 * (j + 1))
                            turn_rows(XR[1], ov_turn)
                            pe.wait_ge(ov_turned, j + 1)
                            gate_or_up(SLOT[0], PS[2], XT[1])
                            gate_or_up(SLOT[1], PS[4], XT[1]).then_inc(ov_gu, 1)
                            pe.wait_ge(ov_hid, j + 1)
                            down(SLOT[2], HT[0]).then_inc(ov_y, 1)
                    pe.nop()

                @block.scalar
                def _(act):
                    ac = nc.scalar.activation
                    roots = [0]

                    def root(t):
                        roots[0] += 1
                        act.wait_ge(root_in, roots[0])
                        ac(t, t, ACT.Sqrt).then_inc(root_out, 1)

                    for i in range(NT):
                        ac(XNTb[:, i * D:(i + 1) * D], X3[:, i, :], ACT.Square,
                           accum_out=ss1[:, i:i + 1]).then_inc(n1_squares, 1)
                    root(rs1)
                    act.wait_ge(params_in, 96)
                    act.wait_ge(n1_scaled, 4)
                    for k in range(0, KD, 2):
                        act.wait_ge(n1_turned, k + 1)
                        ac(XNT[:, k, :], PS[k][:, :], ACT.Copy, scale=pc("g1", k)).then_inc(n1_copied_a, 1)
                    act.wait_ge(prep_done, 1)
                    for g in range(8):
                        act.wait_ge(proj_ps, g + 1)
                        ac(XS[:, g, :], PS[g][:, :], ACT.Copy, scale=OMU[:, g:g + 1]).then_inc(xs_scaled, 1)
                        if g == 6:
                            act.wait_ge(xs_mixed, 1)
                            ac(XS[0:64, 0, :], XS[0:64, 0, :], ACT.Tanh).then_inc(lora_in, 1)
                        if g == 7:
                            act.wait_ge(xs_mixed, 6)
                            ac(XS[:, 5, :], XS[:, 5, :], ACT.Sigmoid).then_inc(lora_in, 1)
                    for g, (kind, a) in enumerate(PROJ):
                        if kind == "b":
                            continue
                        act.wait_ge(proj_ps, g + 1)
                        src = PS[g % 8][:, :]
                        if kind == "t":
                            b, i = a
                            dst = (TK[0], TK[1], TK[2], TK[3])[b][:, i, :]
                            ac(dst, src, ACT.Copy).then_inc(proj_copied, 1)
                        elif kind == "n":
                            ac(WORK[5 + a][:, 0:SEQ], src, ACT.Sqrt).then_inc(proj_copied, 1)
                        else:
                            w, c = divmod(a, 2)
                            if w == 0:
                                ac(WORK[0 + c][:, 0:SEQ], src, ACT.Sigmoid, bias=pc("w0", c)).then_inc(proj_copied, 1)
                            elif w == 1:
                                ac(WORK[2 + c][:, 0:SEQ], src, ACT.Sigmoid, bias=pc("a0", c)).then_inc(proj_copied, 1)
                            else:
                                ac(XS[:, (0, 5)[c], :], src, ACT.Copy).then_inc(proj_copied, 1)
                    for c in range(2):
                        act.wait_ge(cs_ready, c + 1)
                        if c:
                            act.wait_ge(scan_in, 1)
                        ac(WORK[4], WORK[0], ACT.Exp).then_inc(exps_ready, 1)
                        ac(WORK[2], WORK[0], ACT.Exp, scale=-1.0).then_inc(exps_ready, 1)
                    act.wait_ge(lam_in, 1)
                    ac(lamt[:, 0:2], lamt[:, 0:2], ACT.Exp).then_inc(lam_in, 1)
                    for t in range(2):
                        ac(UV[:, 2 * t:2 * t + 2, :], UV[:, 2 * t:2 * t + 2, :], ACT.Gelu).then_inc(gelu_done, 1)
                    root(srs)

                    def rwkv(c, m, step):
                        s = mix[m]
                        if step == "T":
                            for w in range(3):
                                act.wait_ge(s["turn_ps"], w + 1)
                                ac(TT[:, w, :, :].rearrange("p m n -> p (m n)"), PS[1 + w][:, :], ACT.Copy).then_inc(s["turned"], 1)
                        elif step[0] == "L":
                            for q in range(2):
                                act.wait_ge(s["m1_ps"], 2 * (step[1] - 1) + q + 1)
                                if step[1] > 1:
                                    act.wait_ge(s["de_ps"], 4 * (step[1] - 2) + 2 * q + 2)
                                ac(MB[:, 4 * q:4 * q + 4, :].rearrange("p u n -> p (u n)"), PS[1 + q][:, :], ACT.Copy).then_inc(s["m1_copied"], 1)
                        elif step[0] == "C":
                            ch = step[1]
                            act.wait_ge(s["z_ps"], ch + 1)
                            ac(ZB, PS[1][:, 0:P], ACT.Copy).then_inc(s["z_copied"], 1)
                            act.wait_ge(s["y_ps"], ch + 1)
                            ac(Y[:, c, ch * P:(ch + 1) * P], PS[3][:, 0:P], ACT.Copy).then_inc(s["y_copied"], 1)
                        elif step == "F":
                            act.wait_ge(s["fin_in"], 2)
                            ac(UB[:, 2, :], Y[:, c, :], ACT.Square).then_inc(s["fin_sq"], 1)
                            root(UB[:, 3, :])

                    def attn(m, u):
                        s, nm = mix[m], 2 if m == "D" else 1
                        if u == 0:
                            scale = float(HD) ** -0.5 if m == "A" else 32.0 ** -0.5
                            for j in range(4):
                                act.wait_ge(s["qk_ps"], j + 1)
                                ac(QKT[:, j, :], PS[5 + j % 2][:, :], ACT.Copy, scale=scale if j < 2 else 1.0).then_inc(s["qk_copied"], 1)
                        if u < 16:
                            i, h = unit_of[u]
                            w = (i + 1) * P
                            if u >= 2:
                                act.wait_ge(s["pt_ps"], u - 1)
                            for a in range(nm):
                                n = nm * u + a
                                col = (0 if m == "A" else 16) + n
                                act.wait_ge(s["maxed"], n + 1)
                                ac(PB[:, u % 2, a, 0:w], PS[5 + n % 2][:, 0:w], ACT.Exp, bias=nmx[:, col:col + 1],
                                   accum_out=sums[:, col:col + 1]).then_inc(s["exped"], 1)
                        if 1 <= u <= 16:
                            i, h = unit_of[u - 1]
                            w = (i + 1) * P
                            act.wait_ge(s["pt_ps"], u)
                            if u >= 3:
                                act.wait_ge(s["o_ps"], u - 2)
                            ac(PT[:, (u - 1) % 2, 0:w], PS[7][:, 0:w], ACT.Copy).then_inc(s["pt_copied"], 1)

                    for c, m in HALVES:
                        for kind, step in half_steps():
                            rwkv(c, m, step) if kind == "rwkv" else attn(m, step)
                    root(dss)
                    for j in range(0, 6, 2):
                        act.wait_ge(mt_ps, j + 1)
                        ac(MT[:, j, :], PS[j][:, :], ACT.Copy).then_inc(mt_a, 1)
                    for i in range(NT):
                        act.wait_ge(res_added, 5 + i)
                        ac(TOK[:, i * D:(i + 1) * D], X3[:, i, :], ACT.Square, accum_out=ss2[:, i:i + 1]).then_inc(n2_squares, 1)
                    root(rs2)
                    for k in range(0, KD, 2):
                        act.wait_ge(n2_turned, k + 1)
                        ac(XNT[:, k, :], PS[k][:, :], ACT.Copy).then_inc(n2_copied_a, 1)
                    act.wait_ge(exp_in, 1)
                    ac(RW[:, 640:640 + 16], RW[:, 640:640 + 16], ACT.Exp).then_inc(exp_done, 1)
                    act.wait_ge(exp_in, 2)
                    ac(RW[:, 656:660], RW[:, 656:660], ACT.Exp).then_inc(exp_done, 1)

                    act.sem_inc(y2_copied, 1)
                    for h in range(2):
                        act.sem_inc(y2_stored[h], 16)
                    with act.Fori(0, NE // 2) as i:
                        for h in range(2):
                            e = 2 * i + h
                            act.wait_ge(gate_ps, e + 1)
                            ac(HS[h].rearrange("p k s -> p (k s)"), PS[2 + h][:, 0:KF * CAP], ACT.Silu).then_inc(gated, 1)
                            act.wait_ge(y2_ps, e + 1)
                            act.wait_ge(y2_stored[h], 16 * (i + 1))
                            ac(YS[h][0:CAP, :], PSALL[0:CAP, 6 * BN:8 * BN], ACT.Copy).then_inc(y2_copied, 1)
                            act.wait_ge(y2_copied, e + 2)
                            act.dma_start(ys_e[bass.ds(e, 1)].rearrange("a s d -> s (a d)"), YS[h][0:CAP, :]).then_inc(y2_stored[h], 16)
                    nov = act.value_load(OVI[0:1, NOV:NOV + 1], min_val=0, max_val=NOV)
                    for h in range(2):
                        act.wait_ge(y2_stored[h], 16 * (NE // 2 + 1))
                    with act.If(nov > 0):
                        with act.Fori(0, nov) as j:
                            act.wait_ge(ov_gu, j + 1)
                            ac(HS[0].rearrange("p k s -> p (k s)"), PS[2][:, 0:KF * CAP], ACT.Silu).then_inc(ov_silu, 1)
                            act.wait_ge(ov_y, j + 1)
                            ac(YS[0][0:CAP, :], PSALL[0:CAP, 6 * BN:8 * BN], ACT.Copy).then_inc(ov_out, 1)
                    act.nop()

                @block.vector
                def _(dve):
                    V = nc.vector
                    count, roots = [0], [0]

                    def link(ins):
                        count[0] += 1
                        ins.then_inc(vec, 1)
                        dve.wait_ge(vec, count[0])

                    def rstd(out, ss, scale, eps):
                        V.tensor_scalar(out, ss, scale, eps, ALU.mult, ALU.add).then_inc(root_in, 1)
                        roots[0] += 1
                        dve.wait_ge(root_out, roots[0])
                        link(V.reciprocal(out, out))

                    dve.wait_ge(n1_squares, 4)
                    rstd(rs1, ss1, 1.0 / D, RMS_EPS)
                    for i in range(NT):
                        V.tensor_scalar(XN[:, i, :], X3[:, i, :], rs1[:, i:i + 1], None, ALU.mult).then_inc(n1_scaled, 1)
                    dve.wait_ge(params_in, 96)
                    link(V.tensor_scalar(OMU[:, :], PCs[:, PC["mu"][0]:PC["mu"][0] + 8], -1.0, 1.0, ALU.mult, ALU.add))
                    V.tensor_scalar(OKA[:, :], PCs[:, PC["ka"][0]:PC["ka"][0] + 2], -1.0, 1.0, ALU.mult, ALU.add).then_inc(prep_done, 1)
                    for k in range(1, KD, 2):
                        dve.wait_ge(n1_turned, k + 1)
                        V.tensor_scalar(XNT[:, k, :], PS[k][:, :], pc("g1", k), None, ALU.mult).then_inc(n1_copied_v, 1)
                    V.tensor_tensor(SGT, SGT, CFs[:, CF["unit"][0] + P:CF["unit"][0] + 2 * P][:, None, :].to_broadcast([P, HEADS, P]),
                                    ALU.mult).then_inc(sgu_w, 1)
                    lt = SA[:, 0:64]
                    link(V.tensor_tensor(lt[:, 0:32], pr("lq1"), pr("lk1"), ALU.mult))
                    link(V.tensor_tensor(lt[:, 32:64], pr("lq2"), pr("lk2"), ALU.mult))
                    V.tensor_reduce(lamt[:, 0:2], lt.rearrange("p (a n) -> p a n", a=2), AX.X, ALU.add).then_inc(lam_in, 1)
                    for g in range(8):
                        dve.wait_ge(xs_scaled, g + 1)
                        V.scalar_tensor_tensor(XS[:, g, 1:], PS[g][:, 0:SEQ - 1], pc("mu", g), XS[:, g, 1:], ALU.mult, ALU.add).then_inc(xs_mixed, 1)
                    dve.wait_ge(xs_mixed, 8)
                    for c in range(2):
                        link(V.tensor_scalar(BT[:, c, :], XS[:, 1 + c, :], pc("kk", c), None, ALU.mult))
                        V.tensor_tensor(WORK[5 + c][:, 0:SEQ], BT[:, c, :], BT[:, c, :], ALU.mult).then_inc(kk_sq, 1)
                    for c in range(2):
                        dve.wait_ge(proj_copied, copied("n", c))
                        a, k, b = WORK[2 + c][:, 0:SEQ], XS[:, 1 + c, :], BT[:, c, :]
                        link(V.tensor_scalar(WORK[5][:, 0:SEQ], WORK[5 + c][:, 0:SEQ], 1e-12, None, ALU.max))
                        link(V.reciprocal(WORK[5][:, 0:SEQ], WORK[5][:, 0:SEQ]))
                        link(V.tensor_tensor(b, b, WORK[5][:, 0:SEQ], ALU.mult))
                        link(V.tensor_scalar(WORK[5][:, 0:SEQ], a, pc("ka", c), OKA[:, c:c + 1], ALU.mult, ALU.add))
                        link(V.tensor_tensor(k, k, WORK[5][:, 0:SEQ], ALU.mult))
                        link(V.tensor_tensor(KT[:, c, :], b, a, ALU.mult))
                        sg = WORK[0 + c][:, 0:SEQ].rearrange("p (m t) -> p m t", m=4)
                        cs = WORK[5]
                        cs3 = cs.rearrange("p (m t) -> p m t", m=4)
                        link(V.memset(cs3[:, :, 0:1], 0.0))
                        for ch in range(4):
                            link(V.tensor_tensor_scan(cs3[:, ch, 1:P + 1], cst("ones"), sg[:, ch, :], 0.0, ALU.mult, ALU.add))
                        link(V.tensor_tensor(WORK[0].rearrange("p (m t) -> p m t", m=4), cs3,
                                             cs3[:, :, 64:65].to_broadcast([P, 4, P + 1]), ALU.subtract))
                        V.tensor_scalar(WORK[0], WORK[0], LOG_DECAY, None, ALU.mult).then_inc(cs_ready, 1)
                        dve.wait_ge(exps_ready, 2 * c + 2)
                        ep = WORK[4].rearrange("p (m t) -> p m t", m=4)
                        en = WORK[2].rearrange("p (m t) -> p m t", m=4)
                        b3 = b.rearrange("p (m t) -> p m t", m=4)
                        kb3 = KT[:, c, :].rearrange("p (m t) -> p m t", m=4)
                        link(V.tensor_copy(epend[:, 4 * c:4 * c + 4], ep[:, :, P]))
                        link(V.tensor_copy(enbeg[:, 4 * c:4 * c + 4], en[:, :, 0]))
                        link(V.tensor_tensor(carry[:, 4 * c:4 * c + 3], epend[:, 4 * c:4 * c + 3], enbeg[:, 4 * c + 1:4 * c + 4], ALU.mult))
                        link(V.scalar_tensor_tensor(AR[:, c, :, 0, :], b3, -1.0, ep[:, :, 0:P], ALU.mult, ALU.mult))
                        link(V.tensor_tensor(AR[:, c, :, 1, :], XS[:, 6 + c, :].rearrange("p (m t) -> p m t", m=4), ep[:, :, 1:], ALU.mult))
                        link(V.tensor_tensor(b3, kb3, en[:, :, 1:], ALU.mult))
                        V.tensor_tensor(kb3, k.rearrange("p (m t) -> p m t", m=4), en[:, :, 1:], ALU.mult).then_inc(scan_in, 1)
                    dve.wait_ge(gelu_done, 2)
                    for i in range(NT):
                        link(V.bn_stats(bns[:, 6 * i:6 * i + 6], UV[:, i, GW:]))
                        link(V.bn_aggr(bnv[:, 2 * i:2 * i + 2], bns[:, 6 * i:6 * i + 6]))
                    rstd(srs, bnv.rearrange("p (i t) -> p i t", t=2)[:, :, 1], 1.0, LN_EPS)
                    for i in range(NT):
                        link(V.tensor_scalar(UV[:, i, GW:], UV[:, i, GW:], bnv[:, 2 * i:2 * i + 1], srs[:, i:i + 1], ALU.subtract, ALU.mult))
                    link(V.tensor_tensor(UV[:, :, GW:], UV[:, :, GW:], pr("sgug")[:, None, :].to_broadcast([P, NT, GW]), ALU.mult))
                    V.tensor_tensor(UV[:, :, GW:], UV[:, :, GW:], pr("sgub")[:, None, :].to_broadcast([P, NT, GW]), ALU.add).then_inc(sgu_v, 1)
                    dve.wait_ge(lam_in, 2)
                    link(V.tensor_tensor(lamt[:, 2:3], lamt[:, 0:1], lamt[:, 1:2], ALU.subtract))
                    link(V.tensor_tensor(lamv, lamt[:, 2:3], pr("lam"), ALU.add))
                    dve.wait_ge(sgu_ps, 1)
                    for h in range(HEADS):
                        for t in range(2):
                            ps = PS[6 + t][:, :].rearrange("p (i n) -> p i n", i=2)[:, :, h * HD:(h + 1) * HD]
                            u = UV[:, 2 * t:2 * t + 2, h * HD:(h + 1) * HD]
                            link(V.scalar_tensor_tensor(u, ps, pc("sgub", h), u, ALU.add, ALU.mult))
                    dve.sem_inc(sgu_done, 1)

                    def rwkv(c, m, step):
                        s = mix[m]
                        mask = lambda n, up: CMs[:, (7 * up + n) * P:(7 * up + n + 1) * P][:, None, :].to_broadcast([P, 4, P])
                        if step == "P":
                            for u in range(8):
                                dve.wait_ge(s["prod_ps"], u + 1)
                                V.tensor_tensor(UB[:, u, :], PS[1 + u % 2][:, :], cst("unit"), ALU.mult).then_inc(s["prod_masked"], 1)
                            dve.wait_ge(s["eye"], 2)
                            for j in range(2):
                                dve.wait_ge(s["prod_ps"], 9 + j)
                                V.copy_predicated(DB[:, j::2, :], mask(0, 0), PS[3 + j][:, :].rearrange("p (u n) -> p u n", u=4)).then_inc(s["prod_masked"], 1)
                            dve.wait_ge(s["prod_masked"], 10)
                            for q in range(2):
                                V.copy_predicated(EB[:, 4 * q:4 * q + 4, :], mask(0, 1), UB[:, 4 * q:4 * q + 4, 0:P]).then_inc(s["eye"], 2)
                        elif step[0] == "L":
                            n = step[1]
                            for q in range(2):
                                for side in range(2):
                                    if n == 6 and side == 0:
                                        continue
                                    done = 4 * (n - 1) + 2 * q + side + 1 if n < 6 else 21 + q
                                    dve.wait_ge(s["de_ps"], done)
                                    dst = (DB, EB)[side][:, 4 * q:4 * q + 4, :]
                                    V.copy_predicated(dst, mask(n, side), PS[3 + side][:, :].rearrange("p (u n) -> p u n", u=4)).then_inc(s["de_merged"], 1)
                        elif step[0] == "C":
                            ch = step[1]
                            dve.wait_ge(s["sa_ps"], ch + 1)
                            V.tensor_copy(SA, PS[2][:, 0:P]).then_inc(s["sa_copied"], 1)
                            if ch < 3:
                                dve.wait_ge(s["s_ps"], ch + 1)
                                cc = carry[:, 4 * c + ch:4 * c + ch + 1]
                                dve.wait_ge(s["y_ps"], ch + 1)
                                t = PS[4][:, 0:P]
                                if ch:
                                    link(V.tensor_tensor(ST, t, ST, ALU.add))
                                    t = ST
                                V.scalar_tensor_tensor(ST, t, cc, cst("head"), ALU.mult, ALU.mult).then_inc(s["s_done"], 1)
                        elif step == "F":
                            y, r, k, v = Y[:, c, :], XS[:, 6 + c, :], XS[:, 1 + c, :], XS[:, 3 + c, :]
                            dve.wait_ge(s["y_ps"], 4)
                            link(V.tensor_tensor(UB[:, 1, :], r, k, ALU.mult))
                            V.tensor_scalar(UB[:, 1, :], UB[:, 1, :], pc("rk", c), None, ALU.mult).then_inc(s["fin_in"], 1)
                            dve.wait_ge(s["fin_ps"], 1)
                            V.scalar_tensor_tensor(y, PS[1][:, :], -1.0 / HD, y, ALU.mult, ALU.add).then_inc(s["fin_in"], 1)
                            dve.wait_ge(s["fin_ps"], 3)
                            rstd(UB[:, 3, :], PS[3][:, :], 1.0 / HD, RWKV_LN_EPS)
                            dve.wait_ge(s["fin_in"], 2)
                            link(V.tensor_tensor(y, y, UB[:, 3, :], ALU.mult))
                            link(V.tensor_scalar(y, y, pc("lng", c), pc("lnb", c), ALU.mult, ALU.add))
                            link(V.tensor_tensor(UB[:, 4, :], PS[2][:, :], v, ALU.mult))
                            link(V.tensor_tensor(y, y, UB[:, 4, :], ALU.add))
                            link(V.tensor_tensor(y, y, XS[:, (0, 5)[c], :], ALU.mult))
                            dve.sem_inc(s["y_done"], 1)

                    def attn(m, u):
                        s, nm = mix[m], 2 if m == "D" else 1
                        base = 0 if m == "A" else 16
                        if u < 16:
                            i, h = unit_of[u]
                            w = (i + 1) * P
                            for a in range(nm):
                                n = nm * u + a
                                dve.wait_ge(s["scores"], n + 1)
                                V.tensor_reduce(nmx[:, base + n:base + n + 1], PS[5 + n % 2][:, 0:w], AX.X, ALU.max, negate=True).then_inc(s["maxed"], 1)
                        if 1 <= u <= 16:
                            i, h = unit_of[u - 1]
                            w = (i + 1) * P
                            n = nm * (u - 1)
                            dve.wait_ge(s["exped"], n + nm)
                            link(V.reciprocal(rsum[:, base + n:base + n + nm], sums[:, base + n:base + n + nm]))
                            if m == "D":
                                r2 = rsum[:, base + n + 1:base + n + 2]
                                link(V.tensor_scalar(r2, r2, lamv, -1.0, ALU.mult, ALU.mult))
                                p0, p1 = PB[:, (u - 1) % 2, 0, 0:w], PB[:, (u - 1) % 2, 1, 0:w]
                                link(V.tensor_scalar(p1, p1, r2, None, ALU.mult))
                                V.scalar_tensor_tensor(p1, p0, rsum[:, base + n:base + n + 1], p1, ALU.mult, ALU.add).then_inc(s["probs"], 1)
                        if u >= 2:
                            n = u - 2
                            i, h = unit_of[n]
                            dve.wait_ge(s["o_ps"], n + 1)
                            o = QKV[m][:, i, h * HD:(h + 1) * HD]
                            if m == "A":
                                V.tensor_scalar(o, PS[0][:, 0:HD], rsum[:, n:n + 1], None, ALU.mult).then_inc(s["o_done"], 1)
                            else:
                                V.tensor_copy(o, PS[0][:, 0:HD]).then_inc(s["o_done"], 1)

                    for c, m in HALVES:
                        for kind, step in half_steps():
                            rwkv(c, m, step) if kind == "rwkv" else attn(m, step)

                    dve.wait_ge(mix["D"]["o_done"], 16)
                    o = QKV["D"][:, :, 0:GW].rearrange("p i (h n) -> p i h n", h=HEADS)
                    sq = UB[:, 0:2, :].rearrange("p u n -> p (u n)").rearrange("p (i h n) -> p i h n", i=NT, h=HEADS)
                    for i in range(NT):
                        link(V.tensor_tensor(sq[:, i], o[:, i], o[:, i], ALU.mult))
                    link(V.tensor_reduce(dss, UB[:, 0:2, :].rearrange("p u n -> p (u n)").rearrange("p (a n) -> p a n", n=HD), AX.X, ALU.add))
                    rstd(dss, dss, 1.0 / HD, SUBLN_EPS)
                    link(V.tensor_scalar(dss, dss, pr("oml"), None, ALU.mult))
                    d3 = dss.rearrange("p (i h) -> p i h", i=NT)
                    for i in range(NT):
                        link(V.tensor_tensor(o[:, i], o[:, i], d3[:, i, :, None].to_broadcast([P, HEADS, HD]), ALU.mult))
                    for i in range(NT):
                        link(V.tensor_tensor(o[:, i], o[:, i], pr("subln")[:, None, :].to_broadcast([P, HEADS, HD]), ALU.mult))
                    dve.sem_inc(mixed_done, 1)

                    for j in range(1, 6, 2):
                        dve.wait_ge(mt_ps, j + 1)
                        V.tensor_copy(MT[:, j, :], PS[j][:, :]).then_inc(mt_v, 1)
                    for g in range(8):
                        n, i = divmod(g, 4)
                        dve.wait_ge(res_ps, g + 1)
                        xv = X3[:, i, n * BN:(n + 1) * BN]
                        V.tensor_tensor(xv, PS[g][:, :], xv, ALU.add).then_inc(res_added, 1)
                    dve.wait_ge(n2_squares, 4)
                    rstd(rs2, ss2, 1.0 / D, RMS_EPS)
                    dve.wait_ge(g2row_in, 16)
                    for i in range(NT):
                        V.scalar_tensor_tensor(XN2[:, i, :], X3[:, i, :], rs2[:, i:i + 1], G2ROW, ALU.mult, ALU.mult).then_inc(n2_scaled, 1)
                    for k in range(1, KD, 2):
                        dve.wait_ge(n2_turned, k + 1)
                        V.tensor_copy(XNT[:, k, :], PS[k][:, :]).then_inc(n2_copied_v, 1)

                    dve.wait_ge(logits, 1)
                    rv = lambda lo, n: RW[:, lo:lo + n]
                    L = rv(0, NT * NR).rearrange("p (i n) -> p i n", i=NT)
                    link(V.tensor_tensor(L, PS[0][:, 0:NT * NR].rearrange("p (i n) -> p i n", i=NT),
                                         pr("rb")[:, None, :].to_broadcast([P, NT, NR]), ALU.add))

                    def first_max(vals, n, down, top, hot):
                        t3 = top[:, :, None]
                        wide = [P, NT, n]
                        link(V.tensor_reduce(top, vals, AX.X, ALU.max))
                        link(V.tensor_tensor(hot, vals, t3.to_broadcast(wide), ALU.is_equal))
                        link(V.tensor_tensor(hot, hot, down[:, None, :].to_broadcast(wide), ALU.mult))
                        link(V.tensor_reduce(rv(760, 4), hot, AX.X, ALU.max))
                        link(V.tensor_tensor(hot, hot, rv(760, 4)[:, :, None].to_broadcast(wide), ALU.is_equal))

                    gl = L[:, :, 0:GROUPS]
                    gtop, ghot = rv(144, 4), rv(148, 16).rearrange("p (i n) -> p i n", i=NT)
                    first_max(gl, GROUPS, cst("down4"), gtop, ghot)
                    gexp = rv(640, 16).rearrange("p (i n) -> p i n", i=NT)
                    V.tensor_tensor(gexp, gl, gtop[:, :, None].to_broadcast([P, NT, GROUPS]), ALU.subtract).then_inc(exp_in, 1)
                    pg = rv(164, 128).rearrange("p (i g e) -> p i g e", i=NT, g=GROUPS)
                    for i in range(NT):
                        link(V.tensor_tensor(pg[:, i], L[:, i, GROUPS:].rearrange("p (g e) -> p g e", g=GROUPS),
                                             ghot[:, i, :, None].to_broadcast([P, GROUPS, EPG]), ALU.mult))
                    el = rv(292, 32).rearrange("p (i e) -> p i e", i=NT)
                    link(V.tensor_reduce(el, rv(164, 128).rearrange("p (i g e) -> p i e g", i=NT, g=GROUPS), AX.X, ALU.add))
                    t1, h1 = rv(324, 4), rv(328, 32).rearrange("p (i e) -> p i e", i=NT)
                    first_max(el, EPG, cst("down8"), t1, h1)
                    link(V.scalar_tensor_tensor(el, h1, NEG, el, ALU.mult, ALU.add))
                    t2, h2 = rv(360, 4), rv(364, 32).rearrange("p (i e) -> p i e", i=NT)
                    first_max(el, EPG, cst("down8"), t2, h2)
                    V.tensor_tensor(rv(656, 4), t2, t1, ALU.subtract).then_inc(exp_in, 1)
                    dve.wait_ge(exp_done, 2)
                    link(V.tensor_reduce(rv(144, 4), gexp, AX.X, ALU.add))
                    link(V.scalar_tensor_tensor(rv(144, 4), rv(656, 4), 1.0, rv(144, 4), ALU.add, ALU.mult))
                    W2 = WT[:, :].rearrange("p (i j) -> p i j", j=2)
                    link(V.reciprocal(W2[:, :, 0], rv(144, 4)))
                    link(V.tensor_tensor(W2[:, :, 1], W2[:, :, 0], rv(656, 4), ALU.mult))
                    O1 = rv(396, 128).rearrange("p (i g e) -> p i g e", i=NT, g=GROUPS)
                    O2 = rv(164, 128).rearrange("p (i g e) -> p i g e", i=NT, g=GROUPS)
                    for i in range(NT):
                        gh = ghot[:, i, :, None].to_broadcast([P, GROUPS, EPG])
                        link(V.tensor_tensor(O1[:, i], gh, h1[:, i, None, :].to_broadcast([P, GROUPS, EPG]), ALU.mult))
                        link(V.tensor_tensor(O2[:, i], gh, h2[:, i, None, :].to_broadcast([P, GROUPS, EPG]), ALU.mult))
                    V.tensor_tensor(rv(0, 128), rv(396, 128), rv(164, 128), ALU.add).then_inc(chosen, 1)
                    dve.wait_ge(ranks, 1)
                    cnt, ov = PS[1][:, NT * NE:(NT + 1) * NE], rv(524, 32)
                    link(V.tensor_scalar(ov, cnt, CAP + 0.5, None, ALU.is_ge))
                    for b in range(2, -(-SEQ // CAP)):
                        link(V.scalar_tensor_tensor(ov, cnt, b * CAP + 0.5, ov, ALU.is_ge, ALU.add))
                    ends = rv(556, 32)
                    link(V.tensor_tensor_scan(ends, CFs[:, CF["ones"][0]:CF["ones"][0] + NE], ov, 0.0, ALU.mult, ALU.add))
                    hop = rv(588, 32)
                    link(V.tensor_tensor(hop, ends, ov, ALU.subtract))
                    link(V.scalar_tensor_tensor(hop, hop, float(CAP), cst("hop"), ALU.mult, ALU.add))
                    cmp = XSb[:, 0:NOV * NE].rearrange("p (b e) -> p b e", b=NOV)
                    link(V.tensor_tensor(cmp, ends[:, None, :].to_broadcast([P, NOV, NE]),
                                         cst("blocks")[:, :, None].to_broadcast([P, NOV, NE]), ALU.is_le))
                    link(V.tensor_reduce(rv(620, NOV), cmp, AX.X, ALU.add))
                    link(V.tensor_copy(OVI[:, 0:NOV], rv(620, NOV)))
                    link(V.tensor_copy(OVI[:, NOV:NOV + 1], ends[:, NE - 1:NE]))
                    rk = PS[1][:, 0:NT * NE].rearrange("p (i e) -> p i e", i=NT)
                    sl = rv(0, 128).rearrange("p (i e) -> p i e", i=NT)
                    wide = [P, NT, NE]
                    link(V.tensor_scalar(sl, rk, CAP - 0.5, None, ALU.is_ge))
                    link(V.tensor_tensor(sl, sl, hop[:, None, :].to_broadcast(wide), ALU.mult))
                    link(V.tensor_tensor(sl, sl, rk, ALU.add))
                    link(V.tensor_tensor(sl, sl, cst("slot0")[:, None, :].to_broadcast(wide), ALU.add))
                    for j, o in enumerate((rv(396, 128), rv(164, 128))):
                        link(V.tensor_tensor(o, o, rv(0, 128), ALU.mult))
                        link(V.tensor_reduce(rv(144 + 4 * j, 4), o.rearrange("p (i e) -> p i e", i=NT), AX.X, ALU.add))
                        link(V.tensor_copy(IDX[:, 4 * j:4 * j + 4], rv(144 + 4 * j, 4)))
                    dve.sem_inc(route_in, 1)
                    dve.sem_inc(routed, 1)

                    dve.sem_inc(hidden, 2)

                    def copy_rows(xt):
                        return V.tensor_copy(xt.rearrange("p (t k) s -> p t (k s)", t=2),
                                             PSALL[:, 0:2 * BN].rearrange("p (t n) -> p t n", t=2)[:, :, 0:4 * CAP])

                    dve.wait_ge(xt_ps, 1)
                    copy_rows(XT[0]).then_inc(xt_copied, 1)
                    with dve.Fori(0, NE // 2) as i:
                        for h in range(2):
                            e = 2 * i + h
                            dve.wait_ge(xt_ps, e + 2)
                            copy_rows(XT[1 - h]).then_inc(xt_copied, 1)
                            dve.wait_ge(up_ps, e + 1)
                            dve.wait_ge(gated, e + 1)
                            V.tensor_tensor(HT[h].rearrange("p k s -> p (k s)"), HS[h].rearrange("p k s -> p (k s)"),
                                            PS[4 + h][:, 0:KF * CAP], ALU.mult).then_inc(hidden, 1)
                    nov = dve.value_load(OVI[0:1, NOV:NOV + 1], min_val=0, max_val=NOV)
                    with dve.If(nov > 0):
                        with dve.Fori(0, nov) as j:
                            dve.wait_ge(ov_turn, j + 1)
                            copy_rows(XT[1]).then_inc(ov_turned, 1)
                            dve.wait_ge(ov_silu, j + 1)
                            V.tensor_tensor(HT[0].rearrange("p k s -> p (k s)"), HS[0].rearrange("p k s -> p (k s)"),
                                            PS[4][:, 0:KF * CAP], ALU.mult).then_inc(ov_hid, 1)
                    for n in range(8):
                        i, j = divmod(n, 2)
                        dve.wait_ge(gathered[n], 16 * (layer + 1))
                        ins = V.scalar_tensor_tensor(X3[:, i, :], YG[n], WT[:, n:n + 1], X3[:, i, :], ALU.mult, ALU.add)
                        ins.then_inc(combined, 1)
                        dve.wait_ge(combined, n + 1)

                @block.gpsimd
                def _(pool):
                    G = nc.gpsimd
                    done = [0]

                    def link(ins):
                        done[0] += 1
                        ins.then_inc(gp, 1)
                        pool.wait_ge(gp, done[0])

                    for m, b, heads, half in (("A", 0, 8, 8), ("D", 2, 16, 4)):
                        pool.wait_ge(proj_copied, copied("t", (b, NT - 1)))
                        t = QKV[m].rearrange("p i (g n) -> p i g n", g=heads)
                        a1, a2 = t[:, :, :, 0:half], t[:, :, :, half:2 * half]
                        shp = [P, NT, heads, half]
                        cos, sin = (cst(f + m).rearrange("p (i n) -> p i n", i=NT)[:, :, None, :].to_broadcast(shp) for f in ("cos", "sin"))
                        w = [view(RING, SC0 + 10112 + q * 256, 256, "p (i g n) -> p i g n", i=NT, g=heads) for q in range(4)]
                        G.tensor_tensor(w[0], a1, cos, ALU.mult)
                        G.tensor_tensor(w[1], a2, sin, ALU.mult)
                        G.tensor_tensor(w[2], a2, cos, ALU.mult)
                        link(G.tensor_tensor(w[3], a1, sin, ALU.mult))
                        G.tensor_tensor(a1, w[0], w[1], ALU.subtract).then_inc(roped[m], 1)
                        G.tensor_tensor(a2, w[2], w[3], ALU.add).then_inc(roped[m], 1)
                        pool.wait_ge(roped[m], 2)
                    eye = cst("ident")[:, None, :].to_broadcast([P, 8, P])
                    for buf in (DB, EB):
                        G.tensor_copy(buf, eye).then_inc(mix["A"]["eye"], 1)
                    pool.wait_ge(mix["A"]["y_ps"], 4)
                    for buf in (DB, EB):
                        G.tensor_copy(buf, eye).then_inc(mix["D"]["eye"], 1)
                    pool.wait_ge(routed, 1)
                    pool.wait_ge(n2_scaled, 4)
                    for n in range(8):
                        i, j = n // 2, n % 2
                        pool.indirect_dma_start(xslots[:, :], bass.IndirectOffsetOnAxis(ap=IDX[:, 4 * j + i:4 * j + i + 1], axis=0),
                                                XN2[:, i, :], None).then_inc(scattered, 16)
                    pool.wait_ge(scattered, 128 * (layer + 1))
                    pool.sem_inc(rows_sent, 1)
                    for h in range(2):
                        pool.wait_ge(y2_stored[h], 16 * (NE // 2 + 1))
                    pool.wait_ge(xt_copied, NE + 1)
                    pool.wait_ge(ov_end, 1)
                    for n in range(8):
                        i, j = divmod(n, 2)
                        pool.indirect_dma_start(YG[n], None, yslots[:, :],
                                                bass.IndirectOffsetOnAxis(ap=IDX[:, 4 * j + i:4 * j + i + 1], axis=0)).then_inc(gathered[n], 16)

            lo, hi = min(s.num for s in sems), max(s.num for s in sems)
            nc.all_engine_barrier(sems_to_clear=range(lo, hi + 1))

        of_layer.close()

        fin_in, fin_sq, fin_vec, fin_done, fin_out = (ctx.enter_context(nc.semaphore(n)) for n in
                                                      ("fin_g", "fin_squares", "fin_vec", "fin_done", "fin_out"))
        OUTB = view(TOK, 0, 4096, "p (i d) -> p i d", i=NT)
        with nc.Block() as block:
            @block.sync
            def _(sp):
                sp.dma_start(G2ROW, final_g.rearrange("(a n) -> a n", a=1).to_broadcast([P, D])).then_inc(fin_in, 16)
                for i in range(NT):
                    sp.wait_ge(fin_done, i + 1)
                    sp.dma_start(out[0, i * P:(i + 1) * P, :], OUTB[:, i, :]).then_inc(fin_out, 16)
                sp.wait_ge(fin_out, 16 * NT)

            @block.scalar
            def _(act):
                for i in range(NT):
                    nc.scalar.activation(XNTb[:, i * D:(i + 1) * D], X3[:, i, :], ACT.Square, accum_out=ss1[:, i:i + 1]).then_inc(fin_sq, 1)
                act.wait_ge(fin_vec, 1)
                nc.scalar.activation(rs1, rs1, ACT.Sqrt).then_inc(fin_sq, 1)

            @block.vector
            def _(dve):
                dve.wait_ge(fin_sq, NT)
                nc.vector.tensor_scalar(rs1, ss1, 1.0 / D, RMS_EPS, ALU.mult, ALU.add).then_inc(fin_vec, 1)
                dve.wait_ge(fin_sq, NT + 1)
                nc.vector.reciprocal(rs1, rs1).then_inc(fin_vec, 1)
                dve.wait_ge(fin_vec, 2)
                dve.wait_ge(fin_in, 16)
                for i in range(NT):
                    nc.vector.scalar_tensor_tensor(OUTB[:, i, :], X3[:, i, :], rs1[:, i:i + 1], G2ROW, ALU.mult, ALU.mult).then_inc(fin_done, 1)


def constants():
    t = np.arange(P)
    cf = np.zeros((P, NCF), np.float32)

    def put(name, a):
        lo, n = CF[name]
        cf[:, lo:lo + n] = a

    before, upto = t[:, None] < t[None, :], t[:, None] <= t[None, :]
    put("ident", np.eye(P))
    put("causal", np.where(t[None, :] <= t[:, None], 0.0, NEG))
    put("unit", np.concatenate([before, upto, before, upto], 1))
    put("head", t[:, None] // HD == t[None, :] // HD)
    put("ones", 1.0)
    for m, rot in (("A", HD // 4), ("D", HD // 8)):
        inv = (np.float32(500000.0) ** (-np.arange(0, rot, 2, dtype=np.float32) / np.float32(rot))).astype(np.float32)
        ang = (np.arange(SEQ, dtype=np.float32)[:, None] * inv[None, :]).astype(np.float32).astype(np.float64)
        for f, fn in (("cos", np.cos), ("sin", np.sin)):
            put(f + m, fn(ang).reshape(NT, P, rot // 2).transpose(1, 0, 2).reshape(P, -1))
    put("down4", np.arange(GROUPS, 0, -1))
    put("down8", np.arange(EPG, 0, -1))
    put("slot0", np.arange(NE) * CAP)
    put("hop", (NE - 1 - np.arange(NE)) * CAP)
    put("blocks", np.arange(NOV))
    cm = np.zeros((P, 14 * P), np.float32)
    for n, b in enumerate(LEVELS):
        i, j = t[:, None], t[None, :]
        low = (i // (2 * b) == j // (2 * b)) & ((i // b) % 2 == 1) & ((j // b) % 2 == 0)
        cm[:, n * P:(n + 1) * P] = low
        cm[:, (7 + n) * P:(8 + n) * P] = low.T
    return cf, cm


def kernel(x, norm1_g, w_in, rwkv_mu, rwkv_w0, rwkv_w2, rwkv_a0, rwkv_a2, rwkv_g2, rwkv_kk, rwkv_ka, rwkv_rk,
           rwkv_ln_g, rwkv_ln_b, sgu_ln_g, sgu_ln_b, sgu_w, sgu_b, diff_lq1, diff_lk1, diff_lq2, diff_lk2,
           diff_subln_g, w_out, norm2_g, router_group_w, router_group_b, router_expert_w, router_expert_b,
           moe_w_gate, moe_w_up, moe_w_down, final_g):
    import concourse.bacc as bacc
    from concourse.bass_utils import run_bass_kernel_spmd

    L = DEPTH
    b0 = 3 * GW
    wd0, k0 = b0 + 256, b0 + 320
    v0, ad0, gd0 = k0 + 256, k0 + 512, k0 + 576
    c0, d0 = b0 + 1024, b0 + 1536
    rng = lambda a, n: list(range(a, a + n))
    tiles = [rng(wd0, 64) + rng(ad0, 64), rng(k0, 128), rng(k0 + 128, 128), rng(v0, 128),
             rng(v0 + 128, 128), rng(gd0, 128), rng(b0, 128), rng(b0 + 128, 128)]
    blocks = [sum(tiles[:4], []), sum(tiles[4:], []), rng(0, 512), rng(512, 256) + rng(d0 + 512, 256),
              rng(d0, 512), rng(c0, 512)]

    def slots(w, cols):
        parts = [np.asarray(w)[:, :, c].reshape(L, KD, P, len(c)).transpose(0, 2, 1, 3).reshape(L, P, -1) for c in cols]
        return np.ascontiguousarray(np.stack(parts, 1))

    def per_channel(a, n):
        return np.asarray(a).reshape(L, n, P).transpose(0, 2, 1)

    mu = np.asarray(rwkv_mu)[:, np.array(sum(tiles, [])) - b0]
    pcol = np.concatenate([per_channel(norm1_g, KD), per_channel(mu, 8)]
                          + [per_channel(a, 2) for a in (rwkv_w0, rwkv_a0, rwkv_kk, rwkv_ka, rwkv_rk, rwkv_ln_g, rwkv_ln_b)]
                          + [np.asarray(sgu_b).transpose(0, 2, 1)], 2)
    lam = np.array([0.8 - 0.6 * math.exp(-0.3 * l) for l in range(L)])
    prow = np.concatenate([np.asarray(a) for a in (sgu_ln_g, sgu_ln_b, diff_subln_g, diff_lq1, diff_lk1, diff_lq2, diff_lk2)]
                          + [np.stack([lam, 1 - lam], 1).astype(np.float32), np.asarray(router_group_b), np.asarray(router_expert_b)], 1)
    router = np.concatenate([np.asarray(router_group_w), np.asarray(router_expert_w)], 2)
    cf, cm = constants()
    arrays = {
        "x": np.asarray(x), "w_in_blocks": slots(w_in, blocks), "w_out_blocks": slots(w_out, [rng(0, 512), rng(512, 512)]),
        "channel_params": pcol, "row_params": prow,
        "w2_a2": np.concatenate([np.asarray(rwkv_w2), np.asarray(rwkv_a2)], 1), "g2": np.asarray(rwkv_g2),
        "sgu_w_turned": np.asarray(sgu_w).transpose(0, 3, 1, 2),
        "router": router.reshape(L, KD, P, NR).transpose(0, 2, 1, 3).reshape(L, P, KD * NR),
        "norm2_g": np.asarray(norm2_g), "w_gate": np.asarray(moe_w_gate), "w_up": np.asarray(moe_w_up),
        "w_down": np.asarray(moe_w_down), "final_g": np.asarray(final_g), "cf": cf, "cm": cm,
    }
    arrays = {k: np.ascontiguousarray(v) for k, v in arrays.items()}
    nc = bacc.Bacc("TRN2", target_bir_lowering=False, num_devices=1)
    args = [nc.dram_tensor(f"in_{k}", a.shape, mybir.dt.from_np(a.dtype), kind="ExternalInput").ap() for k, a in arrays.items()]
    out = nc.dram_tensor("out_dram", (1, SEQ, D), F32, kind="ExternalOutput").ap()
    build(nc, *args, out)
    r = run_bass_kernel_spmd(nc, [{f"in_{k}": a for k, a in arrays.items()}], core_ids=[0])
    return r.results[0]["out_dram"]
```

```python
import math
from contextlib import ExitStack

import concourse.bass as bass
from concourse import mybir
import numpy as np

F32 = mybir.dt.float32
I32 = mybir.dt.int32
U8 = mybir.dt.uint8
ALU = mybir.AluOpType
ACT = mybir.ActivationFunctionType
AX = mybir.AxisListType

P = 128
SEQ, D, DEPTH = 512, 1024, 2
NT = SEQ // P
KD = D // P
HEADS, HD, GW = 4, 64, 256
NE, GROUPS, EPG, FF = 32, 4, 8, 512
KF = FF // P
CAP = 80
NOV = (2 * SEQ - NE) // CAP
ROWS = (NE + NOV) * CAP
ZB_N = 4
ZEROING = -(-(NE + NOV) // ZB_N) + -(-NOV // ZB_N)
NR = GROUPS + NE
BN = 512
NEG = -1.0e30
RMS_EPS, SUBLN_EPS, LN_EPS, RWKV_LN_EPS = 1e-6, 1e-5, 1e-5, 64e-5
LOG_DECAY = -math.exp(-0.5)
LEVELS = [1, 2, 4, 8, 16, 32, 64]


def layout(fields):
    at, out = 0, {}
    for name, n in fields:
        out[name] = (at, n)
        at += n
    return out, at


CF, NCF = layout([("ident", P), ("causal", P), ("unit", 4 * P), ("head", P), ("ones", P),
                  ("cosA", NT * 8), ("sinA", NT * 8), ("cosD", NT * 4), ("sinD", NT * 4),
                  ("down4", GROUPS), ("down8", EPG), ("slot0", NE), ("hop", NE), ("blocks", NOV)])
PC, NPC = layout([("g1", KD), ("mu", 8), ("w0", 2), ("a0", 2), ("kk", 2), ("ka", 2), ("rk", 2),
                  ("lng", 2), ("lnb", 2), ("sgub", HEADS)])
PR, NPR = layout([("sgug", GW), ("sgub", GW), ("subln", HD), ("lq1", 32), ("lk1", 32), ("lq2", 32),
                  ("lk2", 32), ("lam", 1), ("oml", 1), ("rb", NR)])


def build(nc, x, w_in, w_out, pcol, prow, w2a2, g2, sguT, router, norm2_g, w_gate, w_up, w_down,
          final_g, cf, cm, out):
    ctx, of_layer = ExitStack(), ExitStack()
    with ctx:
        def sb(name, n, dt=F32):
            return ctx.enter_context(nc.sbuf_tensor(name, [P, n], dt))

        def view(t, lo, n, pat=None, **kw):
            v = t[:, lo:lo + n]
            return v.rearrange(pat, **kw) if pat else v

        sems = []

        def sem(name):
            sems.append(of_layer.enter_context(nc.semaphore(name)))
            return sems[-1]

        X = sb("X", NT * D)
        XNTb = sb("XNT", KD * SEQ)
        RING = sb("RING", 6 * 4096)
        TOK = sb("TOK", 4 * 2048)
        XSb = sb("XS", 8 * SEQ)
        SC = sb("SCAN", 4096)
        CFs = sb("CF", NCF)
        CMs = sb("CM", 14 * P, U8)
        PCs = sb("PCOL", NPC)
        PRs = sb("PROW", NPR)
        OMU = sb("OMU", 8)
        OKA = sb("OKA", 2)
        RT = sb("ROUTER", KD * NR)
        SM = sb("SMALL", 300)
        IDX = sb("IDX", 8, I32)
        WT = sb("WT", 8)
        OVI = sb("OVI", NOV + 1, I32)
        PSALL = ctx.enter_context(nc.psum_tensor("banks", [P, 8 * BN], F32))
        PS = [PSALL[:, i * BN:(i + 1) * BN] for i in range(8)]

        def half_banks(b):
            return PSALL[:, b * BN:(b + 2) * BN].rearrange("p (t n) -> p t n", t=2)[:, :, 0:4 * CAP]

        def cst(name):
            lo, n = CF[name]
            return CFs[:, lo:lo + n]

        def pc(name, i):
            return PCs[:, PC[name][0] + i:PC[name][0] + i + 1]

        def pr(name):
            lo, n = PR[name]
            return PRs[:, lo:lo + n]

        X3 = X[:, :].rearrange("p (i d) -> p i d", i=NT)
        XNT = XNTb[:, :].rearrange("p (k t) -> p k t", k=KD)
        QKT = view(XNTb, 0, 2048, "p (j t) -> p j t", j=4)
        PB = view(XNTb, 2048, 2048, "p (b m t) -> p b m t", b=2, m=2)
        MT = view(XNTb, 0, 3072, "p (j t) -> p j t", j=6)
        SLOT = [RING[:, s * 4096:(s + 1) * 4096] for s in range(6)]
        SC0 = 3 * 4096
        XN = view(RING, SC0, 4096, "p (i d) -> p i d", i=NT)
        WORK = [view(RING, SC0 + 516 * i, 516) for i in range(7)]
        UB = view(RING, SC0, 4096, "p (u n) -> p u n", u=8)
        DB = view(RING, SC0 + 4096, 1024, "p (u n) -> p u n", u=8)
        EB = view(RING, SC0 + 5120, 1024, "p (u n) -> p u n", u=8)
        MB = view(RING, SC0 + 6144, 1024, "p (u n) -> p u n", u=8)
        TT = view(RING, SC0 + 7168, 1536, "p (w m n) -> p w m n", w=3, m=4)
        ZB = view(RING, SC0 + 8704, 128)
        SA = view(RING, SC0 + 8832, 128)
        ST = view(RING, SC0 + 8960, 128)
        PT = view(RING, SC0 + 9088, 1024, "p (b t) -> p b t", b=2)
        Y = view(RING, SC0 + 10112, 1024, "p (c t) -> p c t", c=2)
        W2A2 = view(RING, SC0 + 11136, 256)
        G2 = view(RING, SC0 + 11392, 256)
        SGT = view(RING, SC0 + 11648, 512, "p (h t) -> p h t", h=HEADS)
        TK = [view(TOK, b * 2048, 2048, "p (i n) -> p i n", i=NT) for b in range(4)]
        QKV = {"A": TK[0], "D": TK[2]}
        BLOCK_TO = [TK[0], TK[1], TK[3], TK[2]]
        VAD, UV = TK[1], TK[3]
        XS = XSb[:, :].rearrange("p (g t) -> p g t", g=8)
        AR = view(SC, 0, 2048, "p (c m w t) -> p c m w t", c=2, m=4, w=2)
        BT = view(SC, 2048, 1024, "p (c t) -> p c t", c=2)
        KT = view(SC, 3072, 1024, "p (c t) -> p c t", c=2)
        G2ROW = view(SC, 0, D)
        XN2 = view(TOK, 0, 4096, "p (i d) -> p i d", i=NT)
        XR = [view(TOK, 4096 + b * 1024, 1024) for b in range(2)]
        XT = view(TOK, 6144, KD * CAP, "p (k s) -> p k s", k=KD)
        HS, HT = view(XSb, 0, KF * CAP), view(XSb, KF * CAP, KF * CAP)
        YT = view(XSb, 2 * KF * CAP, KD * CAP)
        YS = [view(XSb, 1280 + b * 1024, 1024) for b in range(2)]
        YG = [view(TOK, n * 1024, 1024) for n in range(8)]
        RW = view(XSb, 3328, 768)
        small_at = [0]

        def small(n):
            lo = small_at[0]
            small_at[0] += n
            assert small_at[0] <= 300
            return SM[:, lo:lo + n]

        ss1, rs1, ss2, rs2 = small(4), small(4), small(4), small(4)
        epend, enbeg, carry = small(8), small(8), small(8)
        nmx, sums, rsum = small(48), small(48), small(48)
        lamt, lamv = small(4), small(1)
        bnv, bns, srs = small(8), small(24), small(4)
        dss = small(16)
        xslots = nc.dram_tensor("x_slots", (ROWS, D), F32).ap()
        yslots = nc.dram_tensor("y_slots", (ROWS, D), F32).ap()
        xs_e = xslots.rearrange("(e s) d -> e s d", s=CAP)
        ys_e = yslots.rearrange("(e s) d -> e s d", s=CAP)
        wg_v = w_gate.rearrange("l e (p k) f -> (l e) p (k f)", p=P)
        wu_v = w_up.rearrange("l e (p k) f -> (l e) p (k f)", p=P)
        wd_v = w_down.rearrange("l e (k p) d -> (l e) p k d", p=P)

        const_in = ctx.enter_context(nc.semaphore("const_in"))
        slots_zeroed = ctx.enter_context(nc.semaphore("slots_zeroed"))
        zero_tile = ctx.enter_context(nc.semaphore("zero_tile"))
        masks_made = ctx.enter_context(nc.semaphore("masks_made"))

        scattered = ctx.enter_context(nc.semaphore("scattered"))
        gathered = [ctx.enter_context(nc.semaphore(f"gathered{n}")) for n in range(8)]

        with nc.Block() as block:
            @block.sync
            def _(sp):
                sp.dma_start(X3, x.rearrange("b (i p) d -> p (b i) d", p=P)).then_inc(const_in, 16)
                sp.dma_start(CFs[:, :], cf).then_inc(const_in, 16)
                sp.dma_start(SLOT[5][:, 0:14 * P], cm).then_inc(const_in, 16)
                sp.wait_ge(const_in, 48)

            @block.vector
            def _(dve):
                dve.wait_ge(const_in, 48)
                nc.vector.tensor_copy(CMs[:, :], SLOT[5][:, 0:14 * P]).then_inc(masks_made, 1)

            @block.gpsimd
            def _(pool):
                nc.gpsimd.memset(XR[0], 0.0).then_inc(zero_tile, 1)

        params_in = sem("params_in")
        g2row_in = sem("g2row_in")
        slot_full = [sem(f"slot_full{s}") for s in range(6)]
        prep_done = sem("prep_done")
        n1_squares, n1_scaled = sem("n1_squares"), sem("n1_scaled")
        n1_turned = sem("n1_turned")
        n1_copied_a, n1_copied_v = sem("n1_copied_a"), sem("n1_copied_v")
        proj_ps, xs_scaled, xs_mixed, proj_copied = sem("proj_ps"), sem("xs_scaled"), sem("xs_mixed"), sem("proj_copied")
        lora_in = sem("lora_in")
        vec, gp, root_in, root_out = sem("vec"), sem("gp"), sem("root_in"), sem("root_out")
        cs_ready, exps_ready, scan_in, kk_sq = sem("cs_ready"), sem("exps_ready"), sem("scan_in"), sem("kk_sq")
        gelu_done, sgu_v, sgu_ps, sgu_w = sem("gelu_done"), sem("sgu_v"), sem("sgu_ps"), sem("sgu_w")
        roped = {m: sem(f"roped{m}") for m in "AD"}
        mix = {}
        for m in "AD":
            mix[m] = {n: sem(f"{n}{m}") for n in (
                "qk_ps", "qk_copied", "scores", "maxed", "exped", "probs", "pt_ps", "pt_copied", "o_ps", "o_done",
                "eye", "prod_ps", "prod_masked", "turn_ps", "turned", "m1_ps", "m1_copied",
                "de_ps", "de_merged", "z_ps", "z_copied", "sa_ps", "sa_copied", "y_ps", "y_copied", "s_ps", "s_done",
                "fin_in", "fin_ps", "fin_sq", "y_done") if (n, m) != ("probs", "A")}
        mixed_done, mt_ps, mt_a, mt_v = sem("mixed_done"), sem("mt_ps"), sem("mt_a"), sem("mt_v")
        res_ps, res_added = sem("res_ps"), sem("res_added")
        n2_squares, n2_scaled, n2_turned, n2_copied_a, n2_copied_v = (
            sem("n2_squares"), sem("n2_scaled"), sem("n2_turned"), sem("n2_copied_a"), sem("n2_copied_v"))
        logits, exp_in, exp_done, chosen, ranks, routed = sem("logits"), sem("exp_in"), sem("exp_done"), sem("chosen"), sem("ranks"), sem("routed")
        route_in = sem("route_in")
        xt_ps, xt_copied = sem("xt_ps"), sem("xt_copied")
        gate_ps, up_ps, gated, hidden = sem("gate_ps"), sem("up_ps"), sem("gated"), sem("hidden")
        pe_passed, sp_passed = sem("pe_passed"), sem("sp_passed")
        yt_copied, rows_ps = sem("yt_copied"), sem("rows_ps")
        y2_ps, y2_copied, y2_stored = sem("y2_ps"), sem("y2_copied"), [sem("y2_stored0"), sem("y2_stored1")]
        ov_in, ov_turn, ov_turned, ov_gu, ov_silu, ov_hid, ov_y, ov_yt, ov_rows, ov_out, ov_st, ov_end = (
            sem(f"ov_{n}") for n in ("in", "turn", "turned", "gu", "silu", "hid", "y", "yt", "rows", "out", "st", "end"))
        combined = sem("combined")
        rows_full, rows_sent = [sem("rows_full0"), sem("rows_full1")], sem("rows_sent")
        lam_in, sgu_done = sem("lam_in"), sem("sgu_done")

        PROJ = ([("b", g) for g in range(8)] + [("t", (0, 0))] + [("l", n) for n in range(6)]
                + [("n", c) for c in range(2)] + [("t", (0, i)) for i in range(1, NT)]
                + [("t", (b, i)) for b in range(1, 4) for i in range(NT)])
        LATE = len(PROJ) - 2 * NT
        bank_of = [g % 8 if g < LATE else (0, 5)[g % 2] for g in range(len(PROJ))]

        def mixer_steps():
            tri = [(0, "A", st) for st in ["P", "T"] + [("L", n) for n in range(1, 7)]]
            for n in range(8):
                yield "proj", (LATE + n,)
                yield "rwkv", tri[n]
                if n == 3:
                    yield "sgu_in", ()
                if n == 5:
                    yield "sgu_out", ()
            rest = ([(0, "A", ("C", ch)) for ch in range(4)] + [(0, "A", "F"), (1, "D", "P"), (1, "D", "T")]
                    + [(1, "D", ("L", n)) for n in range(1, 7)] + [(1, "D", ("C", ch)) for ch in range(4)] + [(1, "D", "F")])
            units = [(m, u) for m in "AD" for u in range(18)]
            for n, step in enumerate(rest):
                yield "rwkv", step
                for mu in units[2 * n:2 * n + 2]:
                    yield "attn", mu

        def run_mixers(**do):
            for kind, args in mixer_steps():
                if kind in do:
                    do[kind](*args)

        def copied(*group):
            return PROJ.index(group) - 7

        BLOCK_USED = [4, 8] + [PROJ.index(("t", (b, NT - 1))) + 1 for b in range(4)]
        MT_OF = {0: 0, 1: 1, 4: 2, 5: 3, 6: 4, 7: 5}
        unit_of = [(i, h) for i in range(NT) for h in range(HEADS)]

        with nc.Fori(0, DEPTH) as layer:
            with nc.Block() as block:

                @block.sync
                def _(sp):
                    one = bass.ds(layer, 1)
                    for dst, src in ((PCs[:, :], pcol[one].rearrange("a p n -> p (a n)")),
                                     (PRs[:, :], prow[one, :].to_broadcast([P, NPR])),
                                     (W2A2, w2a2[one].rearrange("a p n -> p (a n)")),
                                     (G2, g2[one].rearrange("a p n -> p (a n)")),
                                     (SGT, sguT[one].rearrange("a p h t -> p (a h) t")),
                                     (RT[:, :], router[one].rearrange("a p n -> p (a n)"))):
                        sp.dma_start(dst, src).then_inc(params_in, 16)
                    for n in range(6):
                        if n >= 3:
                            sp.wait_ge(proj_ps, BLOCK_USED[n - 3])
                        sp.dma_start(SLOT[n % 3], w_in[one, n].rearrange("a p n -> p (a n)")).then_inc(slot_full[n % 3], 16)
                    for n in range(2):
                        sp.wait_ge(proj_ps, BLOCK_USED[n + 3])
                        sp.dma_start(SLOT[n], w_out[one, n].rearrange("a p n -> p (a n)")).then_inc(slot_full[n], 16)

                    def load(e, h, waits):
                        for m, v in enumerate((wg_v, wu_v, wd_v)):
                            s = (2 + 3 * h + m) % 6
                            sp.wait_ge(*waits[m])
                            src = v[bass.ds(layer * NE + e, 1)]
                            if m < 2:
                                sp.dma_start(SLOT[s], src.rearrange("a p n -> p (a n)")).then_inc(slot_full[s], 16)
                            else:
                                sp.dma_start(SLOT[s].rearrange("p (k d) -> p k d", k=KF),
                                             src.rearrange("a p k d -> p (a k) d")).then_inc(slot_full[s], 16)

                    load(0, 0, [(proj_ps, BLOCK_USED[5]), (mixed_done, 1), (mixed_done, 1)])
                    sp.dma_start(G2ROW, norm2_g[one, :].to_broadcast([P, D])).then_inc(g2row_in, 16)
                    load(1, 1, [(res_ps, 8), (res_ps, 8), (res_ps, 8)])
                    def load_rows(e, h):
                        sp.dma_start(XR[h][0:CAP, :], xs_e[bass.ds(e, 1)].rearrange("a s d -> s (a d)")).then_inc(rows_full[h], 16)

                    sp.wait_ge(rows_sent, 1)
                    load_rows(0, 0)
                    load_rows(1, 1)
                    with sp.Fori(1, NE // 2) as i:
                        for h in range(2):
                            e = 2 * i + h
                            sp.wait_ge(xt_ps, e - 1)
                            load_rows(e, h)
                            load(e, h, [(gate_ps, e - 1), (up_ps, e - 1), (y2_ps, e - 1)])
                    sp.wait_ge(xt_ps, NE - 1)
                    load_rows(NE, 0)
                    sp.wait_ge(routed, 1)
                    nov = sp.value_load(OVI[0:1, NOV:NOV + 1], min_val=0, max_val=NOV)
                    sp.wait_ge(y2_ps, NE - 1)
                    with sp.If(nov > 0):
                        with sp.Fori(0, nov) as j:
                            e = sp.value_load(OVI[0:1, bass.ds(j, 1)], min_val=0, max_val=NE - 1)
                            w = layer * NE + e
                            sp.dma_start(SLOT[2], wg_v[bass.ds(w, 1)].rearrange("a p n -> p (a n)")).then_inc(ov_in, 16)
                            sp.dma_start(SLOT[3], wu_v[bass.ds(w, 1)].rearrange("a p n -> p (a n)")).then_inc(ov_in, 16)
                            sp.dma_start(SLOT[4].rearrange("p (k d) -> p k d", k=KF),
                                         wd_v[bass.ds(w, 1)].rearrange("a p k d -> p (a k) d")).then_inc(ov_in, 16)
                            sp.dma_start(XR[1][0:CAP, :], xs_e[bass.ds(j + NE, 1)].rearrange("a s d -> s (a d)")).then_inc(ov_in, 16)
                            sp.wait_ge(ov_out, j + 1)
                            sp.dma_start(ys_e[bass.ds(j + NE, 1)].rearrange("a s d -> s (a d)"), YS[0][0:CAP, :]).then_inc(ov_st, 16)
                            sp.wait_ge(ov_st, 16 * (j + 1))
                            sp.sem_inc(sp_passed, 1)
                    sp.sem_inc(ov_end, 1)

                @block.tensor
                def _(pe):
                    mm, tr = nc.tensor.matmul, nc.tensor.transpose
                    ident = cst("ident")

                    for k in range(KD):
                        for i in range(NT):
                            if k == 0:
                                pe.wait_ge(n1_scaled, i + 1)
                            last = tr(PS[k][:, i * P:(i + 1) * P], XN[:, i, k * P:(k + 1) * P], ident)
                        last.then_inc(n1_turned, 1)

                    pe.wait_ge(n1_copied_a, 4)
                    pe.wait_ge(n1_copied_v, 4)
                    def project(g):
                        kind, a = PROJ[g]
                        bank = PS[bank_of[g]]
                        before = [q for q in range(g) if bank_of[q] == bank_of[g]]
                        if before:
                            if before[-1] < 8:
                                pe.wait_ge(xs_mixed, before[-1] + 1)
                            else:
                                pe.wait_ge(proj_copied, before[-1] - 7)
                        if kind == "b":
                            n, j = g // 4, g % 4
                            if j == 0:
                                pe.wait_ge(slot_full[n], 16)
                            w = SLOT[n].rearrange("p (k n) -> p k n", k=KD)
                            for k in range(KD):
                                last = mm(bank[:, :], w[:, k, j * P:(j + 1) * P], XNT[:, k, :], start=(k == 0), stop=(k == KD - 1))
                            last.then_inc(proj_ps, 1)
                        elif kind == "t":
                            b, i = a
                            n = b + 2
                            if i == 0:
                                pe.wait_ge(slot_full[n % 3], 16 * (n // 3 + 1))
                            w = SLOT[n % 3].rearrange("p (k n) -> p k n", k=KD)
                            for k in range(KD):
                                last = mm(bank[:, :], XNT[:, k, i * P:(i + 1) * P], w[:, k, :], start=(k == 0), stop=(k == KD - 1))
                            last.then_inc(proj_ps, 1)
                        elif kind == "n":
                            pe.wait_ge(kk_sq, a + 1)
                            mm(bank[:, :], cst("head"), WORK[5 + a][:, 0:SEQ], start=True, stop=True).then_inc(proj_ps, 1)
                        else:
                            w, c = divmod(a, 2)
                            cols = slice(c * P, (c + 1) * P)
                            if a == 0:
                                pe.wait_ge(params_in, 96)
                                pe.wait_ge(lora_in, 1)
                                pe.wait_ge(xs_mixed, 8)
                            if w == 0:
                                last = mm(bank[:, :], W2A2[0:64, cols], XS[0:64, 0, :], start=True, stop=True)
                            elif w == 1:
                                last = mm(bank[:, :], W2A2[64:128, cols], XS[64:128, 0, :], start=True, stop=True)
                            else:
                                pe.wait_ge(lora_in, 2)
                                last = mm(bank[:, :], G2[:, cols], XS[:, 5, :], start=True, stop=True)
                            last.then_inc(proj_ps, 1)

                    for g in range(LATE):
                        project(g)

                    def mix_positions():
                        pe.wait_ge(sgu_v, 1)
                        pe.wait_ge(sgu_w, 1)
                        for i in range(NT):
                            for h in range(HEADS):
                                last = mm(PS[6 + i // 2][:, (i % 2) * GW + h * HD:(i % 2) * GW + (h + 1) * HD],
                                          SGT[:, h, :], UV[:, i, GW + h * HD:GW + (h + 1) * HD], start=True, stop=True)
                        last.then_inc(sgu_ps, 1)

                    def rwkv(c, m, step):
                        s = mix[m]
                        head = lambda t, j: t[j * HD:(j + 1) * HD]
                        if step == "P":
                            pe.wait_ge(scan_in, c + 1)
                            if c == 0:
                                pe.wait_ge(proj_copied, LATE - 8)
                            if c:
                                pe.wait_ge(mix["A"]["y_done"], 1)
                            for u in range(8):
                                ch, j = divmod(u, 2)
                                if u >= 2:
                                    pe.wait_ge(s["prod_masked"], u - 1)
                                bank, t = PS[1 + u % 2], slice(ch * P, (ch + 1) * P)
                                ar = head(AR[:, c, ch, :, :], j).rearrange("p w t -> p (w t)")
                                mm(bank[:, 0:256], head(BT[:, c, t], j), ar, start=True, stop=True)
                                mm(bank[:, 256:512], head(KT[:, c, t], j), ar, start=True, stop=True).then_inc(s["prod_ps"], 1)
                            for j in range(2):
                                for ch in range(4):
                                    last = mm(PS[3 + j][:, ch * P:(ch + 1) * P], head(AR[:, c, ch, 0, :], j),
                                              head(BT[:, c, ch * P:(ch + 1) * P], j), start=True, stop=True)
                                last.then_inc(s["prod_ps"], 1)
                        elif step == "T":
                            pe.wait_ge(s["prod_masked"], 10)
                            for w, src in enumerate((BT[:, c, :], KT[:, c, :], XS[:, 3 + c, :])):
                                for ch in range(4):
                                    last = tr(PS[1 + w][:, ch * P:(ch + 1) * P], src[:, ch * P:(ch + 1) * P], ident)
                                last.then_inc(s["turn_ps"], 1)
                        elif step[0] == "L":
                            n = step[1]
                            for q in range(2):
                                if n == 1:
                                    pe.wait_ge(s["turned"], 3)
                                    pe.wait_ge(s["eye"], 6)
                                else:
                                    pe.wait_ge(s["de_merged"], 4 * (n - 2) + 2 * q + 2)
                                for w in range(4):
                                    u = 4 * q + w
                                    last = mm(PS[1 + q][:, w * P:(w + 1) * P], UB[:, u, 0:P], DB[:, u, :], start=True, stop=True)
                                last.then_inc(s["m1_ps"], 1)
                            for q in range(2):
                                pe.wait_ge(s["m1_copied"], 2 * (n - 1) + q + 1)
                                for side in range(2):
                                    if n == 6 and side == 0:
                                        continue
                                    if n == 6:
                                        pe.wait_ge(s["de_merged"], 20 + q)
                                    elif n > 1 or q > 0:
                                        pe.wait_ge(s["de_merged"], 4 * (n - 1) + 2 * q + side - 1)
                                    for w in range(4):
                                        u = 4 * q + w
                                        if side == 0:
                                            last = mm(PS[3][:, w * P:(w + 1) * P], EB[:, u, :], MB[:, u, :], start=True, stop=True)
                                        else:
                                            last = mm(PS[4][:, w * P:(w + 1) * P], MB[:, u, :], EB[:, u, :], start=True, stop=True)
                                    last.then_inc(s["de_ps"], 1)
                        elif step[0] == "C":
                            ch = step[1]
                            if ch == 0:
                                pe.wait_ge(s["de_merged"], 22)
                            else:
                                pe.wait_ge(s["s_done"], ch)
                            v = lambda j: TT[:, 2, ch, j * HD:(j + 1) * HD]
                            hc = lambda j: slice(j * HD, (j + 1) * HD)
                            for j in range(2):
                                last = mm(PS[1][:, hc(j)], UB[:, 2 * ch + j, 256:384], v(j), start=(j == 0), stop=(ch == 0 and j == 1))
                            if ch:
                                last = mm(PS[1][:, 0:P], AR[:, c, ch, 0, :], ST, start=False, stop=True)
                            last.then_inc(s["z_ps"], 1)
                            pe.wait_ge(s["z_copied"], ch + 1)
                            for j in range(2):
                                last = mm(PS[2][:, hc(j)], EB[:, 2 * ch + j, :], ZB[:, hc(j)], start=True, stop=True)
                            last.then_inc(s["sa_ps"], 1)
                            pe.wait_ge(s["sa_copied"], ch + 1)
                            if ch < 3:
                                mm(PS[4][:, 0:P], TT[:, 0, ch, :], SA, start=True, stop=False)
                                last = mm(PS[4][:, 0:P], TT[:, 1, ch, :], TT[:, 2, ch, :], start=False, stop=True)
                                last.then_inc(s["s_ps"], 1)
                            if ch:
                                pe.wait_ge(s["y_copied"], ch)
                            for j in range(2):
                                u, o = 2 * ch + j, PS[3][j * HD:(j + 1) * HD, 0:P]
                                mm(o, SA[:, hc(j)], UB[:, u, 128:256], start=True, stop=False)
                                last = mm(o, v(j), UB[:, u, 384:512], start=False, stop=(ch == 0))
                            if ch:
                                last = mm(PS[3][:, 0:P], ST, AR[:, c, ch, 1, :], start=False, stop=True)
                            last.then_inc(s["y_ps"], 1)
                        else:
                            pe.wait_ge(s["y_copied"], 4)
                            mm(PS[1][:, :], cst("head"), Y[:, c, :], start=True, stop=True).then_inc(s["fin_ps"], 1)
                            pe.wait_ge(s["fin_in"], 1)
                            mm(PS[2][:, :], cst("head"), UB[:, 1, :], start=True, stop=True).then_inc(s["fin_ps"], 1)
                            pe.wait_ge(s["fin_sq"], 1)
                            mm(PS[3][:, :], cst("head"), UB[:, 2, :], start=True, stop=True).then_inc(s["fin_ps"], 1)

                    def attn(m, u):
                        s, nm = mix[m], 2 if m == "D" else 1
                        if u == 0:
                            pe.wait_ge(roped[m], 2)
                            pe.wait_ge(sgu_done, 1)
                            pe.wait_ge(proj_copied, len(PROJ) - 8)
                            for j in range(4):
                                if j >= 2:
                                    pe.wait_ge(s["qk_copied"], j - 1)
                                for i in range(NT):
                                    last = tr(PS[5 + j % 2][:, i * P:(i + 1) * P], QKV[m][:, i, j * P:(j + 1) * P], ident)
                                last.then_inc(s["qk_ps"], 1)
                            pe.wait_ge(s["qk_copied"], 4)
                        if u < 16:
                            i, h = unit_of[u]
                            w = (i + 1) * P
                            for a in range(nm):
                                n = u if m == "A" else 2 * u + a
                                if n >= 2:
                                    pe.wait_ge(s["exped"], n - 1)
                                if m == "A":
                                    rows = slice((h % 2) * 64, (h % 2) * 64 + 64)
                                else:
                                    rows = slice((h % 2) * 64 + a * 32, (h % 2) * 64 + a * 32 + 32)
                                bank = PS[5 + n % 2]
                                mm(bank[:, 0:w], QKT[rows, h // 2, i * P:w], QKT[rows, 2 + h // 2, 0:w], start=True, stop=False)
                                mm(bank[:, i * P:w], ident, cst("causal"), start=False, stop=True).then_inc(s["scores"], 1)
                        if 1 <= u <= 16:
                            i, h = unit_of[u - 1]
                            pe.wait_ge(s["exped"] if m == "A" else s["probs"], u)
                            if u >= 2:
                                pe.wait_ge(s["pt_copied"], u - 1)
                            for b in range(i + 1):
                                last = tr(PS[7][:, b * P:(b + 1) * P], PB[:, (u - 1) % 2, nm - 1, b * P:(b + 1) * P], ident)
                            last.then_inc(s["pt_ps"], 1)
                        if u >= 2:
                            n = u - 2
                            i, h = unit_of[n]
                            pe.wait_ge(s["pt_copied"], n + 1)
                            if n >= 1:
                                pe.wait_ge(s["o_done"], n)
                            elif m == "D":
                                pe.wait_ge(mix["A"]["o_done"], 16)
                            v0 = (0 if m == "A" else GW) + h * HD
                            for b in range(i + 1):
                                last = mm(PS[0][:, 0:HD], PT[:, n % 2, b * P:(b + 1) * P], VAD[:, b, v0:v0 + HD],
                                          start=(b == 0), stop=(b == i))
                            last.then_inc(s["o_ps"], 1)

                    run_mixers(proj=project, rwkv=rwkv, attn=attn, sgu_out=mix_positions)

                    pe.wait_ge(mixed_done, 1)
                    srcs = [(QKV["A"], 0), (QKV["A"], 1), (UV, 0), (UV, 1), (QKV["D"], 0), (QKV["D"], 1)]
                    for j, (src, t) in enumerate(srcs):
                        for i in range(NT):
                            last = tr(PS[j][:, i * P:(i + 1) * P], src[:, i, t * P:(t + 1) * P], ident)
                        last.then_inc(mt_ps, 1)
                    pe.wait_ge(mt_a, 3)
                    pe.wait_ge(mt_v, 3)
                    for n in range(2):
                        pe.wait_ge(slot_full[n], 48)
                        w = SLOT[n].rearrange("p (k n) -> p k n", k=KD)
                        for i in range(NT):
                            for k in range(KD):
                                src = Y[:, k - 2, :] if k in (2, 3) else MT[:, MT_OF[k], :]
                                last = mm(PS[4 * n + i][:, :], src[:, i * P:(i + 1) * P], w[:, k, :], start=(k == 0), stop=(k == KD - 1))
                            last.then_inc(res_ps, 1)

                    pe.wait_ge(res_added, 8)
                    for k in range(KD):
                        for i in range(NT):
                            if k == 0:
                                pe.wait_ge(n2_scaled, i + 1)
                            last = tr(PS[k][:, i * P:(i + 1) * P], XN2[:, i, k * P:(k + 1) * P], ident)
                        last.then_inc(n2_turned, 1)
                    pe.wait_ge(n2_copied_a, 4)
                    pe.wait_ge(n2_copied_v, 4)
                    rw = RT[:, :].rearrange("p (k n) -> p k n", k=KD)
                    for i in range(NT):
                        for k in range(KD):
                            last = mm(PS[0][:, i * NR:(i + 1) * NR], XNT[:, k, i * P:(i + 1) * P], rw[:, k, :], start=(k == 0), stop=(k == KD - 1))
                    last.then_inc(logits, 1)
                    pe.wait_ge(chosen, 1)
                    M = RW[:, 0:NT * NE].rearrange("p (i e) -> p i e", i=NT)
                    before_me = CFs[:, CF["unit"][0]:CF["unit"][0] + P]
                    for i in range(NT):
                        o = PS[1][:, i * NE:(i + 1) * NE]
                        mm(o, before_me, M[:, i, :], start=True, stop=(i == 0))
                        for b in range(i):
                            mm(o, cst("ones"), M[:, b, :], start=False, stop=(b == i - 1))
                    for i in range(NT):
                        last = mm(PS[1][:, NT * NE:(NT + 1) * NE], cst("ones"), M[:, i, :], start=(i == 0), stop=(i == NT - 1))
                    last.then_inc(ranks, 1)

                    def turn_rows(src, done):
                        rows = src[0:CAP, :].rearrange("s (p k) -> s p k", k=KD)
                        for k in range(KD):
                            last = tr(PS[k // 4][:, (k % 4) * CAP:(k % 4 + 1) * CAP], rows[:, :, k], ident[0:CAP, 0:CAP])
                        last.then_inc(done, 1)

                    def gate_or_up(w, bank):
                        w = w.rearrange("p (k n) -> p k n", k=KD)
                        for f in range(KF):
                            for k in range(KD):
                                last = mm(bank[:, f * CAP:(f + 1) * CAP], w[:, k, f * P:(f + 1) * P], XT[:, k, :], start=(k == 0), stop=(k == KD - 1))
                        return last

                    def down(w):
                        w = w.rearrange("p (k d) -> p k d", k=KF)
                        for n in range(KD):
                            for k in range(KF):
                                last = mm(PS[4 + n // 4][:, (n % 4) * CAP:(n % 4 + 1) * CAP], w[:, k, n * P:(n + 1) * P], HT[:, k * CAP:(k + 1) * CAP],
                                          start=(k == 0), stop=(k == KF - 1))
                        return last

                    def turn_results():
                        for n in range(KD):
                            last = tr(PS[6 + n // 4][0:CAP, (n % 4) * P:(n % 4 + 1) * P], YT[:, n * CAP:(n + 1) * CAP], ident)
                        return last

                    full0 = (3, 3, 2, 0, 0, 0)

                    def weights(m, i, h):
                        slot = (2 + 3 * h + m) % 6
                        pe.wait_ge(slot_full[slot], 16 * (i + full0[slot] + 1))
                        return SLOT[slot]

                    def gate(i, h):
                        pe.wait_ge(xt_copied, 2 * i + h + 1)
                        gate_or_up(weights(0, i, h), PS[2]).then_inc(gate_ps, 1)

                    def expert(i, h, last=False):
                        e = 2 * i + h
                        gate_or_up(weights(1, i, h), PS[3]).then_inc(up_ps, 1)
                        if h == 0:
                            pe.wait_ge(rows_full[1], 16 * (i + 1))
                        else:
                            pe.wait_ge(rows_full[0], 16 * (i + 2))
                        pe.sem_inc(pe_passed, 1)
                        turn_rows(XR[1 - h], xt_ps)
                        pe.wait_ge(hidden, e + 1)
                        pe.wait_ge(yt_copied, e + 1)
                        down(weights(2, i, h)).then_inc(y2_ps, 1)
                        if not last:
                            gate(i + h, 1 - h)
                        pe.wait_ge(yt_copied, e + 2)
                        pe.wait_ge(y2_copied, e + 1)
                        pe.sem_inc(pe_passed, 1)
                        turn_results().then_inc(rows_ps, 1)

                    pe.sem_inc(rows_ps, 1)
                    pe.wait_ge(route_in, 1)
                    pe.wait_ge(rows_full[0], 16)
                    turn_rows(XR[0], xt_ps)
                    gate(0, 0)
                    with pe.Fori(0, NE // 2 - 1) as i:
                        for h in range(2):
                            expert(i, h)
                    expert(NE // 2 - 1, 0)
                    expert(NE // 2 - 1, 1, last=True)
                    nov = pe.value_load(OVI[0:1, NOV:NOV + 1], min_val=0, max_val=NOV)
                    with pe.If(nov > 0):
                        pe.wait_ge(xt_copied, NE + 1)
                        pe.wait_ge(y2_copied, NE + 1)
                        with pe.Fori(0, nov) as j:
                            pe.wait_ge(ov_in, 64 * (j + 1))
                            pe.sem_inc(pe_passed, 1)
                            turn_rows(XR[1], ov_turn)
                            pe.wait_ge(ov_turned, j + 1)
                            gate_or_up(SLOT[2], PS[2])
                            gate_or_up(SLOT[3], PS[3]).then_inc(ov_gu, 1)
                            pe.wait_ge(ov_hid, j + 1)
                            down(SLOT[4]).then_inc(ov_y, 1)
                            pe.wait_ge(ov_yt, j + 1)
                            pe.sem_inc(pe_passed, 1)
                            turn_results().then_inc(ov_rows, 1)
                    pe.nop()

                @block.scalar
                def _(act):
                    ac = nc.scalar.activation
                    roots = [0]

                    def root(t):
                        roots[0] += 1
                        act.wait_ge(root_in, roots[0])
                        ac(t, t, ACT.Sqrt).then_inc(root_out, 1)

                    for i in range(NT):
                        ac(XNTb[:, i * D:(i + 1) * D], X3[:, i, :], ACT.Square,
                           accum_out=ss1[:, i:i + 1]).then_inc(n1_squares, 1)
                    root(rs1)
                    act.wait_ge(params_in, 96)
                    act.wait_ge(n1_scaled, 4)
                    for k in range(0, KD, 2):
                        act.wait_ge(n1_turned, k + 1)
                        ac(XNT[:, k, :], PS[k][:, :], ACT.Copy, scale=pc("g1", k)).then_inc(n1_copied_a, 1)
                    act.wait_ge(prep_done, 1)
                    for g in range(8):
                        act.wait_ge(proj_ps, g + 1)
                        ac(XS[:, g, :], PS[g][:, :], ACT.Copy, scale=OMU[:, g:g + 1]).then_inc(xs_scaled, 1)
                        if g == 0:
                            with act.If(layer < 1):
                                act.wait_ge(zero_tile, 1)
                                for rows, first in ((xs_e, 0), (ys_e, NE)):
                                    for e in range(first, NE + NOV, ZB_N):
                                        n = min(ZB_N, NE + NOV - e)
                                        act.dma_start(rows[e:e + n, :, :].rearrange("e s d -> s e d"),
                                                      XR[0][0:CAP, None, :].to_broadcast([CAP, n, D])).then_inc(slots_zeroed, 16)
                        if g == 6:
                            act.wait_ge(xs_mixed, 1)
                            ac(XS[0:64, 0, :], XS[0:64, 0, :], ACT.Tanh).then_inc(lora_in, 1)
                        if g == 7:
                            act.wait_ge(xs_mixed, 6)
                            ac(XS[:, 5, :], XS[:, 5, :], ACT.Sigmoid).then_inc(lora_in, 1)
                    def take(g):
                        kind, a = PROJ[g]
                        act.wait_ge(proj_ps, g + 1)
                        src = PS[bank_of[g]][:, :]
                        if kind == "t":
                            b, i = a
                            if b == 3 and i == 0:
                                act.wait_ge(slots_zeroed, 16 * ZEROING)
                            ac(BLOCK_TO[b][:, i, :], src, ACT.Copy).then_inc(proj_copied, 1)
                        elif kind == "n":
                            ac(WORK[5 + a][:, 0:SEQ], src, ACT.Sqrt).then_inc(proj_copied, 1)
                        else:
                            w, c = divmod(a, 2)
                            if w == 0:
                                ac(WORK[0 + c][:, 0:SEQ], src, ACT.Sigmoid, bias=pc("w0", c)).then_inc(proj_copied, 1)
                            elif w == 1:
                                ac(WORK[2 + c][:, 0:SEQ], src, ACT.Sigmoid, bias=pc("a0", c)).then_inc(proj_copied, 1)
                            else:
                                ac(XS[:, (0, 5)[c], :], src, ACT.Copy).then_inc(proj_copied, 1)

                    def decays(c):
                        act.wait_ge(cs_ready, c + 1)
                        if c:
                            act.wait_ge(scan_in, 1)
                        ac(WORK[4], WORK[0], ACT.Exp).then_inc(exps_ready, 1)
                        ac(WORK[2], WORK[0], ACT.Exp, scale=-1.0).then_inc(exps_ready, 1)

                    for g in range(8, LATE):
                        take(g)
                        if PROJ[g] == ("t", (0, 1)):
                            decays(0)
                        if PROJ[g] == ("t", (1, 0)):
                            decays(1)

                    def gelus():
                        act.wait_ge(lam_in, 1)
                        ac(lamt[:, 0:2], lamt[:, 0:2], ACT.Exp).then_inc(lam_in, 1)
                        act.wait_ge(proj_copied, copied("t", (2, NT - 1)))
                        for t in range(2):
                            ac(UV[:, 2 * t:2 * t + 2, :], UV[:, 2 * t:2 * t + 2, :], ACT.Gelu).then_inc(gelu_done, 1)
                        root(srs)

                    def rwkv(c, m, step):
                        s = mix[m]
                        if step == "T":
                            for w in range(3):
                                act.wait_ge(s["turn_ps"], w + 1)
                                ac(TT[:, w, :, :].rearrange("p m n -> p (m n)"), PS[1 + w][:, :], ACT.Copy).then_inc(s["turned"], 1)
                        elif step[0] == "L":
                            for q in range(2):
                                act.wait_ge(s["m1_ps"], 2 * (step[1] - 1) + q + 1)
                                if step[1] > 1:
                                    act.wait_ge(s["de_ps"], 4 * (step[1] - 2) + 2 * q + 2)
                                ac(MB[:, 4 * q:4 * q + 4, :].rearrange("p u n -> p (u n)"), PS[1 + q][:, :], ACT.Copy).then_inc(s["m1_copied"], 1)
                        elif step[0] == "C":
                            ch = step[1]
                            act.wait_ge(s["z_ps"], ch + 1)
                            ac(ZB, PS[1][:, 0:P], ACT.Copy).then_inc(s["z_copied"], 1)
                            act.wait_ge(s["y_ps"], ch + 1)
                            act.wait_ge(roped["A"], 2)
                            ac(Y[:, c, ch * P:(ch + 1) * P], PS[3][:, 0:P], ACT.Copy).then_inc(s["y_copied"], 1)
                        elif step == "F":
                            act.wait_ge(s["fin_in"], 2)
                            ac(UB[:, 2, :], Y[:, c, :], ACT.Square).then_inc(s["fin_sq"], 1)
                            root(UB[:, 3, :])

                    def attn(m, u):
                        s, nm = mix[m], 2 if m == "D" else 1
                        if u == 0:
                            scale = float(HD) ** -0.5 if m == "A" else 32.0 ** -0.5
                            for j in range(4):
                                act.wait_ge(s["qk_ps"], j + 1)
                                ac(QKT[:, j, :], PS[5 + j % 2][:, :], ACT.Copy, scale=scale if j < 2 else 1.0).then_inc(s["qk_copied"], 1)
                        if u < 16:
                            i, h = unit_of[u]
                            w = (i + 1) * P
                            if u >= 2:
                                act.wait_ge(s["pt_ps"], u - 1)
                            for a in range(nm):
                                n = nm * u + a
                                col = (0 if m == "A" else 16) + n
                                act.wait_ge(s["maxed"], n + 1)
                                ac(PB[:, u % 2, a, 0:w], PS[5 + n % 2][:, 0:w], ACT.Exp, bias=nmx[:, col:col + 1],
                                   accum_out=sums[:, col:col + 1]).then_inc(s["exped"], 1)
                        if 1 <= u <= 16:
                            i, h = unit_of[u - 1]
                            w = (i + 1) * P
                            act.wait_ge(s["pt_ps"], u)
                            if u >= 3:
                                act.wait_ge(s["o_ps"], u - 2)
                            ac(PT[:, (u - 1) % 2, 0:w], PS[7][:, 0:w], ACT.Copy).then_inc(s["pt_copied"], 1)

                    run_mixers(proj=take, rwkv=rwkv, attn=attn, sgu_in=gelus)
                    root(dss)
                    for j in range(0, 6, 2):
                        act.wait_ge(mt_ps, j + 1)
                        ac(MT[:, j, :], PS[j][:, :], ACT.Copy).then_inc(mt_a, 1)
                    for i in range(NT):
                        act.wait_ge(res_added, 5 + i)
                        ac(TOK[:, i * D:(i + 1) * D], X3[:, i, :], ACT.Square, accum_out=ss2[:, i:i + 1]).then_inc(n2_squares, 1)
                    root(rs2)
                    for k in range(0, KD, 2):
                        act.wait_ge(n2_turned, k + 1)
                        ac(XNT[:, k, :], PS[k][:, :], ACT.Copy).then_inc(n2_copied_a, 1)
                    act.wait_ge(exp_in, 1)
                    ac(RW[:, 640:640 + 16], RW[:, 640:640 + 16], ACT.Exp).then_inc(exp_done, 1)
                    act.wait_ge(exp_in, 2)
                    ac(RW[:, 656:660], RW[:, 656:660], ACT.Exp).then_inc(exp_done, 1)

                    act.sem_inc(yt_copied, 1)
                    with act.Fori(0, NE // 2) as i:
                        for h in range(2):
                            e = 2 * i + h
                            act.wait_ge(gate_ps, e + 1)
                            ac(HS, PS[2][:, 0:KF * CAP], ACT.Silu).then_inc(gated, 1)
                            act.wait_ge(y2_ps, e + 1)
                            act.wait_ge(rows_ps, e + 1)
                            ac(YT.rearrange("p (t n) -> p t n", t=2), half_banks(4), ACT.Copy).then_inc(yt_copied, 1)
                            act.wait_ge(y2_copied, e + 2)
                            act.dma_start(ys_e[bass.ds(e, 1)].rearrange("a s d -> s (a d)"), YS[h][0:CAP, :]).then_inc(y2_stored[h], 16)
                    nov = act.value_load(OVI[0:1, NOV:NOV + 1], min_val=0, max_val=NOV)
                    with act.If(nov > 0):
                        with act.Fori(0, nov) as j:
                            act.wait_ge(ov_gu, j + 1)
                            ac(HS, PS[2][:, 0:KF * CAP], ACT.Silu).then_inc(ov_silu, 1)
                            act.wait_ge(ov_y, j + 1)
                            ac(YT.rearrange("p (t n) -> p t n", t=2), half_banks(4), ACT.Copy).then_inc(ov_yt, 1)
                    act.nop()

                @block.vector
                def _(dve):
                    V = nc.vector
                    count, roots = [0], [0]

                    def link(ins):
                        count[0] += 1
                        ins.then_inc(vec, 1)
                        dve.wait_ge(vec, count[0])

                    def rstd(out, ss, scale, eps):
                        V.tensor_scalar(out, ss, scale, eps, ALU.mult, ALU.add).then_inc(root_in, 1)
                        roots[0] += 1
                        dve.wait_ge(root_out, roots[0])
                        link(V.reciprocal(out, out))

                    dve.wait_ge(n1_squares, 4)
                    rstd(rs1, ss1, 1.0 / D, RMS_EPS)
                    for i in range(NT):
                        V.tensor_scalar(XN[:, i, :], X3[:, i, :], rs1[:, i:i + 1], None, ALU.mult).then_inc(n1_scaled, 1)
                    dve.wait_ge(params_in, 96)
                    link(V.tensor_scalar(OMU[:, :], PCs[:, PC["mu"][0]:PC["mu"][0] + 8], -1.0, 1.0, ALU.mult, ALU.add))
                    V.tensor_scalar(OKA[:, :], PCs[:, PC["ka"][0]:PC["ka"][0] + 2], -1.0, 1.0, ALU.mult, ALU.add).then_inc(prep_done, 1)
                    for k in range(1, KD, 2):
                        dve.wait_ge(n1_turned, k + 1)
                        V.tensor_scalar(XNT[:, k, :], PS[k][:, :], pc("g1", k), None, ALU.mult).then_inc(n1_copied_v, 1)
                    V.tensor_tensor(SGT, SGT, CFs[:, CF["unit"][0] + P:CF["unit"][0] + 2 * P][:, None, :].to_broadcast([P, HEADS, P]),
                                    ALU.mult).then_inc(sgu_w, 1)
                    lt = SA[:, 0:64]
                    link(V.tensor_tensor(lt[:, 0:32], pr("lq1"), pr("lk1"), ALU.mult))
                    link(V.tensor_tensor(lt[:, 32:64], pr("lq2"), pr("lk2"), ALU.mult))
                    V.tensor_reduce(lamt[:, 0:2], lt.rearrange("p (a n) -> p a n", a=2), AX.X, ALU.add).then_inc(lam_in, 1)
                    for g in range(8):
                        dve.wait_ge(xs_scaled, g + 1)
                        V.scalar_tensor_tensor(XS[:, g, 1:], PS[g][:, 0:SEQ - 1], pc("mu", g), XS[:, g, 1:], ALU.mult, ALU.add).then_inc(xs_mixed, 1)
                    dve.wait_ge(xs_mixed, 8)
                    for c in range(2):
                        link(V.tensor_scalar(BT[:, c, :], XS[:, 1 + c, :], pc("kk", c), None, ALU.mult))
                        V.tensor_tensor(WORK[5 + c][:, 0:SEQ], BT[:, c, :], BT[:, c, :], ALU.mult).then_inc(kk_sq, 1)
                    for c in range(2):
                        dve.wait_ge(proj_copied, copied("n", c))
                        a, k, b = WORK[2 + c][:, 0:SEQ], XS[:, 1 + c, :], BT[:, c, :]
                        link(V.tensor_scalar(WORK[5][:, 0:SEQ], WORK[5 + c][:, 0:SEQ], 1e-12, None, ALU.max))
                        link(V.reciprocal(WORK[5][:, 0:SEQ], WORK[5][:, 0:SEQ]))
                        link(V.tensor_tensor(b, b, WORK[5][:, 0:SEQ], ALU.mult))
                        link(V.tensor_scalar(WORK[5][:, 0:SEQ], a, pc("ka", c), OKA[:, c:c + 1], ALU.mult, ALU.add))
                        link(V.tensor_tensor(k, k, WORK[5][:, 0:SEQ], ALU.mult))
                        link(V.tensor_tensor(KT[:, c, :], b, a, ALU.mult))
                        sg = WORK[0 + c][:, 0:SEQ].rearrange("p (m t) -> p m t", m=4)
                        cs = WORK[5]
                        cs3 = cs.rearrange("p (m t) -> p m t", m=4)
                        link(V.memset(cs3[:, :, 0:1], 0.0))
                        for ch in range(4):
                            link(V.tensor_tensor_scan(cs3[:, ch, 1:P + 1], cst("ones"), sg[:, ch, :], 0.0, ALU.mult, ALU.add))
                        link(V.tensor_tensor(WORK[0].rearrange("p (m t) -> p m t", m=4), cs3,
                                             cs3[:, :, 64:65].to_broadcast([P, 4, P + 1]), ALU.subtract))
                        V.tensor_scalar(WORK[0], WORK[0], LOG_DECAY, None, ALU.mult).then_inc(cs_ready, 1)
                        dve.wait_ge(exps_ready, 2 * c + 2)
                        ep = WORK[4].rearrange("p (m t) -> p m t", m=4)
                        en = WORK[2].rearrange("p (m t) -> p m t", m=4)
                        b3 = b.rearrange("p (m t) -> p m t", m=4)
                        kb3 = KT[:, c, :].rearrange("p (m t) -> p m t", m=4)
                        link(V.tensor_copy(epend[:, 4 * c:4 * c + 4], ep[:, :, P]))
                        link(V.tensor_copy(enbeg[:, 4 * c:4 * c + 4], en[:, :, 0]))
                        link(V.tensor_tensor(carry[:, 4 * c:4 * c + 3], epend[:, 4 * c:4 * c + 3], enbeg[:, 4 * c + 1:4 * c + 4], ALU.mult))
                        link(V.scalar_tensor_tensor(AR[:, c, :, 0, :], b3, -1.0, ep[:, :, 0:P], ALU.mult, ALU.mult))
                        link(V.tensor_tensor(AR[:, c, :, 1, :], XS[:, 6 + c, :].rearrange("p (m t) -> p m t", m=4), ep[:, :, 1:], ALU.mult))
                        link(V.tensor_tensor(b3, kb3, en[:, :, 1:], ALU.mult))
                        V.tensor_tensor(kb3, k.rearrange("p (m t) -> p m t", m=4), en[:, :, 1:], ALU.mult).then_inc(scan_in, 1)
                    def norm_v():
                        dve.wait_ge(gelu_done, 2)
                        for i in range(NT):
                            link(V.bn_stats(bns[:, 6 * i:6 * i + 6], UV[:, i, GW:]))
                            link(V.bn_aggr(bnv[:, 2 * i:2 * i + 2], bns[:, 6 * i:6 * i + 6]))
                        rstd(srs, bnv.rearrange("p (i t) -> p i t", t=2)[:, :, 1], 1.0, LN_EPS)
                        for i in range(NT):
                            link(V.tensor_scalar(UV[:, i, GW:], UV[:, i, GW:], bnv[:, 2 * i:2 * i + 1], srs[:, i:i + 1], ALU.subtract, ALU.mult))
                        link(V.tensor_tensor(UV[:, :, GW:], UV[:, :, GW:], pr("sgug")[:, None, :].to_broadcast([P, NT, GW]), ALU.mult))
                        V.tensor_tensor(UV[:, :, GW:], UV[:, :, GW:], pr("sgub")[:, None, :].to_broadcast([P, NT, GW]), ALU.add).then_inc(sgu_v, 1)
                        dve.wait_ge(lam_in, 2)
                        link(V.tensor_tensor(lamt[:, 2:3], lamt[:, 0:1], lamt[:, 1:2], ALU.subtract))
                        link(V.tensor_tensor(lamv, lamt[:, 2:3], pr("lam"), ALU.add))

                    def gate_u():
                        dve.wait_ge(sgu_ps, 1)
                        for h in range(HEADS):
                            for t in range(2):
                                ps = PS[6 + t][:, :].rearrange("p (i n) -> p i n", i=2)[:, :, h * HD:(h + 1) * HD]
                                u = UV[:, 2 * t:2 * t + 2, h * HD:(h + 1) * HD]
                                link(V.scalar_tensor_tensor(u, ps, pc("sgub", h), u, ALU.add, ALU.mult))
                        dve.sem_inc(sgu_done, 1)

                    def rwkv(c, m, step):
                        s = mix[m]
                        mask = lambda n, up: CMs[:, (7 * up + n) * P:(7 * up + n + 1) * P][:, None, :].to_broadcast([P, 4, P])
                        if step == "P":
                            for u in range(8):
                                dve.wait_ge(s["prod_ps"], u + 1)
                                V.tensor_tensor(UB[:, u, :], PS[1 + u % 2][:, :], cst("unit"), ALU.mult).then_inc(s["prod_masked"], 1)
                            dve.wait_ge(s["eye"], 2)
                            for j in range(2):
                                dve.wait_ge(s["prod_ps"], 9 + j)
                                V.copy_predicated(DB[:, j::2, :], mask(0, 0), PS[3 + j][:, :].rearrange("p (u n) -> p u n", u=4)).then_inc(s["prod_masked"], 1)
                            dve.wait_ge(s["prod_masked"], 10)
                            for q in range(2):
                                V.copy_predicated(EB[:, 4 * q:4 * q + 4, :], mask(0, 1), UB[:, 4 * q:4 * q + 4, 0:P]).then_inc(s["eye"], 2)
                        elif step[0] == "L":
                            n = step[1]
                            for q in range(2):
                                for side in range(2):
                                    if n == 6 and side == 0:
                                        continue
                                    done = 4 * (n - 1) + 2 * q + side + 1 if n < 6 else 21 + q
                                    dve.wait_ge(s["de_ps"], done)
                                    dst = (DB, EB)[side][:, 4 * q:4 * q + 4, :]
                                    V.copy_predicated(dst, mask(n, side), PS[3 + side][:, :].rearrange("p (u n) -> p u n", u=4)).then_inc(s["de_merged"], 1)
                        elif step[0] == "C":
                            ch = step[1]
                            dve.wait_ge(s["sa_ps"], ch + 1)
                            V.tensor_copy(SA, PS[2][:, 0:P]).then_inc(s["sa_copied"], 1)
                            if ch < 3:
                                dve.wait_ge(s["s_ps"], ch + 1)
                                cc = carry[:, 4 * c + ch:4 * c + ch + 1]
                                dve.wait_ge(s["y_ps"], ch + 1)
                                t = PS[4][:, 0:P]
                                if ch:
                                    link(V.tensor_tensor(ST, t, ST, ALU.add))
                                    t = ST
                                V.scalar_tensor_tensor(ST, t, cc, cst("head"), ALU.mult, ALU.mult).then_inc(s["s_done"], 1)
                        elif step == "F":
                            y, r, k, v = Y[:, c, :], XS[:, 6 + c, :], XS[:, 1 + c, :], XS[:, 3 + c, :]
                            dve.wait_ge(s["y_ps"], 4)
                            link(V.tensor_tensor(UB[:, 1, :], r, k, ALU.mult))
                            V.tensor_scalar(UB[:, 1, :], UB[:, 1, :], pc("rk", c), None, ALU.mult).then_inc(s["fin_in"], 1)
                            dve.wait_ge(s["fin_ps"], 1)
                            V.scalar_tensor_tensor(y, PS[1][:, :], -1.0 / HD, y, ALU.mult, ALU.add).then_inc(s["fin_in"], 1)
                            dve.wait_ge(s["fin_ps"], 3)
                            rstd(UB[:, 3, :], PS[3][:, :], 1.0 / HD, RWKV_LN_EPS)
                            dve.wait_ge(s["fin_in"], 2)
                            link(V.tensor_tensor(y, y, UB[:, 3, :], ALU.mult))
                            link(V.tensor_scalar(y, y, pc("lng", c), pc("lnb", c), ALU.mult, ALU.add))
                            link(V.tensor_tensor(UB[:, 4, :], PS[2][:, :], v, ALU.mult))
                            link(V.tensor_tensor(y, y, UB[:, 4, :], ALU.add))
                            link(V.tensor_tensor(y, y, XS[:, (0, 5)[c], :], ALU.mult))
                            dve.sem_inc(s["y_done"], 1)

                    def attn(m, u):
                        s, nm = mix[m], 2 if m == "D" else 1
                        base = 0 if m == "A" else 16
                        if u < 16:
                            i, h = unit_of[u]
                            w = (i + 1) * P
                            for a in range(nm):
                                n = nm * u + a
                                dve.wait_ge(s["scores"], n + 1)
                                V.tensor_reduce(nmx[:, base + n:base + n + 1], PS[5 + n % 2][:, 0:w], AX.X, ALU.max, negate=True).then_inc(s["maxed"], 1)
                        if 1 <= u <= 16:
                            i, h = unit_of[u - 1]
                            w = (i + 1) * P
                            n = nm * (u - 1)
                            dve.wait_ge(s["exped"], n + nm)
                            link(V.reciprocal(rsum[:, base + n:base + n + nm], sums[:, base + n:base + n + nm]))
                            if m == "D":
                                r2 = rsum[:, base + n + 1:base + n + 2]
                                link(V.tensor_scalar(r2, r2, lamv, -1.0, ALU.mult, ALU.mult))
                                p0, p1 = PB[:, (u - 1) % 2, 0, 0:w], PB[:, (u - 1) % 2, 1, 0:w]
                                link(V.tensor_scalar(p1, p1, r2, None, ALU.mult))
                                V.scalar_tensor_tensor(p1, p0, rsum[:, base + n:base + n + 1], p1, ALU.mult, ALU.add).then_inc(s["probs"], 1)
                        if u >= 2:
                            n = u - 2
                            i, h = unit_of[n]
                            dve.wait_ge(s["o_ps"], n + 1)
                            o = QKV[m][:, i, h * HD:(h + 1) * HD]
                            if m == "A":
                                V.tensor_scalar(o, PS[0][:, 0:HD], rsum[:, n:n + 1], None, ALU.mult).then_inc(s["o_done"], 1)
                            else:
                                V.tensor_copy(o, PS[0][:, 0:HD]).then_inc(s["o_done"], 1)

                    run_mixers(rwkv=rwkv, attn=attn, sgu_in=norm_v, sgu_out=gate_u)

                    dve.wait_ge(mix["D"]["o_done"], 16)
                    o = QKV["D"][:, :, 0:GW].rearrange("p i (h n) -> p i h n", h=HEADS)
                    sq = UB[:, 0:2, :].rearrange("p u n -> p (u n)").rearrange("p (i h n) -> p i h n", i=NT, h=HEADS)
                    for i in range(NT):
                        link(V.tensor_tensor(sq[:, i], o[:, i], o[:, i], ALU.mult))
                    link(V.tensor_reduce(dss, UB[:, 0:2, :].rearrange("p u n -> p (u n)").rearrange("p (a n) -> p a n", n=HD), AX.X, ALU.add))
                    rstd(dss, dss, 1.0 / HD, SUBLN_EPS)
                    link(V.tensor_scalar(dss, dss, pr("oml"), None, ALU.mult))
                    d3 = dss.rearrange("p (i h) -> p i h", i=NT)
                    for i in range(NT):
                        link(V.tensor_tensor(o[:, i], o[:, i], d3[:, i, :, None].to_broadcast([P, HEADS, HD]), ALU.mult))
                    for i in range(NT):
                        link(V.tensor_tensor(o[:, i], o[:, i], pr("subln")[:, None, :].to_broadcast([P, HEADS, HD]), ALU.mult))
                    dve.sem_inc(mixed_done, 1)

                    for j in range(1, 6, 2):
                        dve.wait_ge(mt_ps, j + 1)
                        V.tensor_copy(MT[:, j, :], PS[j][:, :]).then_inc(mt_v, 1)
                    for g in range(8):
                        n, i = divmod(g, 4)
                        dve.wait_ge(res_ps, g + 1)
                        xv = X3[:, i, n * BN:(n + 1) * BN]
                        V.tensor_tensor(xv, PS[g][:, :], xv, ALU.add).then_inc(res_added, 1)
                    dve.wait_ge(n2_squares, 4)
                    rstd(rs2, ss2, 1.0 / D, RMS_EPS)
                    dve.wait_ge(g2row_in, 16)
                    for i in range(NT):
                        V.scalar_tensor_tensor(XN2[:, i, :], X3[:, i, :], rs2[:, i:i + 1], G2ROW, ALU.mult, ALU.mult).then_inc(n2_scaled, 1)
                    for k in range(1, KD, 2):
                        dve.wait_ge(n2_turned, k + 1)
                        V.tensor_copy(XNT[:, k, :], PS[k][:, :]).then_inc(n2_copied_v, 1)

                    dve.wait_ge(logits, 1)
                    rv = lambda lo, n: RW[:, lo:lo + n]
                    L = rv(0, NT * NR).rearrange("p (i n) -> p i n", i=NT)
                    link(V.tensor_tensor(L, PS[0][:, 0:NT * NR].rearrange("p (i n) -> p i n", i=NT),
                                         pr("rb")[:, None, :].to_broadcast([P, NT, NR]), ALU.add))

                    def first_max(vals, n, down, top, hot):
                        t3 = top[:, :, None]
                        wide = [P, NT, n]
                        link(V.tensor_reduce(top, vals, AX.X, ALU.max))
                        link(V.tensor_tensor(hot, vals, t3.to_broadcast(wide), ALU.is_equal))
                        link(V.tensor_tensor(hot, hot, down[:, None, :].to_broadcast(wide), ALU.mult))
                        link(V.tensor_reduce(rv(760, 4), hot, AX.X, ALU.max))
                        link(V.tensor_tensor(hot, hot, rv(760, 4)[:, :, None].to_broadcast(wide), ALU.is_equal))

                    gl = L[:, :, 0:GROUPS]
                    gtop, ghot = rv(144, 4), rv(148, 16).rearrange("p (i n) -> p i n", i=NT)
                    first_max(gl, GROUPS, cst("down4"), gtop, ghot)
                    gexp = rv(640, 16).rearrange("p (i n) -> p i n", i=NT)
                    V.tensor_tensor(gexp, gl, gtop[:, :, None].to_broadcast([P, NT, GROUPS]), ALU.subtract).then_inc(exp_in, 1)
                    pg = rv(164, 128).rearrange("p (i g e) -> p i g e", i=NT, g=GROUPS)
                    for i in range(NT):
                        link(V.tensor_tensor(pg[:, i], L[:, i, GROUPS:].rearrange("p (g e) -> p g e", g=GROUPS),
                                             ghot[:, i, :, None].to_broadcast([P, GROUPS, EPG]), ALU.mult))
                    el = rv(292, 32).rearrange("p (i e) -> p i e", i=NT)
                    link(V.tensor_reduce(el, rv(164, 128).rearrange("p (i g e) -> p i e g", i=NT, g=GROUPS), AX.X, ALU.add))
                    t1, h1 = rv(324, 4), rv(328, 32).rearrange("p (i e) -> p i e", i=NT)
                    first_max(el, EPG, cst("down8"), t1, h1)
                    link(V.scalar_tensor_tensor(el, h1, NEG, el, ALU.mult, ALU.add))
                    t2, h2 = rv(360, 4), rv(364, 32).rearrange("p (i e) -> p i e", i=NT)
                    first_max(el, EPG, cst("down8"), t2, h2)
                    V.tensor_tensor(rv(656, 4), t2, t1, ALU.subtract).then_inc(exp_in, 1)
                    dve.wait_ge(exp_done, 2)
                    link(V.tensor_reduce(rv(144, 4), gexp, AX.X, ALU.add))
                    link(V.scalar_tensor_tensor(rv(144, 4), rv(656, 4), 1.0, rv(144, 4), ALU.add, ALU.mult))
                    W2 = WT[:, :].rearrange("p (i j) -> p i j", j=2)
                    link(V.reciprocal(W2[:, :, 0], rv(144, 4)))
                    link(V.tensor_tensor(W2[:, :, 1], W2[:, :, 0], rv(656, 4), ALU.mult))
                    O1 = rv(396, 128).rearrange("p (i g e) -> p i g e", i=NT, g=GROUPS)
                    O2 = rv(164, 128).rearrange("p (i g e) -> p i g e", i=NT, g=GROUPS)
                    for i in range(NT):
                        gh = ghot[:, i, :, None].to_broadcast([P, GROUPS, EPG])
                        link(V.tensor_tensor(O1[:, i], gh, h1[:, i, None, :].to_broadcast([P, GROUPS, EPG]), ALU.mult))
                        link(V.tensor_tensor(O2[:, i], gh, h2[:, i, None, :].to_broadcast([P, GROUPS, EPG]), ALU.mult))
                    V.tensor_tensor(rv(0, 128), rv(396, 128), rv(164, 128), ALU.add).then_inc(chosen, 1)
                    dve.wait_ge(ranks, 1)
                    cnt, ov = PS[1][:, NT * NE:(NT + 1) * NE], rv(524, 32)
                    link(V.tensor_scalar(ov, cnt, CAP + 0.5, None, ALU.is_ge))
                    for b in range(2, -(-SEQ // CAP)):
                        link(V.scalar_tensor_tensor(ov, cnt, b * CAP + 0.5, ov, ALU.is_ge, ALU.add))
                    ends = rv(556, 32)
                    link(V.tensor_tensor_scan(ends, CFs[:, CF["ones"][0]:CF["ones"][0] + NE], ov, 0.0, ALU.mult, ALU.add))
                    hop = rv(588, 32)
                    link(V.tensor_tensor(hop, ends, ov, ALU.subtract))
                    link(V.scalar_tensor_tensor(hop, hop, float(CAP), cst("hop"), ALU.mult, ALU.add))
                    cmp = XSb[:, 0:NOV * NE].rearrange("p (b e) -> p b e", b=NOV)
                    link(V.tensor_tensor(cmp, ends[:, None, :].to_broadcast([P, NOV, NE]),
                                         cst("blocks")[:, :, None].to_broadcast([P, NOV, NE]), ALU.is_le))
                    link(V.tensor_reduce(rv(620, NOV), cmp, AX.X, ALU.add))
                    link(V.tensor_copy(OVI[:, 0:NOV], rv(620, NOV)))
                    link(V.tensor_copy(OVI[:, NOV:NOV + 1], ends[:, NE - 1:NE]))
                    rk = PS[1][:, 0:NT * NE].rearrange("p (i e) -> p i e", i=NT)
                    sl = rv(0, 128).rearrange("p (i e) -> p i e", i=NT)
                    wide = [P, NT, NE]
                    link(V.tensor_scalar(sl, rk, CAP - 0.5, None, ALU.is_ge))
                    link(V.tensor_tensor(sl, sl, hop[:, None, :].to_broadcast(wide), ALU.mult))
                    link(V.tensor_tensor(sl, sl, rk, ALU.add))
                    link(V.tensor_tensor(sl, sl, cst("slot0")[:, None, :].to_broadcast(wide), ALU.add))
                    for j, o in enumerate((rv(396, 128), rv(164, 128))):
                        link(V.tensor_tensor(o, o, rv(0, 128), ALU.mult))
                        link(V.tensor_reduce(rv(144 + 4 * j, 4), o.rearrange("p (i e) -> p i e", i=NT), AX.X, ALU.add))
                        link(V.tensor_copy(IDX[:, 4 * j:4 * j + 4], rv(144 + 4 * j, 4)))
                    dve.sem_inc(route_in, 1)
                    dve.sem_inc(routed, 1)

                    def copy_rows(done):
                        V.tensor_copy(XT.rearrange("p (t k) s -> p t (k s)", t=2), half_banks(0)).then_inc(done, 1)

                    def hide(done):
                        V.tensor_tensor(HT, HS, PS[3][:, 0:KF * CAP], ALU.mult).then_inc(done, 1)

                    dve.wait_ge(xt_ps, 1)
                    copy_rows(xt_copied)
                    dve.sem_inc(y2_copied, 1)
                    for h in range(2):
                        dve.sem_inc(y2_stored[h], 16)
                    with dve.Fori(0, NE // 2) as i:
                        for h in range(2):
                            e = 2 * i + h
                            dve.wait_ge(up_ps, e + 1)
                            dve.wait_ge(gated, e + 1)
                            hide(hidden)
                            dve.wait_ge(xt_ps, e + 2)
                            copy_rows(xt_copied)
                            dve.wait_ge(rows_ps, e + 2)
                            dve.wait_ge(y2_stored[h], 16 * (i + 1))
                            V.tensor_copy(YS[h][0:CAP, :], PSALL[0:CAP, 6 * BN:8 * BN]).then_inc(y2_copied, 1)
                    nov = dve.value_load(OVI[0:1, NOV:NOV + 1], min_val=0, max_val=NOV)
                    with dve.If(nov > 0):
                        dve.wait_ge(y2_stored[0], 16 * (NE // 2 + 1))
                        with dve.Fori(0, nov) as j:
                            dve.wait_ge(ov_turn, j + 1)
                            copy_rows(ov_turned)
                            dve.wait_ge(ov_silu, j + 1)
                            hide(ov_hid)
                            dve.wait_ge(ov_rows, j + 1)
                            V.tensor_copy(YS[0][0:CAP, :], PSALL[0:CAP, 6 * BN:8 * BN]).then_inc(ov_out, 1)
                    for n in range(8):
                        i, j = divmod(n, 2)
                        dve.wait_ge(gathered[n], 16 * (layer + 1))
                        ins = V.scalar_tensor_tensor(X3[:, i, :], YG[n], WT[:, n:n + 1], X3[:, i, :], ALU.mult, ALU.add)
                        ins.then_inc(combined, 1)
                        dve.wait_ge(combined, n + 1)

                @block.gpsimd
                def _(pool):
                    G = nc.gpsimd
                    done = [0]

                    def link(ins):
                        done[0] += 1
                        ins.then_inc(gp, 1)
                        pool.wait_ge(gp, done[0])

                    def rope(m, scratch, heads, half):
                        t = QKV[m].rearrange("p i (g n) -> p i g n", g=heads)
                        a1, a2 = t[:, :, :, 0:half], t[:, :, :, half:2 * half]
                        shp = [P, NT, heads, half]
                        cos, sin = (cst(f + m).rearrange("p (i n) -> p i n", i=NT)[:, :, None, :].to_broadcast(shp) for f in ("cos", "sin"))
                        w = [view(RING, scratch + q * 256, 256, "p (i g n) -> p i g n", i=NT, g=heads) for q in range(4)]
                        G.tensor_tensor(w[0], a1, cos, ALU.mult)
                        G.tensor_tensor(w[1], a2, sin, ALU.mult)
                        G.tensor_tensor(w[2], a2, cos, ALU.mult)
                        link(G.tensor_tensor(w[3], a1, sin, ALU.mult))
                        G.tensor_tensor(a1, w[0], w[1], ALU.subtract).then_inc(roped[m], 1)
                        G.tensor_tensor(a2, w[2], w[3], ALU.add).then_inc(roped[m], 1)

                    pool.wait_ge(proj_copied, copied("t", (0, NT - 1)))
                    rope("A", SC0 + 10112, 8, 8)
                    eye = cst("ident")[:, None, :].to_broadcast([P, 8, P])
                    for buf in (DB, EB):
                        G.tensor_copy(buf, eye).then_inc(mix["A"]["eye"], 1)
                    pool.wait_ge(proj_copied, copied("t", (3, NT - 1)))
                    pool.wait_ge(sgu_ps, 1)
                    rope("D", SC0 + 11136, 16, 4)
                    pool.wait_ge(mix["A"]["y_ps"], 4)
                    for buf in (DB, EB):
                        G.tensor_copy(buf, eye).then_inc(mix["D"]["eye"], 1)
                    pool.wait_ge(routed, 1)
                    pool.wait_ge(n2_scaled, 4)
                    pool.wait_ge(slots_zeroed, 16 * ZEROING)
                    for n in range(8):
                        i, j = n // 2, n % 2
                        pool.indirect_dma_start(xslots[:, :], bass.IndirectOffsetOnAxis(ap=IDX[:, 4 * j + i:4 * j + i + 1], axis=0),
                                                XN2[:, i, :], None).then_inc(scattered, 16)
                    pool.wait_ge(scattered, 128 * (layer + 1))
                    pool.sem_inc(rows_sent, 1)
                    for h in range(2):
                        pool.wait_ge(y2_stored[h], 16 * (NE // 2 + 1))
                    pool.wait_ge(xt_copied, NE + 1)
                    pool.wait_ge(ov_end, 1)
                    for n in range(8):
                        i, j = divmod(n, 2)
                        pool.indirect_dma_start(YG[n], None, yslots[:, :],
                                                bass.IndirectOffsetOnAxis(ap=IDX[:, 4 * j + i:4 * j + i + 1], axis=0)).then_inc(gathered[n], 16)

            lo, hi = min(s.num for s in sems), max(s.num for s in sems)
            nc.all_engine_barrier(sems_to_clear=range(lo, hi + 1))

        of_layer.close()

        fin_in, fin_sq, fin_vec, fin_done, fin_out = (ctx.enter_context(nc.semaphore(n)) for n in
                                                      ("fin_g", "fin_squares", "fin_vec", "fin_done", "fin_out"))
        OUTB = view(TOK, 0, 4096, "p (i d) -> p i d", i=NT)
        with nc.Block() as block:
            @block.sync
            def _(sp):
                sp.dma_start(G2ROW, final_g.rearrange("(a n) -> a n", a=1).to_broadcast([P, D])).then_inc(fin_in, 16)
                for i in range(NT):
                    sp.wait_ge(fin_done, i + 1)
                    sp.dma_start(out[0, i * P:(i + 1) * P, :], OUTB[:, i, :]).then_inc(fin_out, 16)
                sp.wait_ge(fin_out, 16 * NT)

            @block.scalar
            def _(act):
                for i in range(NT):
                    nc.scalar.activation(XNTb[:, i * D:(i + 1) * D], X3[:, i, :], ACT.Square, accum_out=ss1[:, i:i + 1]).then_inc(fin_sq, 1)
                act.wait_ge(fin_vec, 1)
                nc.scalar.activation(rs1, rs1, ACT.Sqrt).then_inc(fin_sq, 1)

            @block.vector
            def _(dve):
                dve.wait_ge(fin_sq, NT)
                nc.vector.tensor_scalar(rs1, ss1, 1.0 / D, RMS_EPS, ALU.mult, ALU.add).then_inc(fin_vec, 1)
                dve.wait_ge(fin_sq, NT + 1)
                nc.vector.reciprocal(rs1, rs1).then_inc(fin_vec, 1)
                dve.wait_ge(fin_vec, 2)
                dve.wait_ge(fin_in, 16)
                for i in range(NT):
                    nc.vector.scalar_tensor_tensor(OUTB[:, i, :], X3[:, i, :], rs1[:, i:i + 1], G2ROW, ALU.mult, ALU.mult).then_inc(fin_done, 1)


def constants():
    t = np.arange(P)
    cf = np.zeros((P, NCF), np.float32)

    def put(name, a):
        lo, n = CF[name]
        cf[:, lo:lo + n] = a

    before, upto = t[:, None] < t[None, :], t[:, None] <= t[None, :]
    put("ident", np.eye(P))
    put("causal", np.where(t[None, :] <= t[:, None], 0.0, NEG))
    put("unit", np.concatenate([before, upto, before, upto], 1))
    put("head", t[:, None] // HD == t[None, :] // HD)
    put("ones", 1.0)
    for m, rot in (("A", HD // 4), ("D", HD // 8)):
        inv = (np.float32(500000.0) ** (-np.arange(0, rot, 2, dtype=np.float32) / np.float32(rot))).astype(np.float32)
        ang = (np.arange(SEQ, dtype=np.float32)[:, None] * inv[None, :]).astype(np.float32).astype(np.float64)
        for f, fn in (("cos", np.cos), ("sin", np.sin)):
            put(f + m, fn(ang).reshape(NT, P, rot // 2).transpose(1, 0, 2).reshape(P, -1))
    put("down4", np.arange(GROUPS, 0, -1))
    put("down8", np.arange(EPG, 0, -1))
    put("slot0", np.arange(NE) * CAP)
    put("hop", (NE - 1 - np.arange(NE)) * CAP)
    put("blocks", np.arange(NOV))
    cm = np.zeros((P, 14 * P), np.float32)
    for n, b in enumerate(LEVELS):
        i, j = t[:, None], t[None, :]
        low = (i // (2 * b) == j // (2 * b)) & ((i // b) % 2 == 1) & ((j // b) % 2 == 0)
        cm[:, n * P:(n + 1) * P] = low
        cm[:, (7 + n) * P:(8 + n) * P] = low.T
    return cf, cm


def kernel(x, norm1_g, w_in, rwkv_mu, rwkv_w0, rwkv_w2, rwkv_a0, rwkv_a2, rwkv_g2, rwkv_kk, rwkv_ka, rwkv_rk,
           rwkv_ln_g, rwkv_ln_b, sgu_ln_g, sgu_ln_b, sgu_w, sgu_b, diff_lq1, diff_lk1, diff_lq2, diff_lk2,
           diff_subln_g, w_out, norm2_g, router_group_w, router_group_b, router_expert_w, router_expert_b,
           moe_w_gate, moe_w_up, moe_w_down, final_g):
    import concourse.bacc as bacc
    from concourse.bass_utils import run_bass_kernel_spmd

    L = DEPTH
    b0 = 3 * GW
    wd0, k0 = b0 + 256, b0 + 320
    v0, ad0, gd0 = k0 + 256, k0 + 512, k0 + 576
    c0, d0 = b0 + 1024, b0 + 1536
    rng = lambda a, n: list(range(a, a + n))
    tiles = [rng(wd0, 64) + rng(ad0, 64), rng(k0, 128), rng(k0 + 128, 128), rng(v0, 128),
             rng(v0 + 128, 128), rng(gd0, 128), rng(b0, 128), rng(b0 + 128, 128)]
    blocks = [sum(tiles[:4], []), sum(tiles[4:], []), rng(0, 512), rng(512, 256) + rng(d0 + 512, 256),
              rng(c0, 512), rng(d0, 512)]

    def slots(w, cols):
        parts = [np.asarray(w)[:, :, c].reshape(L, KD, P, len(c)).transpose(0, 2, 1, 3).reshape(L, P, -1) for c in cols]
        return np.ascontiguousarray(np.stack(parts, 1))

    def per_channel(a, n):
        return np.asarray(a).reshape(L, n, P).transpose(0, 2, 1)

    mu = np.asarray(rwkv_mu)[:, np.array(sum(tiles, [])) - b0]
    pcol = np.concatenate([per_channel(norm1_g, KD), per_channel(mu, 8)]
                          + [per_channel(a, 2) for a in (rwkv_w0, rwkv_a0, rwkv_kk, rwkv_ka, rwkv_rk, rwkv_ln_g, rwkv_ln_b)]
                          + [np.asarray(sgu_b).transpose(0, 2, 1)], 2)
    lam = np.array([0.8 - 0.6 * math.exp(-0.3 * l) for l in range(L)])
    prow = np.concatenate([np.asarray(a) for a in (sgu_ln_g, sgu_ln_b, diff_subln_g, diff_lq1, diff_lk1, diff_lq2, diff_lk2)]
                          + [np.stack([lam, 1 - lam], 1).astype(np.float32), np.asarray(router_group_b), np.asarray(router_expert_b)], 1)
    router = np.concatenate([np.asarray(router_group_w), np.asarray(router_expert_w)], 2)
    cf, cm = constants()
    arrays = {
        "x": np.asarray(x), "w_in_blocks": slots(w_in, blocks), "w_out_blocks": slots(w_out, [rng(0, 512), rng(512, 512)]),
        "channel_params": pcol, "row_params": prow,
        "w2_a2": np.concatenate([np.asarray(rwkv_w2), np.asarray(rwkv_a2)], 1), "g2": np.asarray(rwkv_g2),
        "sgu_w_turned": np.asarray(sgu_w).transpose(0, 3, 1, 2),
        "router": router.reshape(L, KD, P, NR).transpose(0, 2, 1, 3).reshape(L, P, KD * NR),
        "norm2_g": np.asarray(norm2_g), "w_gate": np.asarray(moe_w_gate), "w_up": np.asarray(moe_w_up),
        "w_down": np.asarray(moe_w_down), "final_g": np.asarray(final_g), "cf": cf, "cm": cm,
    }
    arrays = {k: np.ascontiguousarray(v) for k, v in arrays.items()}
    nc = bacc.Bacc("TRN2", target_bir_lowering=False, num_devices=1)
    args = [nc.dram_tensor(f"in_{k}", a.shape, mybir.dt.from_np(a.dtype), kind="ExternalInput").ap() for k, a in arrays.items()]
    out = nc.dram_tensor("out_dram", (1, SEQ, D), F32, kind="ExternalOutput").ap()
    build(nc, *args, out)
    r = run_bass_kernel_spmd(nc, [{f"in_{k}": a for k, a in arrays.items()}], core_ids=[0])
    return r.results[0]["out_dram"]
```

```python
import math
from contextlib import ExitStack

import concourse.bass as bass
from concourse import mybir
import numpy as np

F32 = mybir.dt.float32
I32 = mybir.dt.int32
U8 = mybir.dt.uint8
ALU = mybir.AluOpType
ACT = mybir.ActivationFunctionType
AX = mybir.AxisListType

P = 128
SEQ, D, DEPTH = 512, 1024, 2
NT = SEQ // P
KD = D // P
HEADS, HD, GW = 4, 64, 256
NE, GROUPS, EPG, FF = 32, 4, 8, 512
KF = FF // P
CAP = 80
NOV = (2 * SEQ - NE) // CAP
ROWS = (NE + NOV) * CAP
ZB_N = 4
ZEROING = -(-(NE + NOV) // ZB_N) + -(-NOV // ZB_N)
NR = GROUPS + NE
BN = 512
NEG = -1.0e30
RMS_EPS, SUBLN_EPS, LN_EPS, RWKV_LN_EPS = 1e-6, 1e-5, 1e-5, 64e-5
LOG_DECAY = -math.exp(-0.5)
WARM = 24
UNITS_PER_STEP = [1] * 15 + [2, 1] * 3 + [1] * 12 + [0] * 2
LEVELS = [1, 2, 4, 8, 16, 32, 64]


def layout(fields):
    at, out = 0, {}
    for name, n in fields:
        out[name] = (at, n)
        at += n
    return out, at


CF, NCF = layout([("ident", P), ("causal", P), ("unit", 4 * P), ("head", P), ("ones", P),
                  ("cosA", NT * 8), ("sinA", NT * 8), ("cosD", NT * 4), ("sinD", NT * 4),
                  ("down4", GROUPS), ("down8", EPG), ("slot0", NE), ("hop", NE), ("blocks", NOV)])
PC, NPC = layout([("g1", KD), ("mu", 8), ("w0", 2), ("a0", 2), ("kk", 2), ("ka", 2), ("rk", 2),
                  ("lng", 2), ("lnb", 2), ("sgub", HEADS), ("g2", KD)])
PR, NPR = layout([("sgug", GW), ("sgub", GW), ("subln", HD), ("lq1", 32), ("lk1", 32), ("lq2", 32),
                  ("lk2", 32), ("lam", 1), ("oml", 1), ("rb", NR)])


def build(nc, x, w_in, w_out, pcol, prow, w2a2, g2, sguT, router, norm2_g, w_gate, w_up, w_down,
          final_g, cf, cm, out):
    ctx, of_layer = ExitStack(), ExitStack()
    with ctx:
        def sb(name, n, dt=F32):
            return ctx.enter_context(nc.sbuf_tensor(name, [P, n], dt))

        def view(t, lo, n, pat=None, **kw):
            v = t[:, lo:lo + n]
            return v.rearrange(pat, **kw) if pat else v

        sems = []

        def sem(name):
            sems.append(of_layer.enter_context(nc.semaphore(name)))
            return sems[-1]

        X = sb("X", NT * D)
        XNTb = sb("XNT", KD * SEQ)
        RING = sb("RING", 6 * 4096)
        TOK = sb("TOK", 4 * 2048)
        XSb = sb("XS", 8 * SEQ)
        SC = sb("SCAN", 4096)
        CFs = sb("CF", NCF)
        CMs = sb("CM", 14 * P, U8)
        PCs = sb("PCOL", NPC)
        PRs = sb("PROW", NPR)
        OMU = sb("OMU", 8)
        OKA = sb("OKA", 2)
        RT = sb("ROUTER", KD * NR)
        SM = sb("SMALL", 300)
        IDX = sb("IDX", 8, I32)
        WT = sb("WT", 8)
        OVI = sb("OVI", NOV + 1, I32)
        PSALL = ctx.enter_context(nc.psum_tensor("banks", [P, 8 * BN], F32))
        PS = [PSALL[:, i * BN:(i + 1) * BN] for i in range(8)]

        def half_banks(b):
            return PSALL[:, b * BN:(b + 2) * BN].rearrange("p (t n) -> p t n", t=2)[:, :, 0:4 * CAP]

        def cst(name):
            lo, n = CF[name]
            return CFs[:, lo:lo + n]

        def pc(name, i):
            return PCs[:, PC[name][0] + i:PC[name][0] + i + 1]

        def pr(name):
            lo, n = PR[name]
            return PRs[:, lo:lo + n]

        X3 = X[:, :].rearrange("p (i d) -> p i d", i=NT)
        XNT = XNTb[:, :].rearrange("p (k t) -> p k t", k=KD)
        QKT = view(XNTb, 0, 2048, "p (j t) -> p j t", j=4)
        PB = view(XNTb, 2048, 2048, "p (b m t) -> p b m t", b=2, m=2)
        MT = view(XNTb, 0, 3072, "p (j t) -> p j t", j=6)
        SLOT = [RING[:, s * 4096:(s + 1) * 4096] for s in range(6)]
        SC0 = 3 * 4096
        XN = view(RING, SC0, 4096, "p (i d) -> p i d", i=NT)
        WORK = [view(RING, SC0 + 516 * i, 516) for i in range(7)]
        UB = view(RING, SC0, 4096, "p (u n) -> p u n", u=8)
        DB = view(RING, SC0 + 4096, 1024, "p (u n) -> p u n", u=8)
        EB = view(RING, SC0 + 5120, 1024, "p (u n) -> p u n", u=8)
        MB = view(RING, SC0 + 6144, 1024, "p (u n) -> p u n", u=8)
        FIN = [view(RING, SC0 + 6144 + 512 * i, 512) for i in range(2)]
        TT = view(RING, SC0 + 7168, 1536, "p (w m n) -> p w m n", w=3, m=4)
        ZB = view(RING, SC0 + 8704, 128)
        SA = view(RING, SC0 + 8832, 128)
        ST = view(RING, SC0 + 8960, 128)
        PT = view(RING, SC0 + 9088, 1024, "p (b t) -> p b t", b=2)
        Y = view(RING, SC0 + 10112, 1024, "p (c t) -> p c t", c=2)
        W2A2 = view(RING, SC0 + 11136, 256)
        G2 = view(RING, SC0 + 11392, 256)
        SGT = view(RING, SC0 + 11648, 512, "p (h t) -> p h t", h=HEADS)
        TK = [view(TOK, b * 2048, 2048, "p (i n) -> p i n", i=NT) for b in range(4)]
        QKV = {"A": TK[0], "D": TK[2]}
        BLOCK_TO = [TK[0], TK[1], TK[3], TK[2]]
        VAD, UV = TK[1], TK[3]
        XS = XSb[:, :].rearrange("p (g t) -> p g t", g=8)
        AR = view(SC, 0, 2048, "p (c m w t) -> p c m w t", c=2, m=4, w=2)
        BT = view(SC, 2048, 1024, "p (c t) -> p c t", c=2)
        KT = view(SC, 3072, 1024, "p (c t) -> p c t", c=2)
        G2ROW = view(SC, 0, D)
        XN2 = view(TOK, 0, 4096, "p (i d) -> p i d", i=NT)
        X2T = view(XSb, 0, 4096, "p (i k t) -> p i k t", i=NT, k=KD)
        XR = [view(TOK, 4096 + b * 1024, 1024) for b in range(2)]
        XT = view(TOK, 6144, KD * CAP, "p (k s) -> p k s", k=KD)
        HS = view(XSb, 0, KF * CAP)
        HT = view(XSb, KF * CAP, KF * P, "p (k s) -> p k s", k=KF)
        YS = [view(XSb, 1280 + b * 1024, 1024) for b in range(2)]
        YG = [view(TOK, n * 1024, 1024) for n in range(8)]
        RW = view(XSb, 3328, 768)
        PICKS = view(XSb, 1024, (NT + 2) * NE)
        small_at = [0]

        def small(n):
            lo = small_at[0]
            small_at[0] += n
            assert small_at[0] <= 300
            return SM[:, lo:lo + n]

        ss1, rs1, ss2, rs2 = small(4), small(4), small(4), small(4)
        epend, enbeg, carry = small(8), small(8), small(8)
        nmx, sums, rsum = small(48), small(48), small(48)
        lamt, lamv = small(4), small(1)
        bnv, bns, srs = small(8), small(24), small(4)
        dss = small(16)
        xslots = nc.dram_tensor("x_slots", (ROWS, D), F32).ap()
        yslots = nc.dram_tensor("y_slots", (ROWS, D), F32).ap()
        xs_e = xslots.rearrange("(e s) d -> e s d", s=CAP)
        ys_e = yslots.rearrange("(e s) d -> e s d", s=CAP)
        wg_v = w_gate.rearrange("l e (p k) f -> (l e) p (k f)", p=P)
        wu_v = w_up.rearrange("l e (p k) f -> (l e) p (k f)", p=P)
        wd_v = w_down.rearrange("l e (k p) d -> (l e) p k d", p=P)

        const_in = ctx.enter_context(nc.semaphore("const_in"))
        x_in = ctx.enter_context(nc.semaphore("x_in"))
        first_norm = ctx.enter_context(nc.semaphore("first_norm"))
        slots_zeroed = ctx.enter_context(nc.semaphore("slots_zeroed"))
        zero_tile = ctx.enter_context(nc.semaphore("zero_tile"))
        masks_made = ctx.enter_context(nc.semaphore("masks_made"))

        scattered = ctx.enter_context(nc.semaphore("scattered"))
        gathered = [ctx.enter_context(nc.semaphore(f"gathered{n}")) for n in range(8)]

        with nc.Block() as block:
            @block.sync
            def _(sp):
                sp.dma_start(X3, x.rearrange("b (i p) d -> p (b i) d", p=P)).then_inc(x_in, 16)
                sp.dma_start(CFs[:, :], cf).then_inc(const_in, 16)
                sp.dma_start(SLOT[5][:, 0:14 * P], cm).then_inc(const_in, 16)
                sp.wait_ge(const_in, 32)

            @block.vector
            def _(dve):
                dve.wait_ge(const_in, 32)
                nc.vector.tensor_copy(CMs[:, :], SLOT[5][:, 0:14 * P]).then_inc(masks_made, 1)
                dve.wait_ge(first_norm, 4)
                nc.vector.tensor_scalar(rs1, ss1, 1.0 / D, RMS_EPS, ALU.mult, ALU.add).then_inc(first_norm, 1)
                dve.wait_ge(first_norm, 6)
                nc.vector.reciprocal(rs1, rs1).then_inc(first_norm, 1)

            @block.scalar
            def _(act):
                act.wait_ge(x_in, 16)
                for i in range(NT):
                    nc.scalar.activation(XNTb[:, i * D:(i + 1) * D], X3[:, i, :], ACT.Square,
                                         accum_out=ss1[:, i:i + 1]).then_inc(first_norm, 1)
                act.wait_ge(first_norm, 5)
                nc.scalar.activation(rs1, rs1, ACT.Sqrt).then_inc(first_norm, 1)

            @block.gpsimd
            def _(pool):
                nc.gpsimd.memset(XR[0], 0.0).then_inc(zero_tile, 1)

        params_in, pcol_in = sem("params_in"), sem("pcol_in")
        g2row_in = sem("g2row_in")
        slot_full = [sem(f"slot_full{s}") for s in range(6)]
        prep_done = sem("prep_done")
        n1_squares, n1_scaled = sem("n1_squares"), sem("n1_scaled")
        n1_turned = sem("n1_turned")
        n1_copied_a, n1_copied_v = sem("n1_copied_a"), sem("n1_copied_v")
        proj_ps, xs_scaled, xs_mixed, proj_copied = sem("proj_ps"), sem("xs_scaled"), sem("xs_mixed"), sem("proj_copied")
        lora_in = sem("lora_in")
        vec, gp, root_in, root_out = sem("vec"), sem("gp"), sem("root_in"), sem("root_out")
        cs_ready, exps_ready, scan_in, kk_sq = sem("cs_ready"), sem("exps_ready"), sem("scan_in"), sem("kk_sq")
        gelu_done, sgu_v, sgu_ps, sgu_w = sem("gelu_done"), sem("sgu_v"), sem("sgu_ps"), sem("sgu_w")
        roped = {m: sem(f"roped{m}") for m in "AD"}
        mix = {}
        for m in "AD":
            mix[m] = {n: sem(f"{n}{m}") for n in (
                "qk_ps", "qk_copied", "scores", "maxed", "exped", "probs", "pt_ps", "pt_copied", "o_ps", "o_done",
                "eye", "prod_ps", "prod_masked", "turn_ps", "turned", "m1_ps", "m1_copied",
                "de_ps", "de_merged", "z_ps", "z_copied", "sa_ps", "sa_copied", "y_ps", "y_copied", "s_ps", "s_done",
                "fin_in", "fin_ps", "fin_sq", "y_done") if (n, m) != ("probs", "A")}
        mixed_done, mt_ps, mt_a, mt_v = sem("mixed_done"), sem("mt_ps"), sem("mt_a"), sem("mt_v")
        res_ps, res_added = sem("res_ps"), sem("res_added")
        n2_squares, n2_scaled, n2_turned, n2_copied_a, n2_copied_v = (
            sem("n2_squares"), sem("n2_scaled"), sem("n2_turned"), sem("n2_copied_a"), sem("n2_copied_v"))
        logits, exp_in, exp_done, chosen, ranks, routed = sem("logits"), sem("exp_in"), sem("exp_done"), sem("chosen"), sem("ranks"), sem("routed")
        route_in, rt_scaled = sem("route_in"), sem("rt_scaled")
        xt_ps, xt_copied = sem("xt_ps"), sem("xt_copied")
        gate_ps, up_ps, gated, hidden = sem("gate_ps"), sem("up_ps"), sem("gated"), sem("hidden")
        pe_passed, sp_passed = sem("pe_passed"), sem("sp_passed")
        y2_ps, y2_copied, y2_stored = sem("y2_ps"), sem("y2_copied"), [sem("y2_stored0"), sem("y2_stored1")]
        ov_in, ov_turn, ov_turned, ov_gu, ov_silu, ov_hid, ov_y, ov_out, ov_st, ov_end = (
            sem(f"ov_{n}") for n in ("in", "turn", "turned", "gu", "silu", "hid", "y", "out", "st", "end"))
        combined = sem("combined")
        rows_full, rows_sent = [sem("rows_full0"), sem("rows_full1")], sem("rows_sent")
        lam_in, sgu_done = sem("lam_in"), sem("sgu_done")

        PROJ = ([("b", g) for g in range(8)] + [("t", (0, 0))] + [("l", n) for n in range(6)]
                + [("n", c) for c in range(2)] + [("t", (0, i)) for i in range(1, NT)]
                + [("t", (b, i)) for b in range(1, 4) for i in range(NT)])
        LATE = PROJ.index(("t", (1, 1)))
        bank_of = [g % 8 if g < LATE else (0, 5)[g % 2] for g in range(len(PROJ))]

        def mixer_steps():
            steps = ([("P", q) for q in range(4)] + ["T"] + [("L", n) for n in range(1, 7)] + [(part, ch) for ch in range(4) for part in "ZBS"]
                     + ["F", "G"])
            rwkv = [(c, m, step) for c, m in ((0, "A"), (1, "D")) for step in steps]
            rwkv.remove((0, "A", "G"))
            units = [(m, u) for m in "AD" for u in range(18)]
            for g in range(LATE, len(PROJ)):
                yield "proj", (g,)
                for _ in range(4 if g == LATE else 1):
                    yield "rwkv", rwkv.pop(0)
                if PROJ[g] == ("t", (2, NT - 1)):
                    yield "sgu_in", ()
                if PROJ[g] == ("t", (3, 1)):
                    yield "sgu_out", ()
            for n, step in enumerate(rwkv):
                yield "rwkv", step
                for mu in [units.pop(0) for _ in range(UNITS_PER_STEP[n])]:
                    yield "attn", mu

        def run_mixers(**do):
            for kind, args in mixer_steps():
                if kind in do:
                    do[kind](*args)

        def copied(*group):
            return PROJ.index(group) - 7

        BLOCK_USED = [4, 8] + [PROJ.index(("t", (b, NT - 1))) + 1 for b in range(4)]
        MT_OF = {0: 0, 1: 1, 4: 2, 5: 3, 6: 4, 7: 5}
        unit_of = [(i, h) for i in range(NT) for h in range(HEADS)]

        with nc.Fori(0, DEPTH) as layer:
            with nc.Block() as block:

                @block.sync
                def _(sp):
                    one = bass.ds(layer, 1)
                    sp.dma_start(PCs[:, :], pcol[one].rearrange("a p n -> p (a n)")).then_inc(pcol_in, 16)
                    for n in range(6):
                        if n >= 3:
                            sp.wait_ge(proj_ps, BLOCK_USED[n - 3])
                        sp.dma_start(SLOT[n % 3], w_in[one, n].rearrange("a p n -> p (a n)")).then_inc(slot_full[n % 3], 16)
                        if n > 0:
                            continue
                        for dst, src in ((PRs[:, :], prow[one, :].to_broadcast([P, NPR])),
                                         (W2A2, w2a2[one].rearrange("a p n -> p (a n)")),
                                         (G2, g2[one].rearrange("a p n -> p (a n)")),
                                         (SGT, sguT[one].rearrange("a p h t -> p (a h) t")),
                                         (RT[:, :], router[one].rearrange("a p n -> p (a n)"))):
                            sp.dma_start(dst, src).then_inc(params_in, 16)
                    for n in range(2):
                        sp.wait_ge(proj_ps, BLOCK_USED[n + 3])
                        sp.dma_start(SLOT[n], w_out[one, n].rearrange("a p n -> p (a n)")).then_inc(slot_full[n], 16)

                    def load(e, h, waits):
                        for m, v in enumerate((wg_v, wu_v, wd_v)):
                            s = (2 + 3 * h + m) % 6
                            sp.wait_ge(*waits[m])
                            src = v[bass.ds(layer * NE + e, 1)]
                            if m < 2:
                                sp.dma_start(SLOT[s], src.rearrange("a p n -> p (a n)")).then_inc(slot_full[s], 16)
                            else:
                                sp.dma_start(SLOT[s].rearrange("p (k d) -> p k d", k=KF),
                                             src.rearrange("a p k d -> p (a k) d")).then_inc(slot_full[s], 16)

                    load(0, 0, [(proj_ps, BLOCK_USED[5]), (mixed_done, 1), (mixed_done, 1)])
                    sp.dma_start(G2ROW, norm2_g[one, :].to_broadcast([P, D])).then_inc(g2row_in, 16)
                    load(1, 1, [(res_ps, 8), (res_ps, 8), (res_ps, 8)])
                    def load_rows(e, h):
                        sp.dma_start(XR[h][0:CAP, :], xs_e[bass.ds(e, 1)].rearrange("a s d -> s (a d)")).then_inc(rows_full[h], 16)

                    sp.wait_ge(rows_sent, 1)
                    load_rows(0, 0)
                    load_rows(1, 1)
                    with sp.Fori(1, NE // 2) as i:
                        for h in range(2):
                            e = 2 * i + h
                            sp.wait_ge(xt_ps, e - 1)
                            load_rows(e, h)
                            load(e, h, [(gate_ps, e - 1), (up_ps, 2 * e - 2), (y2_ps, e - 1)])
                    sp.wait_ge(xt_ps, NE - 1)
                    load_rows(NE, 0)
                    sp.wait_ge(routed, 3)
                    nov = sp.value_load(OVI[0:1, NOV:NOV + 1], min_val=0, max_val=NOV)
                    sp.wait_ge(y2_ps, NE - 1)
                    with sp.If(nov > 0):
                        with sp.Fori(0, nov) as j:
                            e = sp.value_load(OVI[0:1, bass.ds(j, 1)], min_val=0, max_val=NE - 1)
                            w = layer * NE + e
                            sp.dma_start(SLOT[2], wg_v[bass.ds(w, 1)].rearrange("a p n -> p (a n)")).then_inc(ov_in, 16)
                            sp.dma_start(SLOT[3], wu_v[bass.ds(w, 1)].rearrange("a p n -> p (a n)")).then_inc(ov_in, 16)
                            sp.dma_start(SLOT[4].rearrange("p (k d) -> p k d", k=KF),
                                         wd_v[bass.ds(w, 1)].rearrange("a p k d -> p (a k) d")).then_inc(ov_in, 16)
                            sp.dma_start(XR[1][0:CAP, :], xs_e[bass.ds(j + NE, 1)].rearrange("a s d -> s (a d)")).then_inc(ov_in, 16)
                            sp.wait_ge(ov_out, j + 1)
                            sp.dma_start(ys_e[bass.ds(j + NE, 1)].rearrange("a s d -> s (a d)"), YS[0][0:CAP, :]).then_inc(ov_st, 16)
                            sp.wait_ge(ov_st, 16 * (j + 1))
                            sp.sem_inc(sp_passed, 1)
                    sp.sem_inc(ov_end, 1)

                @block.tensor
                def _(pe):
                    mm, tr = nc.tensor.matmul, nc.tensor.transpose
                    ident = cst("ident")

                    for i in range(NT):
                        pe.wait_ge(n1_scaled, i + 1)
                        for k in range(KD):
                            last = tr(PS[k][:, i * P:(i + 1) * P], XN[:, i, k * P:(k + 1) * P], ident)
                            if i == NT - 1:
                                last.then_inc(n1_turned, 1)

                    def project(g):
                        kind, a = PROJ[g]
                        bank = PS[bank_of[g]]
                        before = [q for q in range(g) if bank_of[q] == bank_of[g]]
                        if before:
                            if before[-1] < 8:
                                pe.wait_ge(xs_mixed, before[-1] + 1)
                            else:
                                pe.wait_ge(proj_copied, before[-1] - 7)
                        if kind == "b":
                            n, j = g // 4, g % 4
                            if j == 0:
                                pe.wait_ge(slot_full[n], 16)
                            w = SLOT[n].rearrange("p (k n) -> p k n", k=KD)
                            for k in range(KD):
                                if g == 0:
                                    pe.wait_ge((n1_copied_a, n1_copied_v)[k % 2], k // 2 + 1)
                                last = mm(bank[:, :], w[:, k, j * P:(j + 1) * P], XNT[:, k, :], start=(k == 0), stop=(k == KD - 1))
                            last.then_inc(proj_ps, 1)
                        elif kind == "t":
                            b, i = a
                            n = b + 2
                            if i == 0:
                                pe.wait_ge(slot_full[n % 3], 16 * (n // 3 + 1))
                            w = SLOT[n % 3].rearrange("p (k n) -> p k n", k=KD)
                            for k in range(KD):
                                last = mm(bank[:, :], XNT[:, k, i * P:(i + 1) * P], w[:, k, :], start=(k == 0), stop=(k == KD - 1))
                            last.then_inc(proj_ps, 1)
                        elif kind == "n":
                            pe.wait_ge(kk_sq, a + 1)
                            mm(bank[:, :], cst("head"), WORK[5 + a][:, 0:SEQ], start=True, stop=True).then_inc(proj_ps, 1)
                        else:
                            w, c = divmod(a, 2)
                            cols = slice(c * P, (c + 1) * P)
                            if a == 0:
                                pe.wait_ge(params_in, 80)
                                pe.wait_ge(lora_in, 1)
                                pe.wait_ge(xs_mixed, 8)
                            if w == 0:
                                last = mm(bank[:, :], W2A2[0:64, cols], XS[0:64, 0, :], start=True, stop=True)
                            elif w == 1:
                                last = mm(bank[:, :], W2A2[64:128, cols], XS[64:128, 0, :], start=True, stop=True)
                            else:
                                pe.wait_ge(lora_in, 2)
                                last = mm(bank[:, :], G2[:, cols], XS[:, 5, :], start=True, stop=True)
                            last.then_inc(proj_ps, 1)

                    for g in range(LATE):
                        project(g)

                    def mix_positions():
                        pe.wait_ge(sgu_v, 1)
                        pe.wait_ge(sgu_w, 1)
                        for i in range(NT):
                            for h in range(HEADS):
                                last = mm(PS[6 + i // 2][:, (i % 2) * GW + h * HD:(i % 2) * GW + (h + 1) * HD],
                                          SGT[:, h, :], UV[:, i, GW + h * HD:GW + (h + 1) * HD], start=True, stop=True)
                        last.then_inc(sgu_ps, 1)

                    def rwkv(c, m, step):
                        s = mix[m]
                        head = lambda t, j: t[j * HD:(j + 1) * HD]
                        v = lambda ch, j: TT[:, 2, ch, j * HD:(j + 1) * HD]
                        hc = lambda j: slice(j * HD, (j + 1) * HD)
                        if step[0] == "P":
                            pe.wait_ge(scan_in, c + 1)
                            if c == 0:
                                pe.wait_ge(proj_copied, LATE - 8)
                            if c:
                                pe.wait_ge(mix["A"]["fin_in"], 4)
                            for u in range(2 * step[1], 2 * step[1] + 2):
                                ch, j = divmod(u, 2)
                                if u >= 2:
                                    pe.wait_ge(s["prod_masked"], u - 1)
                                bank, t = PS[1 + u % 2], slice(ch * P, (ch + 1) * P)
                                ar = head(AR[:, c, ch, :, :], j).rearrange("p w t -> p (w t)")
                                mm(bank[:, 0:256], head(BT[:, c, t], j), ar, start=True, stop=True)
                                mm(bank[:, 256:512], head(KT[:, c, t], j), ar, start=True, stop=True).then_inc(s["prod_ps"], 1)
                            for j in range(2 if step[1] == 3 else 0):
                                for ch in range(4):
                                    last = mm(PS[3 + j][:, ch * P:(ch + 1) * P], head(AR[:, c, ch, 0, :], j),
                                              head(BT[:, c, ch * P:(ch + 1) * P], j), start=True, stop=True)
                                last.then_inc(s["prod_ps"], 1)
                        elif step == "T":
                            pe.wait_ge(s["prod_masked"], 10)
                            for w, src in enumerate((BT[:, c, :], KT[:, c, :], XS[:, 3 + c, :])):
                                for ch in range(4):
                                    last = tr(PS[1 + w][:, ch * P:(ch + 1) * P], src[:, ch * P:(ch + 1) * P], ident)
                                last.then_inc(s["turn_ps"], 1)
                        elif step[0] == "L":
                            n = step[1]
                            for q in range(2):
                                if n == 1:
                                    pe.wait_ge(s["turned"], 3)
                                    pe.wait_ge(s["eye"], 6)
                                else:
                                    pe.wait_ge(s["de_merged"], 4 * (n - 2) + 2 * q + 2)
                                for w in range(4):
                                    u = 4 * q + w
                                    last = mm(PS[1 + q][:, w * P:(w + 1) * P], UB[:, u, 0:P], DB[:, u, :], start=True, stop=True)
                                last.then_inc(s["m1_ps"], 1)
                            for q in range(2):
                                pe.wait_ge(s["m1_copied"], 2 * (n - 1) + q + 1)
                                for side in range(2):
                                    if n == 6 and side == 0:
                                        continue
                                    if n == 6:
                                        pe.wait_ge(s["de_merged"], 20 + q)
                                    elif n > 1 or q > 0:
                                        pe.wait_ge(s["de_merged"], 4 * (n - 1) + 2 * q + side - 1)
                                    for w in range(4):
                                        u = 4 * q + w
                                        if side == 0:
                                            last = mm(PS[3][:, w * P:(w + 1) * P], EB[:, u, :], MB[:, u, :], start=True, stop=True)
                                        else:
                                            last = mm(PS[4][:, w * P:(w + 1) * P], MB[:, u, :], EB[:, u, :], start=True, stop=True)
                                    last.then_inc(s["de_ps"], 1)
                        elif step[0] == "Z":
                            ch = step[1]
                            if ch == 0:
                                pe.wait_ge(s["de_merged"], 22)
                            else:
                                pe.wait_ge(s["s_done"], ch)
                            for j in range(2):
                                last = mm(PS[1][:, hc(j)], UB[:, 2 * ch + j, 256:384], v(ch, j), start=(j == 0), stop=(ch == 0 and j == 1))
                            if ch:
                                last = mm(PS[1][:, 0:P], AR[:, c, ch, 0, :], ST, start=False, stop=True)
                            last.then_inc(s["z_ps"], 1)
                        elif step[0] == "B":
                            ch = step[1]
                            pe.wait_ge(s["z_copied"], ch + 1)
                            for j in range(2):
                                last = mm(PS[2][:, hc(j)], EB[:, 2 * ch + j, :], ZB[:, hc(j)], start=True, stop=True)
                            last.then_inc(s["sa_ps"], 1)
                        elif step[0] == "S":
                            ch = step[1]
                            pe.wait_ge(s["sa_copied"], ch + 1)
                            if ch < 3:
                                mm(PS[4][:, 0:P], TT[:, 0, ch, :], SA, start=True, stop=False)
                                last = mm(PS[4][:, 0:P], TT[:, 1, ch, :], TT[:, 2, ch, :], start=False, stop=True)
                                last.then_inc(s["s_ps"], 1)
                            if ch:
                                pe.wait_ge(s["y_copied"], ch)
                            for j in range(2):
                                u, o = 2 * ch + j, PS[3][j * HD:(j + 1) * HD, 0:P]
                                mm(o, SA[:, hc(j)], UB[:, u, 128:256], start=True, stop=False)
                                last = mm(o, v(ch, j), UB[:, u, 384:512], start=False, stop=(ch == 0))
                            if ch:
                                last = mm(PS[3][:, 0:P], ST, AR[:, c, ch, 1, :], start=False, stop=True)
                            last.then_inc(s["y_ps"], 1)
                        elif step == "F":
                            pe.wait_ge(s["y_copied"], 4)
                            mm(PS[1][:, :], cst("head"), Y[:, c, :], start=True, stop=True).then_inc(s["fin_ps"], 1)
                            pe.wait_ge(s["fin_in"], 1)
                            mm(PS[2][:, :], cst("head"), FIN[0], start=True, stop=True).then_inc(s["fin_ps"], 1)
                            pe.wait_ge(s["fin_sq"], 1)
                            mm(PS[3][:, :], cst("head"), FIN[1], start=True, stop=True).then_inc(s["fin_ps"], 1)

                    def attn(m, u):
                        s, nm = mix[m], 2 if m == "D" else 1
                        if u == 0:
                            pe.wait_ge(roped[m], 2)
                            pe.wait_ge(sgu_done, 1)
                            pe.wait_ge(proj_copied, len(PROJ) - 8)
                            for j in range(4):
                                if j >= 2:
                                    pe.wait_ge(s["qk_copied"], j - 1)
                                for i in range(NT):
                                    last = tr(PS[5 + j % 2][:, i * P:(i + 1) * P], QKV[m][:, i, j * P:(j + 1) * P], ident)
                                last.then_inc(s["qk_ps"], 1)
                            pe.wait_ge(s["qk_copied"], 4)
                        if u < 16:
                            i, h = unit_of[u]
                            w = (i + 1) * P
                            for a in range(nm):
                                n = u if m == "A" else 2 * u + a
                                if n >= 2:
                                    pe.wait_ge(s["exped"], n - 1)
                                if m == "A":
                                    rows = slice((h % 2) * 64, (h % 2) * 64 + 64)
                                else:
                                    rows = slice((h % 2) * 64 + a * 32, (h % 2) * 64 + a * 32 + 32)
                                bank = PS[5 + n % 2]
                                mm(bank[:, 0:w], QKT[rows, h // 2, i * P:w], QKT[rows, 2 + h // 2, 0:w], start=True, stop=False)
                                mm(bank[:, i * P:w], ident, cst("causal"), start=False, stop=True).then_inc(s["scores"], 1)
                        if 1 <= u <= 16:
                            i, h = unit_of[u - 1]
                            pe.wait_ge(s["exped"] if m == "A" else s["probs"], u)
                            if u >= 2:
                                pe.wait_ge(s["pt_copied"], u - 1)
                            for b in range(i + 1):
                                last = tr(PS[7][:, b * P:(b + 1) * P], PB[:, (u - 1) % 2, nm - 1, b * P:(b + 1) * P], ident)
                            last.then_inc(s["pt_ps"], 1)
                        if u >= 2:
                            n = u - 2
                            i, h = unit_of[n]
                            pe.wait_ge(s["pt_copied"], n + 1)
                            if n >= 1:
                                pe.wait_ge(s["o_done"], n)
                            elif m == "D":
                                pe.wait_ge(mix["A"]["o_done"], 16)
                            v0 = (0 if m == "A" else GW) + h * HD
                            for b in range(i + 1):
                                last = mm(PS[0][:, 0:HD], PT[:, n % 2, b * P:(b + 1) * P], VAD[:, b, v0:v0 + HD],
                                          start=(b == 0), stop=(b == i))
                            last.then_inc(s["o_ps"], 1)

                    run_mixers(proj=project, rwkv=rwkv, attn=attn, sgu_out=mix_positions)

                    def turn_outputs(j, bank, src, t):
                        for i in range(NT):
                            last = tr(PS[bank][:, i * P:(i + 1) * P], src[:, i, t * P:(t + 1) * P], ident)
                        last.then_inc(mt_ps, 1)

                    pe.wait_ge(mix["D"]["fin_in"], 4)
                    pe.wait_ge(mix["A"]["o_done"], 16)
                    for j, (src, t) in enumerate([(QKV["A"], 0), (QKV["A"], 1), (UV, 0), (UV, 1)]):
                        turn_outputs(j, 1 + j, src, t)
                    def turn_x(i):
                        pe.wait_ge(res_added, 5 + i)
                        if i >= 2:
                            pe.wait_ge(n2_copied_a, i - 1)
                            pe.wait_ge(n2_copied_v, i - 1)
                        for k in range(KD):
                            last = tr(PS[2 * (i % 2) + k // 4][:, (k % 4) * P:(k % 4 + 1) * P], X3[:, i, k * P:(k + 1) * P], ident)
                        last.then_inc(n2_turned, 1)

                    def route_logits(i):
                        rw = RT[:, :].rearrange("p (k n) -> p k n", k=KD)
                        pe.wait_ge(n2_copied_a, i + 1)
                        pe.wait_ge(n2_copied_v, i + 1)
                        pe.wait_ge(rt_scaled, 1)
                        for k in range(KD):
                            last = mm(PS[4][:, i * NR:(i + 1) * NR], X2T[:, i, k, :], rw[:, k, :], start=(k == 0), stop=(k == KD - 1))
                        last.then_inc(logits, 1)

                    for n, ks in ((0, (0, 1, 4, 5)), (0, (2, 3, 6, 7)), (1, range(KD))):
                        if n == 0 and ks[0] == 0:
                            pe.wait_ge(mt_a, 4)
                            pe.wait_ge(mix["D"]["o_done"], 16)
                        elif n == 0:
                            pe.wait_ge(mix["D"]["y_done"], 1)
                            pe.wait_ge(mixed_done, 1)
                            for t in range(2):
                                turn_outputs(4 + t, 5 + t, QKV["D"], t)
                            pe.wait_ge(mt_v, 2)
                        pe.wait_ge(slot_full[n], 48)
                        w = SLOT[n].rearrange("p (k n) -> p k n", k=KD)
                        for i in range(NT):
                            for k in ks:
                                src = Y[:, k - 2, :] if k in (2, 3) else MT[:, MT_OF[k], :]
                                last = mm(PS[4 * n + i][:, :], src[:, i * P:(i + 1) * P], w[:, k, :], start=(k == 0), stop=(k == KD - 1))
                            if ks[-1] == KD - 1:
                                last.then_inc(res_ps, 1)
                            if n == 1 and i >= 1:
                                turn_x(i - 1)
                            if n == 1 and i >= 2:
                                route_logits(i - 2)

                    turn_x(NT - 1)
                    route_logits(NT - 2)
                    route_logits(NT - 1)
                    pe.wait_ge(chosen, 1)
                    before_me = CFs[:, CF["unit"][0]:CF["unit"][0] + P]
                    for b in range(NT):
                        lo = b + 1 if b else 0
                        mm(PS[2][:, lo * NE:(NT + 1) * NE], cst("ones"), PICKS[:, (lo - b) * NE:(NT + 1 - b) * NE], start=(b == 0), stop=False)
                    mm(PS[2][:, 0:(NT + 1) * NE], before_me, PICKS[:, NE:], start=False, stop=True).then_inc(ranks, 1)
                    for n in range(WARM):
                        mm(PS[5][:, :], ident, XNT[:, n % KD, :], start=True, stop=True)

                    def turn_rows(src, done):
                        rows = src[0:CAP, :].rearrange("s (p k) -> s p k", k=KD)
                        for k in range(KD):
                            last = tr(PS[k // 4][:, (k % 4) * CAP:(k % 4 + 1) * CAP], rows[:, :, k], ident[0:CAP, 0:CAP])
                        last.then_inc(done, 1)

                    def gate_or_up(w, bank, tiles=range(KF)):
                        w = w.rearrange("p (k n) -> p k n", k=KD)
                        for f in tiles:
                            for k in range(KD):
                                last = mm(bank[:, f * CAP:(f + 1) * CAP], w[:, k, f * P:(f + 1) * P], XT[:, k, :], start=(k == 0), stop=(k == KD - 1))
                        return last

                    def down(w, tiles=range(KF)):
                        w = w.rearrange("p (k d) -> p k d", k=KF)
                        for k in tiles:
                            for n in range(2):
                                last = mm(PS[6 + n][:, :], HT[:, k, :], w[:, k, n * BN:(n + 1) * BN], start=(k == 0), stop=(k == KF - 1))
                        return last

                    full0 = (3, 3, 2, 0, 0, 0)

                    def weights(m, i, h):
                        slot = (2 + 3 * h + m) % 6
                        pe.wait_ge(slot_full[slot], 16 * (i + full0[slot] + 1))
                        return SLOT[slot]

                    def gate(i, h):
                        pe.wait_ge(xt_copied, 2 * i + h + 1)
                        gate_or_up(weights(0, i, h), PS[2]).then_inc(gate_ps, 1)

                    def expert(i, h, last=False):
                        e = 2 * i + h
                        for half in range(2):
                            gate_or_up(weights(1, i, h), PS[3 + half], (2 * half, 2 * half + 1)).then_inc(up_ps, 1)
                        if h == 0:
                            pe.wait_ge(rows_full[1], 16 * (i + 1))
                        else:
                            pe.wait_ge(rows_full[0], 16 * (i + 2))
                        pe.sem_inc(pe_passed, 1)
                        turn_rows(XR[1 - h], xt_ps)
                        pe.wait_ge(y2_copied, e + 1)
                        pe.wait_ge(hidden, 2 * e + 1)
                        down(weights(2, i, h), (0, 1))
                        pe.wait_ge(hidden, 2 * e + 2)
                        down(weights(2, i, h), (2, 3)).then_inc(y2_ps, 1)
                        if not last:
                            gate(i + h, 1 - h)

                    pe.wait_ge(route_in, 1)
                    pe.wait_ge(rows_full[0], 16)
                    turn_rows(XR[0], xt_ps)
                    gate(0, 0)
                    with pe.Fori(0, NE // 2 - 1) as i:
                        for h in range(2):
                            expert(i, h)
                    expert(NE // 2 - 1, 0)
                    expert(NE // 2 - 1, 1, last=True)
                    nov = pe.value_load(OVI[0:1, NOV:NOV + 1], min_val=0, max_val=NOV)
                    with pe.If(nov > 0):
                        pe.wait_ge(xt_copied, NE + 1)
                        pe.wait_ge(y2_copied, NE + 1)
                        with pe.Fori(0, nov) as j:
                            pe.wait_ge(ov_in, 64 * (j + 1))
                            pe.sem_inc(pe_passed, 1)
                            turn_rows(XR[1], ov_turn)
                            pe.wait_ge(ov_turned, j + 1)
                            gate_or_up(SLOT[2], PS[2])
                            gate_or_up(SLOT[3], PS[3]).then_inc(ov_gu, 1)
                            pe.wait_ge(ov_hid, j + 1)
                            down(SLOT[4]).then_inc(ov_y, 1)
                    pe.nop()

                @block.scalar
                def _(act):
                    ac = nc.scalar.activation
                    roots = [0]

                    def root(t):
                        roots[0] += 1
                        act.wait_ge(root_in, roots[0])
                        ac(t, t, ACT.Sqrt).then_inc(root_out, 1)

                    act.wait_ge(pcol_in, 16)
                    act.wait_ge(n1_scaled, 4)
                    for k in range(0, KD, 2):
                        act.wait_ge(n1_turned, k + 1)
                        ac(XNT[:, k, :], PS[k][:, :], ACT.Copy, scale=pc("g1", k)).then_inc(n1_copied_a, 1)
                    act.wait_ge(prep_done, 1)
                    for g in range(8):
                        act.wait_ge(proj_ps, g + 1)
                        ac(XS[:, g, :], PS[g][:, :], ACT.Copy, scale=OMU[:, g:g + 1]).then_inc(xs_scaled, 1)
                        if g == 0:
                            with act.If(layer < 1):
                                act.wait_ge(zero_tile, 1)
                                for rows, first in ((xs_e, 0), (ys_e, NE)):
                                    for e in range(first, NE + NOV, ZB_N):
                                        n = min(ZB_N, NE + NOV - e)
                                        act.dma_start(rows[e:e + n, :, :].rearrange("e s d -> s e d"),
                                                      XR[0][0:CAP, None, :].to_broadcast([CAP, n, D])).then_inc(slots_zeroed, 16)
                        if g == 6:
                            act.wait_ge(xs_mixed, 1)
                            ac(XS[0:64, 0, :], XS[0:64, 0, :], ACT.Tanh).then_inc(lora_in, 1)
                        if g == 7:
                            act.wait_ge(xs_mixed, 6)
                            ac(XS[:, 5, :], XS[:, 5, :], ACT.Sigmoid).then_inc(lora_in, 1)
                    def take(g):
                        kind, a = PROJ[g]
                        act.wait_ge(proj_ps, g + 1)
                        src = PS[bank_of[g]][:, :]
                        if kind == "t":
                            b, i = a
                            if b == 3 and i == 0:
                                act.wait_ge(slots_zeroed, 16 * ZEROING)
                            ac(BLOCK_TO[b][:, i, :], src, ACT.Copy).then_inc(proj_copied, 1)
                        elif kind == "n":
                            ac(WORK[5 + a][:, 0:SEQ], src, ACT.Sqrt).then_inc(proj_copied, 1)
                        else:
                            w, c = divmod(a, 2)
                            if w == 0:
                                ac(WORK[0 + c][:, 0:SEQ], src, ACT.Sigmoid, bias=pc("w0", c)).then_inc(proj_copied, 1)
                            elif w == 1:
                                ac(WORK[2 + c][:, 0:SEQ], src, ACT.Sigmoid, bias=pc("a0", c)).then_inc(proj_copied, 1)
                            else:
                                ac(XS[:, (0, 5)[c], :], src, ACT.Copy).then_inc(proj_copied, 1)

                    def decays(c):
                        act.wait_ge(cs_ready, c + 1)
                        if c:
                            act.wait_ge(scan_in, 1)
                        ac(WORK[4], WORK[0], ACT.Exp).then_inc(exps_ready, 1)
                        ac(WORK[2], WORK[0], ACT.Exp, scale=-1.0).then_inc(exps_ready, 1)

                    for g in range(8, LATE):
                        take(g)
                        if PROJ[g] == ("t", (0, 1)):
                            decays(0)
                        if PROJ[g] == ("t", (1, 0)):
                            decays(1)

                    def gelus():
                        act.wait_ge(lam_in, 1)
                        ac(lamt[:, 0:2], lamt[:, 0:2], ACT.Exp).then_inc(lam_in, 1)
                        act.wait_ge(proj_copied, copied("t", (2, NT - 1)))
                        for t in range(2):
                            ac(UV[:, 2 * t:2 * t + 2, :], UV[:, 2 * t:2 * t + 2, :], ACT.Gelu).then_inc(gelu_done, 1)
                        root(srs)

                    def rwkv(c, m, step):
                        s = mix[m]
                        if step == "T":
                            for w in range(3):
                                act.wait_ge(s["turn_ps"], w + 1)
                                ac(TT[:, w, :, :].rearrange("p m n -> p (m n)"), PS[1 + w][:, :], ACT.Copy).then_inc(s["turned"], 1)
                        elif step[0] == "L":
                            for q in range(2):
                                act.wait_ge(s["m1_ps"], 2 * (step[1] - 1) + q + 1)
                                if step[1] == 1 and c:
                                    act.wait_ge(mix["A"]["y_done"], 1)
                                if step[1] > 1:
                                    act.wait_ge(s["de_ps"], 4 * (step[1] - 2) + 2 * q + 2)
                                ac(MB[:, 4 * q:4 * q + 4, :].rearrange("p u n -> p (u n)"), PS[1 + q][:, :], ACT.Copy).then_inc(s["m1_copied"], 1)
                        elif step[0] == "Z":
                            ch = step[1]
                            act.wait_ge(s["z_ps"], ch + 1)
                            ac(ZB, PS[1][:, 0:P], ACT.Copy).then_inc(s["z_copied"], 1)
                        elif step[0] == "S":
                            ch = step[1]
                            act.wait_ge(s["y_ps"], ch + 1)
                            act.wait_ge(roped["A"], 2)
                            ac(Y[:, c, ch * P:(ch + 1) * P], PS[3][:, 0:P], ACT.Copy).then_inc(s["y_copied"], 1)
                        elif step == "F":
                            act.wait_ge(s["fin_in"], 2)
                            ac(FIN[1], Y[:, c, :], ACT.Square).then_inc(s["fin_sq"], 1)
                            root(FIN[1])

                    def attn(m, u):
                        s, nm = mix[m], 2 if m == "D" else 1
                        if u == 0:
                            scale = float(HD) ** -0.5 if m == "A" else 32.0 ** -0.5
                            for j in range(4):
                                act.wait_ge(s["qk_ps"], j + 1)
                                ac(QKT[:, j, :], PS[5 + j % 2][:, :], ACT.Copy, scale=scale if j < 2 else 1.0).then_inc(s["qk_copied"], 1)
                        if u < 16:
                            i, h = unit_of[u]
                            w = (i + 1) * P
                            if u >= 2:
                                act.wait_ge(s["pt_ps"], u - 1)
                            for a in range(nm):
                                n = nm * u + a
                                col = (0 if m == "A" else 16) + n
                                act.wait_ge(s["maxed"], n + 1)
                                ac(PB[:, u % 2, a, 0:w], PS[5 + n % 2][:, 0:w], ACT.Exp, bias=nmx[:, col:col + 1],
                                   accum_out=sums[:, col:col + 1]).then_inc(s["exped"], 1)
                        if 1 <= u <= 16:
                            i, h = unit_of[u - 1]
                            w = (i + 1) * P
                            act.wait_ge(s["pt_ps"], u)
                            if u >= 3:
                                act.wait_ge(s["o_ps"], u - 2)
                            ac(PT[:, (u - 1) % 2, 0:w], PS[7][:, 0:w], ACT.Copy).then_inc(s["pt_copied"], 1)

                    run_mixers(proj=take, rwkv=rwkv, attn=attn, sgu_in=gelus)
                    for j in range(4):
                        act.wait_ge(mt_ps, j + 1)
                        ac(MT[:, j, :], PS[1 + j][:, :], ACT.Copy).then_inc(mt_a, 1)
                    root(dss)
                    def copy_x(i):
                        act.wait_ge(n2_turned, i + 1)
                        ac(X2T[:, i, 0:4, :].rearrange("p k t -> p (k t)"), PS[2 * (i % 2)][:, :], ACT.Copy).then_inc(n2_copied_a, 1)

                    for i in range(NT):
                        act.wait_ge(res_added, 5 + i)
                        ac(TOK[:, i * D:(i + 1) * D], X3[:, i, :], ACT.Square, accum_out=ss2[:, i:i + 1]).then_inc(n2_squares, 1)
                        if i:
                            copy_x(i - 1)
                        root(rs2[:, i:i + 1])
                    copy_x(NT - 1)
                    act.wait_ge(exp_in, 1)
                    ac(RW[:, 640:640 + 16], RW[:, 640:640 + 16], ACT.Exp).then_inc(exp_done, 1)
                    act.wait_ge(exp_in, 2)
                    ac(RW[:, 656:660], RW[:, 656:660], ACT.Exp).then_inc(exp_done, 1)

                    with act.Fori(0, NE // 2) as i:
                        for h in range(2):
                            e = 2 * i + h
                            act.wait_ge(gate_ps, e + 1)
                            ac(HS, PS[2][:, 0:KF * CAP], ACT.Silu).then_inc(gated, 1)
                            act.wait_ge(y2_copied, e + 2)
                            act.dma_start(ys_e[bass.ds(e, 1)].rearrange("a s d -> s (a d)"), YS[h][0:CAP, :]).then_inc(y2_stored[h], 16)
                    nov = act.value_load(OVI[0:1, NOV:NOV + 1], min_val=0, max_val=NOV)
                    with act.If(nov > 0):
                        with act.Fori(0, nov) as j:
                            act.wait_ge(ov_gu, j + 1)
                            ac(HS, PS[2][:, 0:KF * CAP], ACT.Silu).then_inc(ov_silu, 1)
                    for i in range(NT):
                        act.wait_ge(combined, 2 * i + 2)
                        ac(XNTb[:, i * D:(i + 1) * D], X3[:, i, :], ACT.Square, accum_out=ss1[:, i:i + 1]).then_inc(n1_squares, 1)
                    root(rs1)

                @block.vector
                def _(dve):
                    V = nc.vector
                    count, roots = [0], [0]

                    def link(ins):
                        count[0] += 1
                        ins.then_inc(vec, 1)
                        dve.wait_ge(vec, count[0])

                    def root(out, ss, scale, eps):
                        V.tensor_scalar(out, ss, scale, eps, ALU.mult, ALU.add).then_inc(root_in, 1)
                        roots[0] += 1
                        dve.wait_ge(root_out, roots[0])

                    def rstd(out, ss, scale, eps):
                        root(out, ss, scale, eps)
                        link(V.reciprocal(out, out))

                    for i in range(NT):
                        V.tensor_scalar(XN[:, i, :], X3[:, i, :], rs1[:, i:i + 1], None, ALU.mult).then_inc(n1_scaled, 1)
                    dve.wait_ge(pcol_in, 16)
                    link(V.tensor_scalar(OMU[:, :], PCs[:, PC["mu"][0]:PC["mu"][0] + 8], -1.0, 1.0, ALU.mult, ALU.add))
                    V.tensor_scalar(OKA[:, :], PCs[:, PC["ka"][0]:PC["ka"][0] + 2], -1.0, 1.0, ALU.mult, ALU.add).then_inc(prep_done, 1)
                    for k in range(1, KD, 2):
                        dve.wait_ge(n1_turned, k + 1)
                        V.tensor_scalar(XNT[:, k, :], PS[k][:, :], pc("g1", k), None, ALU.mult).then_inc(n1_copied_v, 1)
                    dve.wait_ge(params_in, 80)
                    V.tensor_tensor(SGT, SGT, CFs[:, CF["unit"][0] + P:CF["unit"][0] + 2 * P][:, None, :].to_broadcast([P, HEADS, P]),
                                    ALU.mult).then_inc(sgu_w, 1)
                    lt = SA[:, 0:64]
                    link(V.tensor_tensor(lt[:, 0:32], pr("lq1"), pr("lk1"), ALU.mult))
                    link(V.tensor_tensor(lt[:, 32:64], pr("lq2"), pr("lk2"), ALU.mult))
                    V.tensor_reduce(lamt[:, 0:2], lt.rearrange("p (a n) -> p a n", a=2), AX.X, ALU.add).then_inc(lam_in, 1)
                    for g in range(8):
                        dve.wait_ge(xs_scaled, g + 1)
                        V.scalar_tensor_tensor(XS[:, g, 1:], PS[g][:, 0:SEQ - 1], pc("mu", g), XS[:, g, 1:], ALU.mult, ALU.add).then_inc(xs_mixed, 1)
                    dve.wait_ge(xs_mixed, 8)
                    for c in range(2):
                        link(V.tensor_scalar(BT[:, c, :], XS[:, 1 + c, :], pc("kk", c), None, ALU.mult))
                        V.tensor_tensor(WORK[5 + c][:, 0:SEQ], BT[:, c, :], BT[:, c, :], ALU.mult).then_inc(kk_sq, 1)
                    for c in range(2):
                        dve.wait_ge(proj_copied, copied("n", c))
                        a, k, b = WORK[2 + c][:, 0:SEQ], XS[:, 1 + c, :], BT[:, c, :]
                        link(V.tensor_scalar(WORK[5][:, 0:SEQ], WORK[5 + c][:, 0:SEQ], 1e-12, None, ALU.max))
                        link(V.reciprocal(WORK[5][:, 0:SEQ], WORK[5][:, 0:SEQ]))
                        link(V.tensor_tensor(b, b, WORK[5][:, 0:SEQ], ALU.mult))
                        link(V.tensor_scalar(WORK[5][:, 0:SEQ], a, pc("ka", c), OKA[:, c:c + 1], ALU.mult, ALU.add))
                        link(V.tensor_tensor(k, k, WORK[5][:, 0:SEQ], ALU.mult))
                        link(V.tensor_tensor(KT[:, c, :], b, a, ALU.mult))
                        sg = WORK[0 + c][:, 0:SEQ].rearrange("p (m t) -> p m t", m=4)
                        cs = WORK[5]
                        cs3 = cs.rearrange("p (m t) -> p m t", m=4)
                        link(V.memset(cs3[:, :, 0:1], 0.0))
                        for ch in range(4):
                            link(V.tensor_tensor_scan(cs3[:, ch, 1:P + 1], cst("ones"), sg[:, ch, :], 0.0, ALU.mult, ALU.add))
                        link(V.tensor_tensor(WORK[0].rearrange("p (m t) -> p m t", m=4), cs3,
                                             cs3[:, :, 64:65].to_broadcast([P, 4, P + 1]), ALU.subtract))
                        V.tensor_scalar(WORK[0], WORK[0], LOG_DECAY, None, ALU.mult).then_inc(cs_ready, 1)
                        dve.wait_ge(exps_ready, 2 * c + 2)
                        ep = WORK[4].rearrange("p (m t) -> p m t", m=4)
                        en = WORK[2].rearrange("p (m t) -> p m t", m=4)
                        b3 = b.rearrange("p (m t) -> p m t", m=4)
                        kb3 = KT[:, c, :].rearrange("p (m t) -> p m t", m=4)
                        link(V.tensor_copy(epend[:, 4 * c:4 * c + 4], ep[:, :, P]))
                        link(V.tensor_copy(enbeg[:, 4 * c:4 * c + 4], en[:, :, 0]))
                        link(V.tensor_tensor(carry[:, 4 * c:4 * c + 3], epend[:, 4 * c:4 * c + 3], enbeg[:, 4 * c + 1:4 * c + 4], ALU.mult))
                        link(V.scalar_tensor_tensor(AR[:, c, :, 0, :], b3, -1.0, ep[:, :, 0:P], ALU.mult, ALU.mult))
                        link(V.tensor_tensor(AR[:, c, :, 1, :], XS[:, 6 + c, :].rearrange("p (m t) -> p m t", m=4), ep[:, :, 1:], ALU.mult))
                        link(V.tensor_tensor(b3, kb3, en[:, :, 1:], ALU.mult))
                        V.tensor_tensor(kb3, k.rearrange("p (m t) -> p m t", m=4), en[:, :, 1:], ALU.mult).then_inc(scan_in, 1)
                    def norm_v():
                        dve.wait_ge(gelu_done, 2)
                        for i in range(NT):
                            link(V.bn_stats(bns[:, 6 * i:6 * i + 6], UV[:, i, GW:]))
                            link(V.bn_aggr(bnv[:, 2 * i:2 * i + 2], bns[:, 6 * i:6 * i + 6]))
                        rstd(srs, bnv.rearrange("p (i t) -> p i t", t=2)[:, :, 1], 1.0, LN_EPS)
                        for i in range(NT):
                            link(V.tensor_scalar(UV[:, i, GW:], UV[:, i, GW:], bnv[:, 2 * i:2 * i + 1], srs[:, i:i + 1], ALU.subtract, ALU.mult))
                        link(V.tensor_tensor(UV[:, :, GW:], UV[:, :, GW:], pr("sgug")[:, None, :].to_broadcast([P, NT, GW]), ALU.mult))
                        V.tensor_tensor(UV[:, :, GW:], UV[:, :, GW:], pr("sgub")[:, None, :].to_broadcast([P, NT, GW]), ALU.add).then_inc(sgu_v, 1)
                        dve.wait_ge(lam_in, 2)
                        link(V.tensor_tensor(lamt[:, 2:3], lamt[:, 0:1], lamt[:, 1:2], ALU.subtract))
                        link(V.tensor_tensor(lamv, lamt[:, 2:3], pr("lam"), ALU.add))

                    def gate_u():
                        dve.wait_ge(sgu_ps, 1)
                        for h in range(HEADS):
                            for t in range(2):
                                ps = PS[6 + t][:, :].rearrange("p (i n) -> p i n", i=2)[:, :, h * HD:(h + 1) * HD]
                                u = UV[:, 2 * t:2 * t + 2, h * HD:(h + 1) * HD]
                                link(V.scalar_tensor_tensor(u, ps, pc("sgub", h), u, ALU.add, ALU.mult))
                        dve.sem_inc(sgu_done, 1)

                    def finish(c, m, part):
                        y = Y[:, c, :]
                        if part == 0:
                            dve.wait_ge(mix[m]["fin_in"], 4)
                            link(V.reciprocal(FIN[1], FIN[1]))
                        elif part == 1:
                            link(V.tensor_tensor(y, y, FIN[1], ALU.mult))
                        elif part == 2:
                            link(V.tensor_scalar(y, y, pc("lng", c), pc("lnb", c), ALU.mult, ALU.add))
                        elif part == 3:
                            link(V.tensor_tensor(y, y, FIN[0], ALU.add))
                        else:
                            link(V.tensor_tensor(y, y, XS[:, (0, 5)[c], :], ALU.mult))
                            dve.sem_inc(mix[m]["y_done"], 1)

                    def rwkv(c, m, step):
                        s = mix[m]
                        mask = lambda n, up: CMs[:, (7 * up + n) * P:(7 * up + n + 1) * P][:, None, :].to_broadcast([P, 4, P])
                        if step[0] == "P":
                            for u in range(2 * step[1], 2 * step[1] + 2):
                                dve.wait_ge(s["prod_ps"], u + 1)
                                V.tensor_tensor(UB[:, u, :], PS[1 + u % 2][:, :], cst("unit"), ALU.mult).then_inc(s["prod_masked"], 1)
                            if c:
                                for part in ((0,), (1,), (2,), (3, 4))[step[1]]:
                                    finish(0, "A", part)
                            if step[1] < 3:
                                return
                            dve.wait_ge(s["eye"], 2)
                            for j in range(2):
                                dve.wait_ge(s["prod_ps"], 9 + j)
                                V.copy_predicated(DB[:, j::2, :], mask(0, 0), PS[3 + j][:, :].rearrange("p (u n) -> p u n", u=4)).then_inc(s["prod_masked"], 1)
                            dve.wait_ge(s["prod_masked"], 10)
                            for q in range(2):
                                V.copy_predicated(EB[:, 4 * q:4 * q + 4, :], mask(0, 1), UB[:, 4 * q:4 * q + 4, 0:P]).then_inc(s["eye"], 2)
                        elif step[0] == "L":
                            n = step[1]
                            for q in range(2):
                                for side in range(2):
                                    if n == 6 and side == 0:
                                        continue
                                    done = 4 * (n - 1) + 2 * q + side + 1 if n < 6 else 21 + q
                                    dve.wait_ge(s["de_ps"], done)
                                    dst = (DB, EB)[side][:, 4 * q:4 * q + 4, :]
                                    V.copy_predicated(dst, mask(n, side), PS[3 + side][:, :].rearrange("p (u n) -> p u n", u=4)).then_inc(s["de_merged"], 1)
                        elif step[0] == "B":
                            ch = step[1]
                            dve.wait_ge(s["sa_ps"], ch + 1)
                            V.tensor_copy(SA, PS[2][:, 0:P]).then_inc(s["sa_copied"], 1)
                        elif step[0] == "S":
                            ch = step[1]
                            if ch < 3:
                                dve.wait_ge(s["s_ps"], ch + 1)
                                cc = carry[:, 4 * c + ch:4 * c + ch + 1]
                                dve.wait_ge(s["y_ps"], ch + 1)
                                t = PS[4][:, 0:P]
                                if ch:
                                    link(V.tensor_tensor(ST, t, ST, ALU.add))
                                    t = ST
                                V.scalar_tensor_tensor(ST, t, cc, cst("head"), ALU.mult, ALU.mult).then_inc(s["s_done"], 1)
                        elif step == "F":
                            y, r, k, v = Y[:, c, :], XS[:, 6 + c, :], XS[:, 1 + c, :], XS[:, 3 + c, :]
                            dve.wait_ge(s["de_ps"], 22)
                            dve.wait_ge(s["y_ps"], 4)
                            link(V.tensor_tensor(FIN[0], r, k, ALU.mult))
                            V.tensor_scalar(FIN[0], FIN[0], pc("rk", c), None, ALU.mult).then_inc(s["fin_in"], 1)
                            dve.wait_ge(s["fin_ps"], 1)
                            V.scalar_tensor_tensor(y, PS[1][:, :], -1.0 / HD, y, ALU.mult, ALU.add).then_inc(s["fin_in"], 1)
                            dve.wait_ge(s["fin_ps"], 2)
                            V.tensor_tensor(FIN[0], PS[2][:, :], v, ALU.mult).then_inc(s["fin_in"], 1)
                            dve.wait_ge(s["fin_ps"], 3)
                            root(FIN[1], PS[3][:, :], 1.0 / HD, RWKV_LN_EPS)
                            dve.sem_inc(s["fin_in"], 1)
                        elif step == "G":
                            for part in range(5):
                                finish(c, m, part)

                    def attn(m, u):
                        s, nm = mix[m], 2 if m == "D" else 1
                        base = 0 if m == "A" else 16
                        if 1 <= u <= 16:
                            i, h = unit_of[u - 1]
                            w = (i + 1) * P
                            n = nm * (u - 1)
                            dve.wait_ge(s["exped"], n + nm)
                            link(V.reciprocal(rsum[:, base + n:base + n + nm], sums[:, base + n:base + n + nm]))
                            if m == "D":
                                r2 = rsum[:, base + n + 1:base + n + 2]
                                link(V.tensor_scalar(r2, r2, lamv, -1.0, ALU.mult, ALU.mult))
                                p0, p1 = PB[:, (u - 1) % 2, 0, 0:w], PB[:, (u - 1) % 2, 1, 0:w]
                                link(V.tensor_scalar(p1, p1, r2, None, ALU.mult))
                                V.scalar_tensor_tensor(p1, p0, rsum[:, base + n:base + n + 1], p1, ALU.mult, ALU.add).then_inc(s["probs"], 1)
                        if u < 16:
                            i, h = unit_of[u]
                            w = (i + 1) * P
                            for a in range(nm):
                                n = nm * u + a
                                dve.wait_ge(s["scores"], n + 1)
                                V.tensor_reduce(nmx[:, base + n:base + n + 1], PS[5 + n % 2][:, 0:w], AX.X, ALU.max, negate=True).then_inc(s["maxed"], 1)
                        if u >= 2:
                            n = u - 2
                            i, h = unit_of[n]
                            dve.wait_ge(s["o_ps"], n + 1)
                            o = QKV[m][:, i, h * HD:(h + 1) * HD]
                            if m == "A":
                                V.tensor_scalar(o, PS[0][:, 0:HD], rsum[:, n:n + 1], None, ALU.mult).then_inc(s["o_done"], 1)
                            else:
                                V.tensor_copy(o, PS[0][:, 0:HD]).then_inc(s["o_done"], 1)

                    run_mixers(rwkv=rwkv, attn=attn, sgu_in=norm_v, sgu_out=gate_u)

                    dve.wait_ge(mix["D"]["o_done"], 16)
                    o = QKV["D"][:, :, 0:GW].rearrange("p i (h n) -> p i h n", h=HEADS)
                    sq = UB[:, 0:2, :].rearrange("p u n -> p (u n)").rearrange("p (i h n) -> p i h n", i=NT, h=HEADS)
                    for i in range(NT):
                        link(V.tensor_tensor(sq[:, i], o[:, i], o[:, i], ALU.mult))
                    link(V.tensor_reduce(dss, UB[:, 0:2, :].rearrange("p u n -> p (u n)").rearrange("p (a n) -> p a n", n=HD), AX.X, ALU.add))
                    rstd(dss, dss, 1.0 / HD, SUBLN_EPS)
                    link(V.tensor_scalar(dss, dss, pr("oml"), None, ALU.mult))
                    d3 = dss.rearrange("p (i h) -> p i h", i=NT)
                    for i in range(NT):
                        link(V.tensor_tensor(o[:, i], o[:, i], d3[:, i, :, None].to_broadcast([P, HEADS, HD]), ALU.mult))
                    for i in range(NT):
                        link(V.tensor_tensor(o[:, i], o[:, i], pr("subln")[:, None, :].to_broadcast([P, HEADS, HD]), ALU.mult))
                    dve.sem_inc(mixed_done, 1)

                    for j in range(4, 6):
                        dve.wait_ge(mt_ps, j + 1)
                        V.tensor_copy(MT[:, j, :], PS[1 + j][:, :]).then_inc(mt_v, 1)
                    def copy_x(i):
                        dve.wait_ge(n2_turned, i + 1)
                        V.tensor_copy(X2T[:, i, 4:8, :].rearrange("p k t -> p (k t)"), PS[2 * (i % 2) + 1][:, :]).then_inc(n2_copied_v, 1)

                    def scale_x(i):
                        V.scalar_tensor_tensor(XN2[:, i, :], X3[:, i, :], rs2[:, i:i + 1], G2ROW, ALU.mult, ALU.mult).then_inc(n2_scaled, 1)

                    rw = RT[:, :].rearrange("p (k n) -> p k n", k=KD)
                    V.tensor_tensor(rw, rw, PCs[:, PC["g2"][0]:PC["g2"][0] + KD][:, :, None].to_broadcast([P, KD, NR]), ALU.mult).then_inc(rt_scaled, 1)
                    for g in range(8):
                        n, i = divmod(g, 4)
                        dve.wait_ge(res_ps, g + 1)
                        xv = X3[:, i, n * BN:(n + 1) * BN]
                        V.tensor_tensor(xv, PS[g][:, :], xv, ALU.add).then_inc(res_added, 1)
                        if n:
                            if i:
                                copy_x(i - 1)
                            dve.wait_ge(n2_squares, i + 1)
                            rstd(rs2[:, i:i + 1], ss2[:, i:i + 1], 1.0 / D, RMS_EPS)
                            if i == 0:
                                dve.wait_ge(g2row_in, 16)
                            if i < NT - 1:
                                scale_x(i)
                    copy_x(NT - 1)

                    dve.wait_ge(logits, NT)
                    link(V.memset(PICKS, 0.0))
                    rv = lambda lo, n: RW[:, lo:lo + n]
                    L = rv(0, NT * NR).rearrange("p (i n) -> p i n", i=NT)
                    link(V.tensor_tensor(L, PS[4][:, 0:NT * NR].rearrange("p (i n) -> p i n", i=NT),
                                         rs2[:, :, None].to_broadcast([P, NT, NR]), ALU.mult))
                    link(V.tensor_tensor(L, L, pr("rb")[:, None, :].to_broadcast([P, NT, NR]), ALU.add))

                    def first_max(vals, n, down, top, hot):
                        t3 = top[:, :, None]
                        wide = [P, NT, n]
                        link(V.tensor_reduce(top, vals, AX.X, ALU.max))
                        link(V.tensor_tensor(hot, vals, t3.to_broadcast(wide), ALU.is_equal))
                        link(V.tensor_tensor(hot, hot, down[:, None, :].to_broadcast(wide), ALU.mult))
                        link(V.tensor_reduce(rv(760, 4), hot, AX.X, ALU.max))
                        link(V.tensor_tensor(hot, hot, rv(760, 4)[:, :, None].to_broadcast(wide), ALU.is_equal))

                    gl = L[:, :, 0:GROUPS]
                    gtop, ghot = rv(144, 4), rv(148, 16).rearrange("p (i n) -> p i n", i=NT)
                    first_max(gl, GROUPS, cst("down4"), gtop, ghot)
                    gexp = rv(640, 16).rearrange("p (i n) -> p i n", i=NT)
                    V.tensor_tensor(gexp, gl, gtop[:, :, None].to_broadcast([P, NT, GROUPS]), ALU.subtract).then_inc(exp_in, 1)
                    pg = rv(164, 128).rearrange("p (i g e) -> p i g e", i=NT, g=GROUPS)
                    every = [P, NT, GROUPS, EPG]
                    gh = ghot[:, :, :, None].to_broadcast(every)
                    link(V.tensor_tensor(pg, L[:, :, GROUPS:].rearrange("p i (g e) -> p i g e", g=GROUPS), gh, ALU.mult))
                    el = rv(292, 32).rearrange("p (i e) -> p i e", i=NT)
                    link(V.tensor_reduce(el, rv(164, 128).rearrange("p (i g e) -> p i e g", i=NT, g=GROUPS), AX.X, ALU.add))
                    t1, h1 = rv(324, 4), rv(328, 32).rearrange("p (i e) -> p i e", i=NT)
                    first_max(el, EPG, cst("down8"), t1, h1)
                    link(V.scalar_tensor_tensor(el, h1, NEG, el, ALU.mult, ALU.add))
                    t2, h2 = rv(360, 4), rv(364, 32).rearrange("p (i e) -> p i e", i=NT)
                    first_max(el, EPG, cst("down8"), t2, h2)
                    V.tensor_tensor(rv(656, 4), t2, t1, ALU.subtract).then_inc(exp_in, 1)
                    dve.wait_ge(exp_done, 2)
                    link(V.tensor_reduce(rv(144, 4), gexp, AX.X, ALU.add))
                    link(V.scalar_tensor_tensor(rv(144, 4), rv(656, 4), 1.0, rv(144, 4), ALU.add, ALU.mult))
                    W2 = WT[:, :].rearrange("p (i j) -> p i j", j=2)
                    link(V.reciprocal(W2[:, :, 0], rv(144, 4)))
                    link(V.tensor_tensor(W2[:, :, 1], W2[:, :, 0], rv(656, 4), ALU.mult))
                    O1 = rv(396, 128).rearrange("p (i g e) -> p i g e", i=NT, g=GROUPS)
                    O2 = rv(164, 128).rearrange("p (i g e) -> p i g e", i=NT, g=GROUPS)
                    link(V.tensor_tensor(O1, gh, h1[:, :, None, :].to_broadcast(every), ALU.mult))
                    link(V.tensor_tensor(O2, gh, h2[:, :, None, :].to_broadcast(every), ALU.mult))
                    V.tensor_tensor(PICKS[:, NE:(NT + 1) * NE], rv(396, 128), rv(164, 128), ALU.add).then_inc(chosen, 1)
                    scale_x(NT - 1)
                    dve.wait_ge(ranks, 1)
                    cnt, ov = PS[2][:, NT * NE:(NT + 1) * NE], rv(524, 32)
                    link(V.tensor_scalar(ov, cnt, CAP + 0.5, None, ALU.is_ge))
                    for b in range(2, -(-SEQ // CAP)):
                        link(V.scalar_tensor_tensor(ov, cnt, b * CAP + 0.5, ov, ALU.is_ge, ALU.add))
                    ends = rv(556, 32)
                    link(V.tensor_tensor_scan(ends, CFs[:, CF["ones"][0]:CF["ones"][0] + NE], ov, 0.0, ALU.mult, ALU.add))
                    hop = rv(588, 32)
                    link(V.tensor_tensor(hop, ends, ov, ALU.subtract))
                    link(V.scalar_tensor_tensor(hop, hop, float(CAP), cst("hop"), ALU.mult, ALU.add))
                    rk = PS[2][:, 0:NT * NE].rearrange("p (i e) -> p i e", i=NT)
                    sl = rv(0, 128).rearrange("p (i e) -> p i e", i=NT)
                    wide = [P, NT, NE]
                    link(V.tensor_scalar(sl, rk, CAP - 0.5, None, ALU.is_ge))
                    link(V.tensor_tensor(sl, sl, hop[:, None, :].to_broadcast(wide), ALU.mult))
                    link(V.tensor_tensor(sl, sl, rk, ALU.add))
                    link(V.tensor_tensor(sl, sl, cst("slot0")[:, None, :].to_broadcast(wide), ALU.add))
                    for j, o in enumerate((rv(396, 128), rv(164, 128))):
                        link(V.tensor_tensor(o, o, rv(0, 128), ALU.mult))
                        link(V.tensor_reduce(rv(144 + 4 * j, 4), o.rearrange("p (i e) -> p i e", i=NT), AX.X, ALU.add))
                        V.tensor_copy(IDX[:, 4 * j:4 * j + 4], rv(144 + 4 * j, 4)).then_inc(routed, 1)
                    dve.sem_inc(route_in, 1)
                    cmp = XSb[:, 0:NOV * NE].rearrange("p (b e) -> p b e", b=NOV)
                    link(V.tensor_tensor(cmp, ends[:, None, :].to_broadcast([P, NOV, NE]),
                                         cst("blocks")[:, :, None].to_broadcast([P, NOV, NE]), ALU.is_le))
                    link(V.tensor_reduce(rv(620, NOV), cmp, AX.X, ALU.add))
                    link(V.tensor_copy(OVI[:, 0:NOV], rv(620, NOV)))
                    link(V.tensor_copy(OVI[:, NOV:NOV + 1], ends[:, NE - 1:NE]))
                    dve.sem_inc(routed, 1)

                    def copy_rows(done):
                        V.tensor_copy(XT.rearrange("p (t k) s -> p t (k s)", t=2), half_banks(0)).then_inc(done, 1)

                    def hide(done, bank=3, lo=0, n=KF):
                        some = slice(lo * CAP, (lo + n) * CAP)
                        V.tensor_tensor(HT[:, lo:lo + n, 0:CAP], HS[:, some].rearrange("p (k s) -> p k s", k=n),
                                        PS[bank][:, some].rearrange("p (k s) -> p k s", k=n), ALU.mult).then_inc(done, 1)

                    link(V.memset(HT, 0.0))
                    dve.wait_ge(xt_ps, 1)
                    copy_rows(xt_copied)
                    dve.sem_inc(y2_copied, 1)
                    for h in range(2):
                        dve.sem_inc(y2_stored[h], 16)
                    with dve.Fori(0, NE // 2) as i:
                        for h in range(2):
                            e = 2 * i + h
                            dve.wait_ge(gated, e + 1)
                            for half in range(2):
                                dve.wait_ge(up_ps, 2 * e + half + 1)
                                hide(hidden, 3 + half, 2 * half, 2)
                            dve.wait_ge(xt_ps, e + 2)
                            copy_rows(xt_copied)
                            dve.wait_ge(y2_ps, e + 1)
                            dve.wait_ge(y2_stored[h], 16 * (i + 1))
                            V.tensor_copy(YS[h][0:CAP, :], PSALL[0:CAP, 6 * BN:8 * BN]).then_inc(y2_copied, 1)
                    nov = dve.value_load(OVI[0:1, NOV:NOV + 1], min_val=0, max_val=NOV)
                    with dve.If(nov > 0):
                        dve.wait_ge(y2_stored[0], 16 * (NE // 2 + 1))
                        with dve.Fori(0, nov) as j:
                            dve.wait_ge(ov_turn, j + 1)
                            copy_rows(ov_turned)
                            dve.wait_ge(ov_silu, j + 1)
                            hide(ov_hid)
                            dve.wait_ge(ov_y, j + 1)
                            V.tensor_copy(YS[0][0:CAP, :], PSALL[0:CAP, 6 * BN:8 * BN]).then_inc(ov_out, 1)
                    for n in range(8):
                        i, j = divmod(n, 2)
                        dve.wait_ge(gathered[n], 16 * (layer + 1))
                        ins = V.scalar_tensor_tensor(X3[:, i, :], YG[n], WT[:, n:n + 1], X3[:, i, :], ALU.mult, ALU.add)
                        ins.then_inc(combined, 1)
                        dve.wait_ge(combined, n + 1)
                    dve.wait_ge(n1_squares, 4)
                    rstd(rs1, ss1, 1.0 / D, RMS_EPS)

                @block.gpsimd
                def _(pool):
                    G = nc.gpsimd
                    done = [0]

                    def link(ins):
                        done[0] += 1
                        ins.then_inc(gp, 1)
                        pool.wait_ge(gp, done[0])

                    def rope(m, scratch, heads, half):
                        t = QKV[m].rearrange("p i (g n) -> p i g n", g=heads)
                        a1, a2 = t[:, :, :, 0:half], t[:, :, :, half:2 * half]
                        shp = [P, NT, heads, half]
                        cos, sin = (cst(f + m).rearrange("p (i n) -> p i n", i=NT)[:, :, None, :].to_broadcast(shp) for f in ("cos", "sin"))
                        w = [view(RING, scratch + q * 256, 256, "p (i g n) -> p i g n", i=NT, g=heads) for q in range(4)]
                        G.tensor_tensor(w[0], a1, cos, ALU.mult)
                        G.tensor_tensor(w[1], a2, sin, ALU.mult)
                        G.tensor_tensor(w[2], a2, cos, ALU.mult)
                        link(G.tensor_tensor(w[3], a1, sin, ALU.mult))
                        G.tensor_tensor(a1, w[0], w[1], ALU.subtract).then_inc(roped[m], 1)
                        G.tensor_tensor(a2, w[2], w[3], ALU.add).then_inc(roped[m], 1)

                    pool.wait_ge(proj_copied, copied("t", (0, NT - 1)))
                    rope("A", SC0 + 10112, 8, 8)
                    eye = cst("ident")[:, None, :].to_broadcast([P, 8, P])
                    for buf in (DB, EB):
                        G.tensor_copy(buf, eye).then_inc(mix["A"]["eye"], 1)
                    pool.wait_ge(proj_copied, copied("t", (3, NT - 1)))
                    pool.wait_ge(sgu_ps, 1)
                    rope("D", SC0 + 11136, 16, 4)
                    pool.wait_ge(mix["A"]["y_ps"], 4)
                    for buf in (DB, EB):
                        G.tensor_copy(buf, eye).then_inc(mix["D"]["eye"], 1)
                    pool.wait_ge(n2_scaled, 4)
                    pool.wait_ge(slots_zeroed, 16 * ZEROING)
                    for n in range(8):
                        j, i = divmod(n, NT)
                        pool.wait_ge(routed, j + 1)
                        pool.indirect_dma_start(xslots[:, :], bass.IndirectOffsetOnAxis(ap=IDX[:, 4 * j + i:4 * j + i + 1], axis=0),
                                                XN2[:, i, :], None).then_inc(scattered, 16)
                    pool.wait_ge(scattered, 128 * (layer + 1))
                    pool.sem_inc(rows_sent, 1)
                    for h in range(2):
                        pool.wait_ge(y2_stored[h], 16 * (NE // 2 + 1))
                    pool.wait_ge(xt_copied, NE + 1)
                    pool.wait_ge(ov_end, 1)
                    for n in range(8):
                        i, j = divmod(n, 2)
                        pool.indirect_dma_start(YG[n], None, yslots[:, :],
                                                bass.IndirectOffsetOnAxis(ap=IDX[:, 4 * j + i:4 * j + i + 1], axis=0)).then_inc(gathered[n], 16)

            lo, hi = min(s.num for s in sems), max(s.num for s in sems)
            nc.all_engine_barrier(sems_to_clear=range(lo, hi + 1))

        of_layer.close()

        fin_in, fin_done, fin_out = (ctx.enter_context(nc.semaphore(n)) for n in ("fin_g", "fin_done", "fin_out"))
        OUTB = view(TOK, 0, 4096, "p (i d) -> p i d", i=NT)
        with nc.Block() as block:
            @block.sync
            def _(sp):
                sp.dma_start(G2ROW, final_g.rearrange("(a n) -> a n", a=1).to_broadcast([P, D])).then_inc(fin_in, 16)
                for i in range(NT):
                    sp.wait_ge(fin_done, i + 1)
                    sp.dma_start(out[0, i * P:(i + 1) * P, :], OUTB[:, i, :]).then_inc(fin_out, 16)
                sp.wait_ge(fin_out, 16 * NT)

            @block.vector
            def _(dve):
                dve.wait_ge(fin_in, 16)
                for i in range(NT):
                    nc.vector.scalar_tensor_tensor(OUTB[:, i, :], X3[:, i, :], rs1[:, i:i + 1], G2ROW, ALU.mult, ALU.mult).then_inc(fin_done, 1)


def constants():
    t = np.arange(P)
    cf = np.zeros((P, NCF), np.float32)

    def put(name, a):
        lo, n = CF[name]
        cf[:, lo:lo + n] = a

    before, upto = t[:, None] < t[None, :], t[:, None] <= t[None, :]
    put("ident", np.eye(P))
    put("causal", np.where(t[None, :] <= t[:, None], 0.0, NEG))
    put("unit", np.concatenate([before, upto, before, upto], 1))
    put("head", t[:, None] // HD == t[None, :] // HD)
    put("ones", 1.0)
    for m, rot in (("A", HD // 4), ("D", HD // 8)):
        inv = (np.float32(500000.0) ** (-np.arange(0, rot, 2, dtype=np.float32) / np.float32(rot))).astype(np.float32)
        ang = (np.arange(SEQ, dtype=np.float32)[:, None] * inv[None, :]).astype(np.float32).astype(np.float64)
        for f, fn in (("cos", np.cos), ("sin", np.sin)):
            put(f + m, fn(ang).reshape(NT, P, rot // 2).transpose(1, 0, 2).reshape(P, -1))
    put("down4", np.arange(GROUPS, 0, -1))
    put("down8", np.arange(EPG, 0, -1))
    put("slot0", np.arange(NE) * CAP)
    put("hop", (NE - 1 - np.arange(NE)) * CAP)
    put("blocks", np.arange(NOV))
    cm = np.zeros((P, 14 * P), np.float32)
    for n, b in enumerate(LEVELS):
        i, j = t[:, None], t[None, :]
        low = (i // (2 * b) == j // (2 * b)) & ((i // b) % 2 == 1) & ((j // b) % 2 == 0)
        cm[:, n * P:(n + 1) * P] = low
        cm[:, (7 + n) * P:(8 + n) * P] = low.T
    return cf, cm


def kernel(x, norm1_g, w_in, rwkv_mu, rwkv_w0, rwkv_w2, rwkv_a0, rwkv_a2, rwkv_g2, rwkv_kk, rwkv_ka, rwkv_rk,
           rwkv_ln_g, rwkv_ln_b, sgu_ln_g, sgu_ln_b, sgu_w, sgu_b, diff_lq1, diff_lk1, diff_lq2, diff_lk2,
           diff_subln_g, w_out, norm2_g, router_group_w, router_group_b, router_expert_w, router_expert_b,
           moe_w_gate, moe_w_up, moe_w_down, final_g):
    import concourse.bacc as bacc
    from concourse.bass_utils import run_bass_kernel_spmd

    L = DEPTH
    b0 = 3 * GW
    wd0, k0 = b0 + 256, b0 + 320
    v0, ad0, gd0 = k0 + 256, k0 + 512, k0 + 576
    c0, d0 = b0 + 1024, b0 + 1536
    rng = lambda a, n: list(range(a, a + n))
    tiles = [rng(wd0, 64) + rng(ad0, 64), rng(k0, 128), rng(k0 + 128, 128), rng(v0, 128),
             rng(v0 + 128, 128), rng(gd0, 128), rng(b0, 128), rng(b0 + 128, 128)]
    blocks = [sum(tiles[:4], []), sum(tiles[4:], []), rng(0, 512), rng(512, 256) + rng(d0 + 512, 256),
              rng(c0, 512), rng(d0, 512)]

    def slots(w, cols):
        parts = [np.asarray(w)[:, :, c].reshape(L, KD, P, len(c)).transpose(0, 2, 1, 3).reshape(L, P, -1) for c in cols]
        return np.ascontiguousarray(np.stack(parts, 1))

    def per_channel(a, n):
        return np.asarray(a).reshape(L, n, P).transpose(0, 2, 1)

    mu = np.asarray(rwkv_mu)[:, np.array(sum(tiles, [])) - b0]
    pcol = np.concatenate([per_channel(norm1_g, KD), per_channel(mu, 8)]
                          + [per_channel(a, 2) for a in (rwkv_w0, rwkv_a0, rwkv_kk, rwkv_ka, rwkv_rk, rwkv_ln_g, rwkv_ln_b)]
                          + [np.asarray(sgu_b).transpose(0, 2, 1), per_channel(norm2_g, KD)], 2)
    lam = np.array([0.8 - 0.6 * math.exp(-0.3 * l) for l in range(L)])
    prow = np.concatenate([np.asarray(a) for a in (sgu_ln_g, sgu_ln_b, diff_subln_g, diff_lq1, diff_lk1, diff_lq2, diff_lk2)]
                          + [np.stack([lam, 1 - lam], 1).astype(np.float32), np.asarray(router_group_b), np.asarray(router_expert_b)], 1)
    router = np.concatenate([np.asarray(router_group_w), np.asarray(router_expert_w)], 2)
    cf, cm = constants()
    arrays = {
        "x": np.asarray(x), "w_in_blocks": slots(w_in, blocks), "w_out_blocks": slots(w_out, [rng(0, 512), rng(512, 512)]),
        "channel_params": pcol, "row_params": prow,
        "w2_a2": np.concatenate([np.asarray(rwkv_w2), np.asarray(rwkv_a2)], 1), "g2": np.asarray(rwkv_g2),
        "sgu_w_turned": np.asarray(sgu_w).transpose(0, 3, 1, 2),
        "router": router.reshape(L, KD, P, NR).transpose(0, 2, 1, 3).reshape(L, P, KD * NR),
        "norm2_g": np.asarray(norm2_g), "w_gate": np.asarray(moe_w_gate), "w_up": np.asarray(moe_w_up),
        "w_down": np.asarray(moe_w_down), "final_g": np.asarray(final_g), "cf": cf, "cm": cm,
    }
    arrays = {k: np.ascontiguousarray(v) for k, v in arrays.items()}
    nc = bacc.Bacc("TRN2", target_bir_lowering=False, num_devices=1)
    args = [nc.dram_tensor(f"in_{k}", a.shape, mybir.dt.from_np(a.dtype), kind="ExternalInput").ap() for k, a in arrays.items()]
    out = nc.dram_tensor("out_dram", (1, SEQ, D), F32, kind="ExternalOutput").ap()
    build(nc, *args, out)
    r = run_bass_kernel_spmd(nc, [{f"in_{k}": a for k, a in arrays.items()}], core_ids=[0])
    return r.results[0]["out_dram"]
```
